# Optimizing a Trainium2 kernel written in Bass

```python
import jax, jax.numpy as jnp
from jax import lax
import numpy as np
import math

D_MODEL = 1024
BATCH = 1
SEQ = 256
DEPTH = 1

CHUNK = 64
QBLOCK = 128
SB_HEADS = 8
SB_HEAD_DIM = 64
SB_WIDTH = SB_HEADS * SB_HEAD_DIM
HG_HEADS = 8
HG_KDIM = 64
HG_VDIM = 64
HG_WIDTH = HG_HEADS * HG_KDIM
HG_VWIDTH = HG_HEADS * HG_VDIM
N_BRANCHES = 2
N_GROUPS = 4
EXPERTS_PER_GROUP = 4
N_EXPERTS = N_GROUPS * EXPERTS_PER_GROUP
TOP_K_INNER = 2
D_EXPERT = 512
IN_COLS = 3 * SB_WIDTH + 2 * HG_WIDTH + 2 * HG_VWIDTH + N_BRANCHES * D_MODEL
EPS = 1e-6


def rmsnorm(x, g):
    xf = x.astype(jnp.float32)
    var = jnp.mean(xf * xf, axis=-1, keepdims=True)
    return (xf * lax.rsqrt(var + EPS) * g.astype(jnp.float32)).astype(x.dtype)

def stick_breaking_attention(q, k, v):
    b, h, s, dh = q.shape
    nb = s // QBLOCK
    scale = dh ** -0.5
    key_pos = jnp.arange(s)
    q_blocks = q.reshape(b, h, nb, QBLOCK, dh).transpose(2, 0, 1, 3, 4)

    def one_block(args):
        q_blk, blk = args
        z = jnp.einsum('bhqd,bhkd->bhqk', q_blk, k, preferred_element_type=jnp.float32) * scale
        q_pos = blk * QBLOCK + jnp.arange(QBLOCK)
        mask = key_pos[None, :] < q_pos[:, None]
        log_beta = jax.nn.log_sigmoid(z)
        log_keep = jnp.where(mask, jax.nn.log_sigmoid(-z), 0.0)
        later = jnp.concatenate([log_keep[..., 1:], jnp.zeros_like(log_keep[..., :1])], axis=-1)
        log_survive = lax.cumsum(later, axis=3, reverse=True)
        a = jnp.where(mask, jnp.exp(log_beta + log_survive), 0.0)
        return jnp.einsum('bhqk,bhkd->bhqd', a.astype(v.dtype), v)

    out = lax.map(one_block, (q_blocks, jnp.arange(nb)))
    return out.transpose(1, 2, 0, 3, 4).reshape(b, h, s, dh)

def hgrn2_chunk_scan(q, k, log_f, v):
    b, s, h, dk = q.shape
    dv = v.shape[-1]
    nc = s // CHUNK

    def to_chunks(t):
        return t.reshape(b, nc, CHUNK, h, t.shape[-1]).transpose(1, 0, 3, 2, 4)

    causal = jnp.tril(jnp.ones((CHUNK, CHUNK), dtype=bool))

    def step(state, xs):
        qc, kc, gc, vc = xs
        cum = jnp.cumsum(gc, axis=2)
        diff = cum[:, :, :, None, :] - cum[:, :, None, :, :]
        decay = jnp.exp(jnp.where(causal[:, :, None], diff, -jnp.inf))
        scores = jnp.einsum('bhtk,bhsk,bhtsk->bhts', qc, kc, decay)
        o = (jnp.einsum('bhts,bhsv->bhtv', scores, vc)
             + jnp.einsum('bhtk,bhkv->bhtv', qc * jnp.exp(cum), state))
        last = cum[:, :, -1, :]
        state = (state * jnp.exp(last)[..., None]
                 + jnp.einsum('bhsk,bhsv->bhkv', kc * jnp.exp(last[:, :, None, :] - cum), vc))
        return state, o

    init = jnp.zeros((b, h, dk, dv), jnp.float32)
    _, out = lax.scan(step, init, (to_chunks(q), to_chunks(k), to_chunks(log_f), to_chunks(v)))
    return out.transpose(1, 0, 3, 2, 4).reshape(b, s, h, dv)

def mixer_sublayer(x, ln1_g, w_in, w_branch_sb, w_branch_hg, hg_norm_g, lb, w_out):
    f32 = jnp.float32
    bsz, s, _ = x.shape
    h = rmsnorm(x, ln1_g)
    proj = h @ w_in
    widths = [SB_WIDTH] * 3 + [HG_WIDTH] * 2 + [HG_VWIDTH] * 2 + [D_MODEL]
    splits = np.cumsum(widths).tolist()
    q_sb, k_sb, v_sb, q_hg, f_hg, i_hg, g_hg, gate_sb, gate_hg = jnp.split(proj, splits, axis=-1)

    def sb_heads(t):
        return t.reshape(bsz, s, SB_HEADS, SB_HEAD_DIM).transpose(0, 2, 1, 3)
    y_sb = stick_breaking_attention(sb_heads(q_sb), sb_heads(k_sb), sb_heads(v_sb))
    y_sb = y_sb.transpose(0, 2, 1, 3).reshape(bsz, s, SB_WIDTH)

    f = lb + (1.0 - lb) * jax.nn.sigmoid(f_hg.astype(f32))
    def hg_heads(t):
        return t.reshape(bsz, s, HG_HEADS, -1)
    o = hgrn2_chunk_scan(hg_heads(jax.nn.silu(q_hg.astype(f32))), hg_heads(1.0 - f),
                         hg_heads(jnp.log(f)), hg_heads(i_hg.astype(f32)))
    o = o * lax.rsqrt(jnp.mean(o * o, axis=-1, keepdims=True) + EPS)
    o = o.reshape(bsz, s, HG_VWIDTH) * hg_norm_g.astype(f32) * jax.nn.silu(g_hg.astype(f32))
    y_hg = o.astype(x.dtype)

    merged = (jax.nn.sigmoid(gate_sb) * (y_sb @ w_branch_sb)
              + jax.nn.sigmoid(gate_hg) * (y_hg @ w_branch_hg))
    return x + merged @ w_out

def hier_moe(h, w_rg, b_rg, w_re, b_re, w_gate, w_up, w_down):
    f32 = jnp.float32
    bsz, s, d = h.shape
    t = h.reshape(-1, d)
    n = t.shape[0]
    g_logits = (t @ w_rg).astype(f32) + b_rg.astype(f32)
    p_group = jax.nn.softmax(g_logits, axis=-1)
    g_idx = jnp.argmax(g_logits, axis=-1)
    w_grp = jnp.take_along_axis(p_group, g_idx[:, None], axis=1)
    e_logits = ((t @ w_re).astype(f32) + b_re.astype(f32)).reshape(n, N_GROUPS, EXPERTS_PER_GROUP)
    in_group = jnp.take_along_axis(e_logits, g_idx[:, None, None], axis=1)[:, 0]
    top_v, top_i = lax.top_k(in_group, TOP_K_INNER)
    w_sel = jax.nn.softmax(top_v, axis=-1) * w_grp
    expert_ids = g_idx[:, None] * EXPERTS_PER_GROUP + top_i
    combine = jnp.sum(jax.nn.one_hot(expert_ids, N_EXPERTS, dtype=f32) * w_sel[..., None], axis=1)
    y = jnp.zeros((n, d), f32)
    for e in range(N_EXPERTS):
        a = jax.nn.silu(t @ w_gate[e]) * (t @ w_up[e])
        y = y + combine[:, e:e + 1] * (a @ w_down[e]).astype(f32)
    return y.astype(h.dtype).reshape(bsz, s, d)

def first_inputs(seed: int = 0) -> dict:
    key = jax.random.key(seed)
    ks = jax.random.split(key, 17)
    f32 = jnp.float32

    def nrm(k, shape, scale):
        return jax.random.normal(k, shape, f32) * scale

    return {
        'x': nrm(ks[0], (BATCH, SEQ, D_MODEL), 1.0),
        'ln1_g': 1.0 + nrm(ks[1], (DEPTH, D_MODEL), 0.02),
        'w_in': nrm(ks[2], (DEPTH, D_MODEL, IN_COLS), D_MODEL ** -0.5),
        'w_branch_sb': nrm(ks[3], (DEPTH, SB_WIDTH, D_MODEL), SB_WIDTH ** -0.5),
        'w_branch_hg': nrm(ks[4], (DEPTH, HG_VWIDTH, D_MODEL), HG_VWIDTH ** -0.5),
        'hg_norm_g': 1.0 + nrm(ks[5], (DEPTH, HG_VWIDTH), 0.02),
        'hg_lb_logits': nrm(ks[6], (DEPTH + 1, HG_WIDTH), 0.1),
        'w_out': nrm(ks[7], (DEPTH, D_MODEL, D_MODEL), D_MODEL ** -0.5),
        'ln2_g': 1.0 + nrm(ks[8], (DEPTH, D_MODEL), 0.02),
        'w_router_group': nrm(ks[9], (DEPTH, D_MODEL, N_GROUPS), D_MODEL ** -0.5),
        'b_router_group': nrm(ks[10], (DEPTH, N_GROUPS), 0.01),
        'w_router_expert': nrm(ks[11], (DEPTH, D_MODEL, N_EXPERTS), D_MODEL ** -0.5),
        'b_router_expert': nrm(ks[12], (DEPTH, N_EXPERTS), 0.01),
        'w_exp_gate': nrm(ks[13], (DEPTH, N_EXPERTS, D_MODEL, D_EXPERT), D_MODEL ** -0.5),
        'w_exp_up': nrm(ks[14], (DEPTH, N_EXPERTS, D_MODEL, D_EXPERT), D_MODEL ** -0.5),
        'w_exp_down': nrm(ks[15], (DEPTH, N_EXPERTS, D_EXPERT, D_MODEL), D_EXPERT ** -0.5),
        'final_g': 1.0 + nrm(ks[16], (D_MODEL,), 0.02),
    }

def first_block(x, ln1_g, w_in, w_branch_sb, w_branch_hg, hg_norm_g, hg_lb_logits, w_out, ln2_g,
              w_router_group, b_router_group, w_router_expert, b_router_expert,
              w_exp_gate, w_exp_up, w_exp_down, final_g):
    lb_all = jnp.cumsum(jax.nn.softmax(hg_lb_logits.astype(jnp.float32), axis=0), axis=0)
    for l in range(DEPTH):
        x = mixer_sublayer(x, ln1_g[l], w_in[l], w_branch_sb[l], w_branch_hg[l], hg_norm_g[l],
                           lb_all[l], w_out[l])
        x = x + hier_moe(rmsnorm(x, ln2_g[l]), w_router_group[l], b_router_group[l],
                         w_router_expert[l], b_router_expert[l],
                         w_exp_gate[l], w_exp_up[l], w_exp_down[l])
    return rmsnorm(x, final_g)


HEAD_DIM = 64
N_HEADS_A = 8
N_KV_A = 2
N_HEADS_B = 8
N_KV_B = 2
N_HEADS = N_HEADS_A + N_HEADS_B
MIX_WIDTH = N_HEADS * HEAD_DIM
WINDOW_A = 128
CMP_LEN = 32
CMP_STRIDE = 16
CMP_HIDDEN = 128
SEL_LEN = 64
SEL_TOPK = 16
WINDOW_B = 512
FORCE_BONUS = 1000.0
BAND_BLOCK = 128
NSA_BLOCK = 32
NUM_BUCKETS = 32
MAX_DISTANCE = 128
D_FF = 2816
NEG = -1e9

QA = N_HEADS_A * HEAD_DIM
KVA = N_KV_A * HEAD_DIM
QB = N_HEADS_B * HEAD_DIM
KVB = N_KV_B * HEAD_DIM
N_GATES = 3 * N_HEADS_B
OFF_KA = QA
OFF_VA = OFF_KA + KVA
OFF_QB = OFF_VA + KVA
OFF_KVB = OFF_QB + QB
OFF_GB = OFF_KVB + 6 * KVB
D_IN = OFF_GB + N_GATES


def rms_norm(x, g):
    x32 = x.astype(jnp.float32)
    y = x32 * lax.rsqrt(jnp.mean(x32 * x32, axis=-1, keepdims=True) + EPS) * g.astype(jnp.float32)
    return y.astype(x.dtype)

def swiglu(h, w_in, w_out):
    gate, up = jnp.split(h @ w_in, 2, axis=-1)
    return (jax.nn.silu(gate) * up) @ w_out

def rel_bucket(rel):
    n = jnp.maximum(rel, 0)
    max_exact = NUM_BUCKETS // 2
    nf = jnp.maximum(n, 1).astype(jnp.float32)
    large = max_exact + (jnp.log(nf / max_exact) / math.log(MAX_DISTANCE / max_exact)
                         * (NUM_BUCKETS - max_exact)).astype(jnp.int32)
    large = jnp.minimum(large, NUM_BUCKETS - 1)
    return jnp.where(n < max_exact, n, large)

def rel_bias(tbl, rel):
    return tbl[rel_bucket(rel)].astype(jnp.float32)

def banded_attention(q, k, v, tbl, window, sinks):
    B, S, G, R, Dh = q.shape
    kv_len = window + BAND_BLOCK
    k_pad = jnp.pad(k, ((0, 0), (window, 0), (0, 0), (0, 0)))
    v_pad = jnp.pad(v, ((0, 0), (window, 0), (0, 0), (0, 0)))

    def block(i):
        start = i * BAND_BLOCK
        qb = lax.dynamic_slice_in_dim(q, start, BAND_BLOCK, axis=1)
        kb = lax.dynamic_slice_in_dim(k_pad, start, kv_len, axis=1)
        vb = lax.dynamic_slice_in_dim(v_pad, start, kv_len, axis=1)
        q_pos = start + jnp.arange(BAND_BLOCK)
        k_pos = start - window + jnp.arange(kv_len)
        rel = q_pos[:, None] - k_pos[None, :]
        mask = (rel >= 0) & (rel < window) & (k_pos[None, :] >= 0)
        bias = rel_bias(tbl, rel).reshape(BAND_BLOCK, kv_len, G, R).transpose(2, 3, 0, 1)
        logits = jnp.einsum('bqgrd,bkgd->bgrqk', qb, kb).astype(jnp.float32) + bias
        logits = jnp.where(mask, logits, NEG)
        m = logits.max(axis=-1, keepdims=True)
        if sinks is None:
            p = jnp.exp(logits - m)
            denom = p.sum(axis=-1, keepdims=True)
        else:
            s = sinks.astype(jnp.float32).reshape(1, G, R, 1, 1)
            m = jnp.maximum(m, s)
            p = jnp.exp(logits - m)
            denom = p.sum(axis=-1, keepdims=True) + jnp.exp(s - m)
        p = p / denom
        return jnp.einsum('bgrqk,bkgd->bqgrd', p.astype(vb.dtype), vb)

    out = lax.map(block, jnp.arange(S // BAND_BLOCK))
    return out.transpose(1, 0, 2, 3, 4, 5).reshape(B, S, G, R, Dh)

def compress_kv(kv, pos, w1, b1, w2, b2):
    _, B, S, G, Dh = kv.shape
    r = CMP_LEN // CMP_STRIDE
    n_chunk = S // CMP_STRIDE
    n_cmp = n_chunk - r + 1
    chunks = kv.reshape(2, B, n_chunk, CMP_STRIDE, G, Dh)
    w1r = w1.reshape(2, r, CMP_STRIDE, Dh, CMP_HIDDEN)
    pre = b1[:, None, None, None, :]
    for j in range(r):
        pe = pos[:, None, None, j * CMP_STRIDE:(j + 1) * CMP_STRIDE, None, :]
        part = jnp.einsum('kbnpgd,kpdh->kbngh', chunks + pe, w1r[:, j])
        pre = pre + part[:, :, j:j + n_cmp]
    hid = jax.nn.silu(pre)
    return jnp.einsum('kbcgh,khd->kbcgd', hid, w2) + b2[:, None, None, None, :]

def nsa_cmp_sel(q, k_c, v_c, k_s, v_s, tbl):
    B, S, G, R, Dh = q.shape
    n_cmp = k_c.shape[1]
    n_slc = S // SEL_LEN
    n_top = min(SEL_TOPK, n_slc)
    cmp_start = jnp.arange(n_cmp) * CMP_STRIDE
    cmp_end = cmp_start + CMP_LEN - 1
    slc_start = jnp.arange(n_slc) * SEL_LEN
    overlap = ((cmp_start[:, None] < slc_start[None, :] + SEL_LEN)
               & (cmp_end[:, None] >= slc_start[None, :])).astype(jnp.float32)
    kb = k_s.reshape(B, n_slc, SEL_LEN, G, Dh).transpose(0, 3, 1, 2, 4)
    vb = v_s.reshape(B, n_slc, SEL_LEN, G, Dh).transpose(0, 3, 1, 2, 4)
    tbl3 = tbl.reshape(NUM_BUCKETS, G, R)
    b_idx = jnp.arange(B)[:, None, None, None]
    g_idx = jnp.arange(G)[None, :, None, None]
    blk = jnp.arange(n_slc)
    offs = jnp.arange(SEL_LEN)

    def block(i):
        start = i * NSA_BLOCK
        qb = lax.dynamic_slice_in_dim(q, start, NSA_BLOCK, axis=1)
        q_pos = start + jnp.arange(NSA_BLOCK)
        rel_c = q_pos[:, None] - cmp_end[None, :]
        mask_c = rel_c >= 0
        bias_c = rel_bias(tbl, rel_c).reshape(NSA_BLOCK, n_cmp, G, R).transpose(2, 3, 0, 1)
        lc = jnp.einsum('bqgrd,bcgd->bgrqc', qb, k_c).astype(jnp.float32) + bias_c
        lc = jnp.where(mask_c, lc, NEG)
        pc = jnp.where(mask_c, jnp.exp(lc - lc.max(axis=-1, keepdims=True)), 0.0)
        pc = pc / jnp.maximum(pc.sum(axis=-1, keepdims=True), jnp.finfo(jnp.float32).tiny)
        o_cmp = jnp.einsum('bgrqc,bcgd->bqgrd', pc.astype(v_c.dtype), v_c)
        imp = jnp.einsum('bgrqc,cn->bgqn', pc, overlap)
        cur = q_pos[:, None] // SEL_LEN
        valid = blk[None, :] <= cur
        forced = (blk[None, :] == 0) | (blk[None, :] == cur) | (blk[None, :] == cur - 1)
        score = jnp.where(valid, imp + jnp.where(forced, FORCE_BONUS, 0.0), NEG)
        top_val, top_idx = lax.top_k(score, n_top)
        sel_ok = top_val > 0.5 * NEG
        ks = kb[b_idx, g_idx, top_idx]
        vs = vb[b_idx, g_idx, top_idx]
        tok = top_idx[..., None] * SEL_LEN + offs
        rel_s = q_pos[None, None, :, None, None] - tok
        mask_s = (sel_ok[..., None] & (rel_s >= 0))[:, :, None]
        bias_s = jnp.moveaxis(tbl3[rel_bucket(rel_s), g_idx[..., None]], -1, 2).astype(jnp.float32)
        ls = jnp.einsum('bqgrd,bgqnld->bgrqnl', qb, ks).astype(jnp.float32) + bias_s
        ls = jnp.where(mask_s, ls, NEG)
        ps = jax.nn.softmax(ls.reshape(B, G, R, NSA_BLOCK, n_top * SEL_LEN), axis=-1).reshape(ls.shape)
        o_sel = jnp.einsum('bgrqnl,bgqnld->bqgrd', ps.astype(vs.dtype), vs)
        return o_cmp, o_sel

    o_cmp, o_sel = lax.map(block, jnp.arange(S // NSA_BLOCK))
    o_cmp = o_cmp.transpose(1, 0, 2, 3, 4, 5).reshape(B, S, G, R, Dh)
    o_sel = o_sel.transpose(1, 0, 2, 3, 4, 5).reshape(B, S, G, R, Dh)
    return o_cmp, o_sel

def hybrid_layer(x, tbl, ffn1_norm, ffn1_w_in, ffn1_w_out, mix_norm, w_mix_in, w_mix_out,
                 q_norm_a, k_norm_a, sinks_a, q_norm_b, k_norm_b,
                 cmp_pos, cmp_w1, cmp_b1, cmp_w2, cmp_b2,
                 ffn2_norm, ffn2_w_in, ffn2_w_out):
    B, S, _ = x.shape
    r_a = N_HEADS_A // N_KV_A
    r_b = N_HEADS_B // N_KV_B
    scale = HEAD_DIM ** -0.5
    x = x + 0.5 * swiglu(rms_norm(x, ffn1_norm), ffn1_w_in, ffn1_w_out)
    h = rms_norm(x, mix_norm)
    proj = h @ w_mix_in
    q_a = rms_norm(proj[..., :OFF_KA].reshape(B, S, N_KV_A, r_a, HEAD_DIM), q_norm_a) * scale
    k_a = rms_norm(proj[..., OFF_KA:OFF_VA].reshape(B, S, N_KV_A, HEAD_DIM), k_norm_a)
    v_a = proj[..., OFF_VA:OFF_QB].reshape(B, S, N_KV_A, HEAD_DIM)
    o_a = banded_attention(q_a, k_a, v_a, tbl[:, :N_HEADS_A], WINDOW_A, sinks_a)
    q_b = rms_norm(proj[..., OFF_QB:OFF_KVB].reshape(B, S, N_KV_B, r_b, HEAD_DIM), q_norm_b) * scale
    kv_b = proj[..., OFF_KVB:OFF_GB].reshape(B, S, 6, N_KV_B, HEAD_DIM)
    kv_c = compress_kv(jnp.moveaxis(kv_b[:, :, 0:2], 2, 0), cmp_pos, cmp_w1, cmp_b1, cmp_w2, cmp_b2)
    k_c = rms_norm(kv_c[0], k_norm_b)
    v_c = kv_c[1]
    k_s = rms_norm(kv_b[:, :, 2], k_norm_b)
    v_s = kv_b[:, :, 3]
    k_w = rms_norm(kv_b[:, :, 4], k_norm_b)
    v_w = kv_b[:, :, 5]
    tbl_b = tbl[:, N_HEADS_A:]
    o_cmp, o_sel = nsa_cmp_sel(q_b, k_c, v_c, k_s, v_s, tbl_b)
    o_win = banded_attention(q_b, k_w, v_w, tbl_b, WINDOW_B, None)
    gates = jax.nn.sigmoid(proj[..., OFF_GB:].astype(jnp.float32)).reshape(B, S, 3, N_KV_B, r_b, 1)
    o_b = gates[:, :, 0] * o_cmp + gates[:, :, 1] * o_sel + gates[:, :, 2] * o_win
    mix = jnp.concatenate([o_a.reshape(B, S, QA).astype(x.dtype),
                           o_b.reshape(B, S, QB).astype(x.dtype)], axis=-1)
    x = x + mix @ w_mix_out
    x = x + 0.5 * swiglu(rms_norm(x, ffn2_norm), ffn2_w_in, ffn2_w_out)
    return x

def second_inputs(seed: int = 0) -> dict:
    key = jax.random.key(seed)
    ks = jax.random.split(key, 24)
    f32 = jnp.float32

    def nrm(k, shape, scale):
        return jax.random.normal(k, shape, f32) * scale

    def gain(k, shape):
        return 1.0 + 0.05 * jax.random.normal(k, shape, f32)

    L = DEPTH
    return {
        'x': nrm(ks[0], (BATCH, SEQ, D_MODEL), 1.0),
        'rel_bias_table': nrm(ks[1], (NUM_BUCKETS, N_HEADS), 0.5),
        'ffn1_norm': gain(ks[2], (L, D_MODEL)),
        'ffn1_w_in': nrm(ks[3], (L, D_MODEL, 2 * D_FF), D_MODEL ** -0.5),
        'ffn1_w_out': nrm(ks[4], (L, D_FF, D_MODEL), D_FF ** -0.5),
        'mix_norm': gain(ks[5], (L, D_MODEL)),
        'w_mix_in': nrm(ks[6], (L, D_MODEL, D_IN), D_MODEL ** -0.5),
        'w_mix_out': nrm(ks[7], (L, MIX_WIDTH, D_MODEL), MIX_WIDTH ** -0.5),
        'q_norm_a': gain(ks[8], (L, HEAD_DIM)),
        'k_norm_a': gain(ks[9], (L, HEAD_DIM)),
        'sinks_a': nrm(ks[10], (L, N_HEADS_A), 0.5),
        'q_norm_b': gain(ks[11], (L, HEAD_DIM)),
        'k_norm_b': gain(ks[12], (L, HEAD_DIM)),
        'cmp_pos': nrm(ks[13], (L, 2, CMP_LEN, HEAD_DIM), 0.5),
        'cmp_w1': nrm(ks[14], (L, 2, CMP_LEN * HEAD_DIM, CMP_HIDDEN), (CMP_LEN * HEAD_DIM) ** -0.5),
        'cmp_b1': nrm(ks[15], (L, 2, CMP_HIDDEN), 0.02),
        'cmp_w2': nrm(ks[16], (L, 2, CMP_HIDDEN, HEAD_DIM), CMP_HIDDEN ** -0.5),
        'cmp_b2': nrm(ks[17], (L, 2, HEAD_DIM), 0.02),
        'ffn2_norm': gain(ks[18], (L, D_MODEL)),
        'ffn2_w_in': nrm(ks[19], (L, D_MODEL, 2 * D_FF), D_MODEL ** -0.5),
        'ffn2_w_out': nrm(ks[20], (L, D_FF, D_MODEL), D_FF ** -0.5),
    }

def second_block(x, rel_bias_table, ffn1_norm, ffn1_w_in, ffn1_w_out, mix_norm, w_mix_in, w_mix_out,
              q_norm_a, k_norm_a, sinks_a, q_norm_b, k_norm_b,
              cmp_pos, cmp_w1, cmp_b1, cmp_w2, cmp_b2,
              ffn2_norm, ffn2_w_in, ffn2_w_out):
    for l in range(DEPTH):
        x = hybrid_layer(x, rel_bias_table, ffn1_norm[l], ffn1_w_in[l], ffn1_w_out[l],
                         mix_norm[l], w_mix_in[l], w_mix_out[l],
                         q_norm_a[l], k_norm_a[l], sinks_a[l], q_norm_b[l], k_norm_b[l],
                         cmp_pos[l], cmp_w1[l], cmp_b1[l], cmp_w2[l], cmp_b2[l],
                         ffn2_norm[l], ffn2_w_in[l], ffn2_w_out[l])
    return x


def setup_inputs(seed=0):
    out = dict(first_inputs(seed))
    for name, value in second_inputs(seed + 1).items():
        if name != "x":
            out[name + "_2"] = value
    return out


def reference(
    x, ln1_g, w_in, w_branch_sb, w_branch_hg, hg_norm_g, hg_lb_logits, w_out, ln2_g,
    w_router_group, b_router_group, w_router_expert, b_router_expert, w_exp_gate, w_exp_up,
    w_exp_down, final_g, rel_bias_table_2, ffn1_norm_2, ffn1_w_in_2, ffn1_w_out_2, mix_norm_2,
    w_mix_in_2, w_mix_out_2, q_norm_a_2, k_norm_a_2, sinks_a_2, q_norm_b_2, k_norm_b_2,
    cmp_pos_2, cmp_w1_2, cmp_b1_2, cmp_w2_2, cmp_b2_2, ffn2_norm_2, ffn2_w_in_2, ffn2_w_out_2,
):
    x = first_block(
        x, ln1_g, w_in, w_branch_sb, w_branch_hg, hg_norm_g, hg_lb_logits, w_out, ln2_g,
        w_router_group, b_router_group, w_router_expert, b_router_expert, w_exp_gate, w_exp_up,
        w_exp_down, final_g,
    )
    return second_block(
        x, rel_bias_table_2, ffn1_norm_2, ffn1_w_in_2, ffn1_w_out_2, mix_norm_2, w_mix_in_2,
        w_mix_out_2, q_norm_a_2, k_norm_a_2, sinks_a_2, q_norm_b_2, k_norm_b_2, cmp_pos_2,
        cmp_w1_2, cmp_b1_2, cmp_w2_2, cmp_b2_2, ffn2_norm_2, ffn2_w_in_2, ffn2_w_out_2,
    )


_drawn_inputs = setup_inputs


def setup_inputs(seed=0):
    import zlib

    import numpy as np

    out = dict(_drawn_inputs(seed))
    spreads = {}
    factors = {'hg_norm_g': 4.723,
     'hg_lb_logits': 3.28,
     'ln2_g': 3.121,
     'b_router_group': 5.125,
     'b_router_expert': 6.138,
     'mix_norm_2': 3.321,
     'q_norm_a_2': 8.0,
     'k_norm_a_2': 8.0,
     'sinks_a_2': 45.922,
     'q_norm_b_2': 8.0,
     'k_norm_b_2': 8.0,
     'cmp_b1_2': 8.0,
     'cmp_b2_2': 7.752,
     'ffn2_norm_2': 2.903}
    for name, (base, spread) in spreads.items():
        noise = np.random.default_rng([zlib.crc32(name.encode()), seed]).standard_normal(out[name].shape)
        drawn = base * np.exp(spread * noise) if base else spread * noise
        out[name] = __import__('jax').numpy.asarray(drawn.astype(out[name].dtype))
    for name, factor in factors.items():
        out[name] = (out[name] * factor).astype(out[name].dtype)
    return out
```

```python
from contextlib import ExitStack

import numpy as np

import concourse.bass as bass
from concourse import mybir

F32 = mybir.dt.float32
F32R = mybir.dt.float32r
I32 = mybir.dt.int32
ALU = mybir.AluOpType
ACT = mybir.ActivationFunctionType
AX = mybir.AxisListType.X

P = 128
D = 1024
S = 256
TT = S // P
KT = D // P
EPS = 1e-6
HEADS = 8
DH = 64
SBW = HEADS * DH
GROUPS, PER_GROUP = 4, 4
N_EXP = GROUPS * PER_GROUP
D_EXP = 512
D_FF = 2816
D_MIX = 2072
GATE_COLS = 3 * HEADS
NEG = -1e9
TINY = float(np.finfo(np.float32).tiny)
CMP_LEN, CMP_STRIDE = 32, 16
N_CMP = (S - CMP_LEN) // CMP_STRIDE + 1
PAIRS = CMP_LEN // 2
REL_W = 384

UNIT = 2048
RAW, SPLIT = 6, 3
STEP = 6
LEVELS = 7

U_IN, N_IN = 0, 22
U_BRANCH = U_IN + N_IN
U_OUT = U_BRANCH + 4
U_MOE = U_OUT + 4
U_FFN1 = U_MOE + N_EXP * STEP
FFN_FULL = D_FF // 512
FFN_UNITS = FFN_FULL * STEP + 3
U_MIX = U_FFN1 + FFN_UNITS
U_MIXOUT = U_MIX + 8
U_FFN2 = U_MIXOUT + 4
U_END = U_FFN2 + FFN_UNITS

OFF_KA, OFF_VA, OFF_QB, OFF_KC, OFF_KS, OFF_VS, OFF_KW, OFF_VW = 512, 640, 768, 1280, 1536, 1664, 1792, 1920
MIX_BLOCKS = 2048 // DH
FAR = 1e8

IN_COLS = dict(q_sb=0, k_sb=512, v_sb=1024, q_hg=1536, f_hg=2048, i_hg=2560, g_hg=3072,
               gate_sb0=3584, gate_sb1=4096, gate_hg0=4608, gate_hg1=5120)
IN_ORDER = ["q_sb", "k_sb", "v_sb", "i_hg", "q_hg", "g_hg", "f_hg", "gate_sb0", "gate_sb1", "gate_hg0", "gate_hg1"]

ROW_LN1, ROW_LN2, ROW_FFN1, ROW_MIX, ROW_FFN2 = 0, 8, 16, 24, 32
ROW_HGN, ROW_LB, ROW_QA, ROW_KA, ROW_QB, ROW_KB, ROW_B1 = 40, 44, 52, 53, 54, 55, 56
ROW_POS = 58
N_ROWS = 90


def shape_constants():
    k = np.arange(P)[:, None]
    q = np.arange(P)[None, :]
    ident = (k == q).astype(np.float32)
    neg_tri = -(k >= q).astype(np.float32)
    neg_ones = -np.ones((P, P), np.float32)
    dense = np.stack([ident, neg_tri, neg_ones], 1)
    masks = []
    for level in range(LEVELS):
        h = 1 << level
        masks.append((k // (2 * h) == q // (2 * h)) & (k % (2 * h) < h) & (q % (2 * h) >= h))
    masks.append(k == q)
    masks = np.stack(masks, 1).astype(np.int32)
    rel = 255 - np.arange(REL_W)
    n = np.maximum(rel, 0)
    nf = np.maximum(n, 1).astype(np.float32)
    large = 16 + (np.log(nf / np.float32(16)) / np.float32(np.log(8.0)) * np.float32(16)).astype(np.int32)
    bucket = np.where(n < 16, n, np.minimum(large, 31))
    hot = (np.arange(32)[:, None] == bucket[None, :]).astype(np.float32)
    off_a = np.where((rel < 0) | (rel >= 128), np.float32(NEG), np.float32(0))[None, :]
    off_b = np.where(rel < 0, np.float32(NEG), np.float32(0))[None, :]
    bias = np.stack([np.concatenate([hot, off_a]), np.concatenate([hot, off_b])], 1).astype(np.float32)
    return dense, masks, bias


def two_blocks_kernel(nc, a, out):
    dense_np, masks_np, bias_np = shape_constants()
    dense_dram = nc.inline_tensor(dense_np, name="dense_const").ap()
    masks_dram = nc.inline_tensor(masks_np, name="masks_const").ap()
    onehot_dram = nc.inline_tensor(bias_np, name="bucket_const").ap()
    bias_rows = nc.dram_tensor("bias_rows", (2, HEADS, P, REL_W), F32, kind="Internal")

    with ExitStack() as ctx:
        def sb(name, shape, dt=F32):
            return ctx.enter_context(nc.sbuf_tensor(name, shape, dt))

        x = sb("x_res", [P, TT, D])
        tok = sb("tok", [P, TT, D])
        h_hi = sb("h_hi", [P, KT, S], F32R)
        h_lo = sb("h_lo", [P, KT, S], F32R)
        w_raw = sb("w_raw", [P, RAW, UNIT])
        w_hi = sb("w_hi", [P, SPLIT, UNIT], F32R)
        w_lo = sb("w_lo", [P, SPLIT, UNIT], F32R)
        aT_hi = sb("aT_hi", [P, 4, S], F32R)
        aT_lo = sb("aT_lo", [P, 4, S], F32R)
        dense = sb("dense", [P, 3, P])
        masks = sb("masks", [P, LEVELS + 1, P], I32)
        rows = sb("rows", [N_ROWS, P])
        cols = sb("cols", [P, N_ROWS])
        final_g = masks[:, :, :].rearrange("p a b -> p (a b)").bitcast(F32)
        arena = sb("arena", [P, 16384])
        sc = sb("scalars", [P, 1024])
        wr_raw = sb("wr_raw", [P, KT, 24])
        wr_hi = sb("wr_hi", [P, KT, 24], F32R)
        wr_lo = sb("wr_lo", [P, KT, 24], F32R)
        small = sb("small", [P, 512])
        one_row = sb("one_row", [1, P])
        rb_row = sb("rb_row", [1, 24])
        tbl = sb("tbl", [33, 2 * HEADS])
        b2_row = sb("b2_row", [1, 2, DH])
        ps = ctx.enter_context(nc.psum_tensor("ps", [P, 8, 512], F32))

        ident, neg_tri, neg_ones = dense[:, 0, :], dense[:, 1, :], dense[:, 2, :]

        def region(off, *dims):
            n = int(np.prod(dims))
            v = arena[:, off:off + n]
            names = "abcd"[:len(dims)]
            if len(dims) == 1:
                return v
            return v.rearrange(f"p ({' '.join(names)}) -> p {' '.join(names)}",
                               **{names[i]: dims[i] for i in range(len(dims))})

        v_sb = region(0, TT, 512)
        v_hg = region(1024, TT, 512)
        g_act = region(2048, TT, 512)
        gates = region(3072, 4, TT, 512)
        stage = region(7168, 4, TT, 512)
        qT = region(11264, 4, S)
        kT = region(12288, 4, S)
        qhT = region(13312, 4, S)
        pre = region(14336, 4, S)
        soft = region(7168, 2, 2, 384)
        att = region(8704, 2, 2, 384)
        hk = region(11264, 4, S)
        suf = region(12288, 4, S)
        q_dec = region(7168, 2, 4, S)
        k_dec = region(9216, 2, 4, S)
        sc_far = region(15360, 2, 4, P)
        sc_near = tok[:, :, :].rearrange("p a (b c) -> p (a b) c", c=P)
        o_gated = region(7168, TT, 512)
        o_sq = region(9216, TT, 512)
        act_s = region(0, TT, 512)
        act_a = region(1024, TT, 512)

        proj = region(0, TT, 2048)
        cmp_w1 = region(4096, 2, PAIRS, P)
        qqT = region(4096, 2, 4, S)
        kkT = region(6144, 6, S)
        sq = region(8192, TT, 2048)
        bias_t = region(8192, 2, HEADS, S)
        k_dup = region(12288, TT, 6, P)
        prob = region(12288, 4, 384)
        kvT = region(13824, 2, 3, S)
        probT = region(13824, 2, 384)
        cmp_w2 = region(15360, 2, DH)
        hidT = region(15488, 2, 32)
        kc_sq = region(15552, P)
        kc_n = region(15680, 2, 2, DH)
        v_c = region(15936, P)
        kcT = region(16064, 2, 16)
        onehot = region(15360, 2, REL_W)
        bias_out = region(14336, 2, REL_W)
        gate_sig = sc[:, 256:304].rearrange("p (t c) -> p t c", t=TT)
        blk_ss, blk_r = sc[:, 320:384], sc[:, 384:448]
        sums, negm = sc[:, 448:512], sc[:, 512:576]
        sink, nsink = sc[:, 576:584], sc[:, 584:592]
        o_scale, sink_t = sc[:, 592:656], sc[:, 656:672]
        gain8, bias2 = sc[:, 672:674], sc[:, 674:676]
        kc_ss, kc_r = sc[:, 676:678], sc[:, 678:680]
        o_part = region(14592, TT, 512)
        KINDS = [(0, 0, OFF_VA, 0), (1, 2, OFF_VS, 1), (1, 4, OFF_VW, 1), (1, None, None, 1)]

        def sem(name):
            return ctx.enter_context(nc.semaphore(name))

        raw_in = [sem(f"raw_in{i}") for i in range(RAW)]
        hi_ready, lo_ready, unit_used = sem("hi_ready"), sem("lo_ready"), sem("unit_used")
        x_in, rows_in, const_in, small_in, tbl_in, wr_in = (sem(n) for n in
            ("x_in", "rows_in", "const_in", "small_in", "tbl_in", "wr_in"))
        ss_ready, rms_ready, tok_ready = sem("ss_ready"), sem("rms_ready"), sem("tok_ready")
        xT_ready, hT_hi, hT_lo = sem("xT_ready"), sem("hT_hi"), sem("hT_lo")
        cols_T, cols_ready = sem("cols_T"), sem("cols_ready")
        lb_diff, lb_exp, lb_ready = sem("lb_diff"), sem("lb_exp"), sem("lb_ready")
        proj_out = sem("proj_out")
        stage_T, sbT_ready, hgT_ready = sem("stage_T"), sem("sbT_ready"), sem("hgT_ready")
        z_ready, ln_ready, sp_ready, spm_ready = sem("z_ready"), sem("ln_ready"), sem("sp_ready"), sem("spm_ready")
        s_ready, a_ready, am_ready, y_ready = sem("s_ready"), sem("a_ready"), sem("am_ready"), sem("y_ready")
        ysb_hi, ysb_lo = sem("ysb_hi"), sem("ysb_lo")
        zeroed, pre_ready, kdec_ready, qdec_ready = sem("zeroed"), sem("pre_ready"), sem("kdec_ready"), sem("qdec_ready")
        level_done, level_kept, far_ready = sem("level_done"), sem("level_kept"), sem("far_ready")
        o_ready, osq_ready, orms_in, orms_ready, og_ready, oT_ready, yhg_hi, yhg_lo = (sem(n) for n in
            ("o_ready", "osq_ready", "orms_in", "orms_ready", "og_ready", "oT_ready", "yhg_hi", "yhg_lo"))
        resid_ready = sem("resid_ready")
        act_seq, dve_seq, pool_seq = sem("act_seq"), sem("dve_seq"), sem("pool_seq")
        wr_split_hi, wr_split_lo, route_T, route_sub, route_exp, route_ready = (sem(n) for n in
            ("wr_split_hi", "wr_split_lo", "route_T", "route_sub", "route_exp", "route_ready"))
        gate_done, up_done, silu_done, a_done, aT_done, aT_hi_r, aT_lo_r, down_done, down_added = (sem(n) for n in
            ("gate_done", "up_done", "silu_done", "a_done", "aT_done", "aT_hi_r", "aT_lo_r", "down_done", "down_added"))
        stored = sem("stored")
        mix_out, gates_T, gsig_ready, blk_summed, blk_rms, q_normed, k_normed = (sem(n) for n in
            ("mix_out", "gates_T", "gsig_ready", "blk_summed", "blk_rms", "q_normed", "k_normed"))
        out_ready = sem("out_ready")
        bias_done, bias_sb, bias_stored, bias_in, onehot_in, cmp_in, wr2_in, pos_set = (sem(n) for n in
            ("bias_done", "bias_sb", "bias_stored", "bias_in", "onehot_in", "cmp_in", "wr2_in", "pos_set"))
        kv_T, kvT_ready, pre_T, bias2_set, hid_ready, kvc_ready, kcsq_ready, kcss_ready, kcr_ready, kcn_ready, kcT_T, kcT_set = (sem(n) for n in
            ("kv_T", "kvT_ready", "pre_T", "bias2_set", "hid_ready", "kvc_ready", "kcsq_ready", "kcss_ready", "kcr_ready",
             "kcn_ready", "kcT_T", "kcT_set"))
        qk_T, qk_set, lg_ready, neg_ready, p_ready, pT_ready, pT_set, pv_done, o_used, sink_ready, sinkexp = (sem(n) for n in
            ("qk_T", "qk_set", "lg_ready", "neg_ready", "p_ready", "pT_ready", "pT_set", "pv_done", "o_used", "sink_ready", "sinkexp"))
        ones_ready = sem("ones_ready")
        fg_in, coef_set = sem("fg_in"), sem("coef_set")

        def key_cols(kind, qt):
            if kind < 3:
                return slice(0, P) if qt == 0 else slice(P, P + S)
            return slice(0, (P - CMP_LEN) // CMP_STRIDE + 1) if qt == 0 else slice(16, 16 + N_CMP)

        class Chain:

            def __init__(self, eng, s):
                self.eng, self.s, self.n = eng, s, 0

            def __call__(self, ins):
                ins.then_inc(self.s, 1)
                self.n = self.n + 1
                self.eng.wait_ge(self.s, self.n)

            def mark(self, ins):
                ins.then_inc(self.s, 1)
                self.n = self.n + 1

            def settle(self):
                self.eng.wait_ge(self.s, self.n)

        w_in, w_out = a["w_in"][0], a["w_out"][0]

        def unit_src(w, r0, c0, width=512):
            n = UNIT // width
            return w[r0:r0 + n * P, c0:c0 + width].rearrange("(k p) n -> p k n", p=P)

        def slot(u):
            return u % RAW, u % SPLIT

        def moe_src(e, j):
            if j < 4:
                w = a["w_exp_gate"] if j < 2 else a["w_exp_up"]
                v = w[0].rearrange("e (k p) n -> e p k n", p=P)
                return v[e, :, 4 * (j % 2):4 * (j % 2) + 4, :] if isinstance(e, int) else \
                    v[bass.ds(e, 1), :, 4 * (j % 2):4 * (j % 2) + 4, :].rearrange("e p k n -> p (e k) n")
            v = a["w_exp_down"][0].rearrange("e (k p) n -> e p k n", p=P)
            c0 = 512 * (j - 4)
            return v[e, :, :, c0:c0 + 512] if isinstance(e, int) else \
                v[bass.ds(e, 1), :, :, c0:c0 + 512].rearrange("e p k n -> p (e k) n")

        def ffn_src(w1, w2, c, j):
            w1, w2 = w1[0], w2[0]
            if j < 4:
                c0 = (0 if j < 2 else D_FF) + 512 * c
                r0 = 512 * (j % 2)
                return w1[r0:r0 + 512, c0:c0 + 512].rearrange("(k p) n -> p k n", p=P) if isinstance(c, int) else \
                    w1[r0:r0 + 512, bass.ds(c0, 512)].rearrange("(k p) n -> p k n", p=P)
            c0 = 512 * (j - 4)
            return w2[512 * c:512 * c + 512, c0:c0 + 512].rearrange("(k p) n -> p k n", p=P) if isinstance(c, int) else \
                w2[bass.ds(512 * c, 512), c0:c0 + 512].rearrange("(k p) n -> p k n", p=P)

        block = ctx.enter_context(nc.Block())

        @block.sync
        def _(sp):
            sp.dma_start(x[:, :, :], a["x"][0].rearrange("(t p) d -> p t d", p=P)).then_inc(x_in, 16)

            def load(u, src, i=None, k=4):
                r = u % RAW
                if u >= RAW:
                    sp.wait_ge(lo_ready, u - RAW + 1 if i is None else STEP * i + (u - RAW + 1))
                dst = w_raw[:, r, :].rearrange("p (k n) -> p k n", k=k)
                sp.dma_start(dst, src).then_inc(raw_in[r], 16)

            u = U_IN
            for name in IN_ORDER:
                for kh in range(2):
                    load(u, unit_src(w_in, 512 * kh, IN_COLS[name]))
                    u += 1
                    if u == 8:
                        sp.wait_ge(bias_sb, 1)
                        for n in range(2):
                            sp.dma_start(bias_rows.ap()[n], bias_out[0:HEADS, n:n + 1, :].broadcast_to((HEADS, P, REL_W))
                                         ).then_inc(bias_stored, 16)
            for half in range(2):
                for w in ("w_branch_sb", "w_branch_hg"):
                    load(u, unit_src(a[w][0], 0, 512 * half))
                    u += 1
            for half in range(2):
                for kh in range(2):
                    load(u, unit_src(w_out, 512 * kh, 512 * half))
                    u += 1

            def chunks(u0, n, src):
                for j in range(4):
                    load(u0 + j, src(0, j))
                with sp.Fori(0, n - 1) as i:
                    for j in range(STEP):
                        load(u0 + 4 + j, src(i + 1, j) if j < 4 else src(i, j), i)

            chunks(U_MOE, N_EXP, moe_src)
            for j in (4, 5):
                load(U_MOE + 4 + STEP * (N_EXP - 1) + j - 4, moe_src(N_EXP - 1, j))

            sp.wait_ge(tok_ready, 4)
            sp.dma_start(cmp_w1, a["cmp_w1_2"][0].rearrange("k (pp q) h -> q k pp h", q=P)).then_inc(cmp_in, 16)
            sp.dma_start(cmp_w2, a["cmp_w2_2"][0].rearrange("k q d -> q k d")).then_inc(cmp_in, 16)

            def ffn(u0, w1, w2):
                src = lambda c, j: ffn_src(a[w1], a[w2], c, j)
                chunks(u0, FFN_FULL, src)
                u = u0 + 4 + STEP * (FFN_FULL - 1)
                w1_, w2_ = a[w1][0], a[w2][0]
                c0 = 512 * FFN_FULL
                load(u, w1_[:, c0:c0 + 256].rearrange("(k p) n -> p k n", p=P), k=KT)
                load(u + 1, w1_[:, D_FF + c0:D_FF + c0 + 256].rearrange("(k p) n -> p k n", p=P), k=KT)
                load(u + 2, src(FFN_FULL - 1, 4))
                load(u + 3, src(FFN_FULL - 1, 5))
                load(u + 4, w2_[c0:c0 + 256, :].rearrange("(k p) n -> p k n", p=P), k=2)

            ffn(U_FFN1, "ffn1_w_in_2", "ffn1_w_out_2")
            def mix_load(u):
                g, kh = (u - U_MIX) // 2, (u - U_MIX) % 2
                load(u, unit_src(a["w_mix_in_2"][0], 512 * kh, 512 * g))


            for j in range(8):
                mix_load(U_MIX + j)
            for half in range(2):
                for kh in range(2):
                    load(U_MIXOUT + 2 * half + kh, unit_src(a["w_mix_out_2"][0], 512 * kh, 512 * half))
            sp.wait_ge(blk_summed, 1)
            sp.wait_ge(bias_stored, 32)
            for n in range(2):
                sp.dma_start(bias_t[:, n], bass.AP(bias_rows, n * HEADS * P * REL_W + P - 1,
                                                   [[REL_W - 1, P], [P * REL_W, HEADS], [1, S]])).then_inc(bias_in, 16)
            ffn(U_FFN2, "ffn2_w_in_2", "ffn2_w_out_2")
            for tt in range(TT):
                sp.wait_ge(out_ready, tt + 1)
                sp.dma_start(out[0, tt * P:(tt + 1) * P, :], x[:, tt, :]).then_inc(stored, 16)
            sp.wait_ge(stored, 16 * TT)

        @block.scalar
        def _(act):
            chain = Chain(act, act_seq)
            act.dma_start(dense[:, :, :], dense_dram).then_inc(const_in, 16)
            act.dma_start(masks[:, :, :], masks_dram).then_inc(const_in, 16)
            per_row = [("ln1_g", ROW_LN1, 8), ("ln2_g", ROW_LN2, 8), ("ffn1_norm_2", ROW_FFN1, 8), ("mix_norm_2", ROW_MIX, 8),
                       ("ffn2_norm_2", ROW_FFN2, 8), ("hg_norm_g", ROW_HGN, 4), ("hg_lb_logits", ROW_LB, 8)]
            for name, r0, n in per_row:
                act.dma_start(rows[r0:r0 + n, :], a[name].rearrange("a (b p) -> (a b) p", p=P)).then_inc(rows_in, 16)
            for name, r in (("q_norm_a_2", ROW_QA), ("k_norm_a_2", ROW_KA), ("q_norm_b_2", ROW_QB), ("k_norm_b_2", ROW_KB)):
                for c in range(2):
                    act.dma_start(rows[r:r + 1, c * DH:(c + 1) * DH], a[name]).then_inc(rows_in, 16)
            act.dma_start(wr_raw[:, :, 0:4], a["w_router_group"][0].rearrange("(k p) n -> p k n", p=P)).then_inc(wr_in, 16)
            act.dma_start(wr_raw[:, :, 4:20], a["w_router_expert"][0].rearrange("(k p) n -> p k n", p=P)).then_inc(wr_in, 16)
            act.dma_start(rb_row[:, 0:4], a["b_router_group"]).then_inc(small_in, 16)
            act.dma_start(rb_row[:, 4:20], a["b_router_expert"]).then_inc(small_in, 16)
            act.dma_start(rows[ROW_B1:ROW_B1 + 2, :], a["cmp_b1_2"][0]).then_inc(rows_in, 16)
            act.dma_start(rows[ROW_POS:ROW_POS + 2 * PAIRS, :],
                          a["cmp_pos_2"][0].rearrange("k (pp two) d -> (k pp) (two d)", two=2)).then_inc(rows_in, 16)
            act.dma_start(b2_row[:, :, :], a["cmp_b2_2"]).then_inc(small_in, 16)
            act.dma_start(sink, a["sinks_a_2"].broadcast_to([P, HEADS])).then_inc(small_in, 16)
            act.dma_start(tbl[0:32, :], a["rel_bias_table_2"]).then_inc(tbl_in, 16)
            act.dma_start(onehot[0:33], onehot_dram).then_inc(onehot_in, 16)

            def split_hi(u, i=None):
                if u >= U_END:
                    return
                act.wait_ge(raw_in[u % RAW], 16 * (u // RAW + 1) if i is None else 16 * i + 16 * (u // RAW + 1))
                if u >= SPLIT:
                    act.wait_ge(unit_used, u - SPLIT + 1 if i is None else STEP * i + (u - SPLIT + 1))
                act.activation(w_hi[:, u % SPLIT, :], w_raw[:, u % RAW, :], ACT.Copy).then_inc(hi_ready, 1)

            def rms(m):
                act.wait_ge(ss_ready, m + 1)
                act.activation(sc[:, 4:6], sc[:, 2:4], ACT.Sqrt, scale=1.0 / D, bias=sc[:, 0:1]).then_inc(rms_ready, 1)

            def transposed_hi(t, gain=None):
                for b in range(4):
                    act.wait_ge(xT_ready, 4 * t + b + 1)
                    for k in (2 * b, 2 * b + 1):
                        src = ps[:, b, (k % 2) * S:(k % 2 + 1) * S]
                        if gain is None:
                            ins = act.activation(h_hi[:, k, :], src, ACT.Copy)
                        else:
                            ins = act.activation(h_hi[:, k, :], src, ACT.Copy, scale=cols[:, gain + k:gain + k + 1])
                    ins.then_inc(hT_hi, 1)

            split_hi(0)
            rms(0)
            split_hi(1)
            act.wait_ge(cols_ready, 1)
            transposed_hi(0, ROW_LN1)
            act.wait_ge(lb_diff, 1)
            act.activation(small[:, 8:16], small[:, 0:8], ACT.Exp).then_inc(lb_exp, 1)

            def leave_proj(g):
                name = IN_ORDER[g]
                src = ps[:, 2 * (g % 4):2 * (g % 4) + 2, :]
                act.wait_ge(unit_used, U_IN + 2 * g + 2)
                if name == "q_sb":
                    ins = act.activation(stage[:, 0], src, ACT.Copy, scale=DH ** -0.5)
                elif name == "k_sb":
                    ins = act.activation(stage[:, 1], src, ACT.Copy)
                elif name == "v_sb":
                    ins = act.activation(v_sb, src, ACT.Copy)
                elif name == "i_hg":
                    ins = act.activation(v_hg, src, ACT.Copy)
                elif name == "q_hg":
                    ins = act.activation(stage[:, 2], src, ACT.Silu)
                elif name == "g_hg":
                    ins = act.activation(g_act, src, ACT.Silu)
                elif name == "f_hg":
                    ins = act.activation(stage[:, 3], src, ACT.Sigmoid)
                else:
                    ins = act.activation(gates[:, g - 7], src, ACT.Sigmoid)
                ins.then_inc(proj_out, 1)

            for g in range(11):
                if g < 10:
                    split_hi(2 * g + 2)
                    split_hi(2 * g + 3)
                leave_proj(g)

            def softplus_parts(ct):
                act.wait_ge(z_ready, ct + 1)
                if ct >= 2:
                    act.wait_ge(s_ready, ct - 1)
                zb = 2 * (ct % 2)
                chain(act.activation(soft[:, ct % 2], ps[:, zb:zb + 2, 0:384], ACT.Abs))
                chain(act.activation(soft[:, ct % 2], soft[:, ct % 2], ACT.Exp, scale=-1.0))
                act.activation(soft[:, ct % 2], soft[:, ct % 2], ACT.Ln, bias=1.0).then_inc(ln_ready, 1)

            def weights(ct):
                act.wait_ge(s_ready, ct + 1)
                if ct >= 2:
                    act.wait_ge(y_ready, ct - 1)
                act.activation(att[:, ct % 2], ps[:, 4:6, 0:384], ACT.Exp).then_inc(a_ready, 1)

            chain(act.activation(small[:, 100:101], sc[:, 0:1], ACT.Ln))
            act.wait_ge(sbT_ready, 2)
            act.wait_ge(hgT_ready, 5)
            softplus_parts(0)
            softplus_parts(1)
            for ct in range(4):
                weights(ct)
                if ct + 2 < 4:
                    softplus_parts(ct + 2)
            act.wait_ge(y_ready, 4)
            act.activation(h_hi[:, 0:4, :].rearrange("p (b k) s -> p b (k s)", b=2), ps[:, 6:8, :], ACT.Copy).then_inc(ysb_hi, 1)

            for j in range(3):
                split_hi(U_BRANCH + j)
            act.wait_ge(o_ready, 1)
            act.activation(o_sq, ps[:, 2:4, :], ACT.Square).then_inc(osq_ready, 1)
            act.wait_ge(orms_in, 1)
            act.activation(small[:, 64:80], small[:, 48:64], ACT.Sqrt, scale=1.0 / DH, bias=sc[:, 0:1]).then_inc(orms_ready, 1)
            act.wait_ge(oT_ready, 1)
            for ct in range(4):
                i = act.activation(h_hi[:, 4 + ct, :], ps[:, 4 + ct // 2, (ct % 2) * S:(ct % 2 + 1) * S], ACT.Copy,
                                   scale=cols[:, ROW_HGN + ct:ROW_HGN + ct + 1])
            i.then_inc(yhg_hi, 1)

            split_hi(U_BRANCH + 3)
            for j in range(3):
                split_hi(U_OUT + j)
            transposed_hi(1)
            split_hi(U_OUT + 3)
            split_hi(U_MOE)
            act.wait_ge(wr_in, 32)
            act.activation(wr_hi[:, :, 0:20], wr_raw[:, :, 0:20], ACT.Copy).then_inc(wr_split_hi, 1)
            split_hi(U_MOE + 1)
            rms(1)
            split_hi(U_MOE + 2)
            transposed_hi(2, ROW_LN2)

            def route_exps():
                act.wait_ge(route_sub, 1)
                chain(act.activation(sc[:, 80:88], sc[:, 80:88], ACT.Exp))
                act.wait_ge(route_sub, 2)
                act.activation(sc[:, 148:150], sc[:, 146:148], ACT.Exp).then_inc(route_exp, 2)

            def silu(c, u_gate, width=512):
                act.wait_ge(unit_used, u_gate + 1)
                if not (isinstance(c, int) and c == 0):
                    act.wait_ge(a_done, c)
                act.activation(act_s[:, :, 0:width], ps[:, 0:2, 0:width], ACT.Silu).then_inc(silu_done, 1)

            def aT_hi_out(c, n_f=4):
                for tt in range(TT):
                    act.wait_ge(aT_done, 2 * c + (tt + 1))
                    act.activation(aT_hi[:, 0:n_f, tt * P:(tt + 1) * P],
                                   ps[:, 2 + tt, 0:n_f * P].rearrange("p (f t) -> p f t", f=n_f), ACT.Copy).then_inc(aT_hi_r, 1)

            def chunks(u0, c0, n):
                split_hi(u0 + 3)
                if c0 == 0:
                    split_hi(u0 + 4)
                    route_exps()
                silu(c0, u0 + 1)
                if c0:
                    split_hi(u0 + 4)
                split_hi(u0 + 5)
                aT_hi_out(c0)
                split_hi(u0 + 6)
                s0 = u0 + 4
                with act.Fori(0, n - 1) as i:
                    split_hi(s0 + 3, i)
                    split_hi(s0 + 4, i)
                    silu(i + (c0 + 1), STEP * i + (s0 + 1))
                    split_hi(s0 + 5, i)
                    split_hi(s0 + 6, i)
                    split_hi(s0 + 7, i)
                    aT_hi_out(i + (c0 + 1))
                    split_hi(s0 + 8, i)
                return s0 + STEP * (n - 1)

            u = chunks(U_MOE, 0, N_EXP)
            assert u == U_FFN1 - 2
            split_hi(U_FFN1 + 1)
            split_hi(U_FFN1 + 2)
            rms(2)
            rms(3)
            transposed_hi(3, ROW_FFN1)

            def ffn(u0, c0):
                u = chunks(u0, c0, FFN_FULL)
                split_hi(u + 3)
                silu(c0 + FFN_FULL, u, 256)
                split_hi(u + 4)
                split_hi(u + 5)
                split_hi(u + 6)
                aT_hi_out(c0 + FFN_FULL, 2)
                split_hi(u + 7)

            ffn(U_FFN1, N_EXP)

            act.wait_ge(wr2_in, 16)
            act.wait_ge(route_T, 1)
            act.activation(wr_hi[:, :, :], wr_raw[:, :, :], ACT.Copy).then_inc(wr_split_hi, 1)
            rms(4)
            transposed_hi(4, ROW_MIX)
            for g in range(4):
                split_hi(U_MIX + 2 * g + 3)
                split_hi(U_MIX + 2 * g + 4)
                act.wait_ge(unit_used, U_MIX + 2 * g + 2)
                cs = slice(512 * g, 512 * g + 512)
                act.activation(proj[:, :, cs], ps[:, 2 * g:2 * g + 2, :], ACT.Copy).then_inc(mix_out, 1)
                act.activation(sq[:, :, cs], ps[:, 2 * g:2 * g + 2, :], ACT.Square).then_inc(mix_out, 1)
            act.wait_ge(gates_T, 1)
            act.activation(gate_sig, ps[:, 0, 0:64].rearrange("p (t c) -> p t c", t=TT)[:, :, 0:GATE_COLS], ACT.Sigmoid).then_inc(gsig_ready, 1)
            act.wait_ge(blk_summed, 1)
            act.activation(blk_r, blk_ss, ACT.Sqrt, scale=1.0 / DH, bias=sc[:, 0:1]).then_inc(blk_rms, 1)
            act.wait_ge(bias2_set, 1)
            for kv in range(2):
                i = act.activation(hidT[:, kv, 0:30], ps[:, 2, 64 * kv:64 * kv + 30], ACT.Silu, bias=bias2[:, kv:kv + 1])
            i.then_inc(hid_ready, 1)
            act.wait_ge(kvc_ready, 1)
            act.activation(kc_sq[0:N_CMP], ps[0:N_CMP, 3, 0:P], ACT.Square).then_inc(kcsq_ready, 1)
            act.wait_ge(kcss_ready, 1)
            act.activation(kc_r[0:N_CMP], kc_ss[0:N_CMP], ACT.Sqrt, scale=1.0 / DH, bias=sc[0:N_CMP, 0:1]).then_inc(kcr_ready, 1)

            def exps(n):
                kind, h = n // HEADS, n % HEADS
                w = prob[:, n % 4]
                act.wait_ge(neg_ready, n + 1)
                for qt in range(TT):
                    cs = key_cols(kind, qt)
                    k = 16 * kind + 8 * qt + h
                    i = act.activation(w[:, cs], w[:, cs], ACT.Exp, scale=-1.0, bias=negm[:, k:k + 1], accum_out=sums[:, k:k + 1])
                i.then_inc(p_ready, 1)

            for n in range(4 * HEADS):
                exps(n)
                if n == HEADS + 1:
                    act.wait_ge(sink_ready, 1)
                    act.activation(sink_t, sink_t, ACT.Exp).then_inc(sinkexp, 1)

            transposed_hi(5)
            split_hi(U_MIXOUT + 3)
            split_hi(U_FFN2)
            rms(5)
            split_hi(U_FFN2 + 1)
            split_hi(U_FFN2 + 2)
            transposed_hi(6, ROW_FFN2)
            ffn(U_FFN2, N_EXP + FFN_FULL + 1)

        @block.vector
        def _(dve):
            chain = Chain(dve, dve_seq)
            chain(dve.memset(sc[:, 0:1], EPS))

            def split_lo(u, i=None):
                if u >= U_END:
                    return
                dve.wait_ge(hi_ready, u + 1 if i is None else STEP * i + (u + 1))
                dve.tensor_tensor(w_lo[:, u % SPLIT, :], w_raw[:, u % RAW, :], w_hi[:, u % SPLIT, :],
                                  ALU.subtract).then_inc(lo_ready, 1)

            def square_sums():
                for t in range(TT):
                    ins = dve.tensor_tensor_reduce(out=tok[:, t, :], in0=x[:, t, :], in1=x[:, t, :], scale=1.0,
                                                   scalar=0.0, op0=ALU.mult, op1=ALU.add,
                                                   accum_out=sc[:, 2 + t:3 + t])
                ins.then_inc(ss_ready, 1)

            def normalize(m):
                dve.wait_ge(rms_ready, m + 1)
                chain(dve.reciprocal(sc[:, 6:8], sc[:, 4:6]))
                for t in range(TT):
                    dve.tensor_scalar(tok[:, t, :], x[:, t, :], sc[:, 6 + t:7 + t], None, ALU.mult).then_inc(tok_ready, 1)

            def transposed_lo(t, gain=None):
                for b in range(4):
                    dve.wait_ge(hT_hi, 4 * t + b + 1)
                    for k in (2 * b, 2 * b + 1):
                        src = ps[:, b, (k % 2) * S:(k % 2 + 1) * S]
                        if gain is None:
                            ins = dve.tensor_tensor(h_lo[:, k, :], src, h_hi[:, k, :], ALU.subtract)
                        else:
                            ins = dve.scalar_tensor_tensor(out=h_lo[:, k, :], in0=src, scalar=cols[:, gain + k:gain + k + 1],
                                                           in1=h_hi[:, k, :], op0=ALU.mult, op1=ALU.subtract)
                    ins.then_inc(hT_lo, 1)

            dve.wait_ge(x_in, 16)
            square_sums()
            normalize(0)
            dve.wait_ge(cols_T, 1)
            dve.tensor_copy(cols[:, 0:N_ROWS], ps[:, 7, 0:N_ROWS]).then_inc(cols_ready, 1)
            dve.wait_ge(bias_done, 1)
            dve.tensor_copy(bias_out[0:HEADS], ps[0:HEADS, 5:7, 0:REL_W]).then_inc(bias_sb, 1)
            split_lo(0)
            split_lo(1)
            transposed_lo(0, ROW_LN1)
            dve.wait_ge(cols_ready, 1)
            l0, l1 = cols[:, ROW_LB:ROW_LB + 4], cols[:, ROW_LB + 4:ROW_LB + 8]
            chain(dve.tensor_tensor(small[:, 16:20], l0, l1, ALU.max))
            dve.tensor_tensor(small[:, 0:4], l0, small[:, 16:20], ALU.subtract)
            dve.tensor_tensor(small[:, 4:8], l1, small[:, 16:20], ALU.subtract).then_inc(lb_diff, 1)
            dve.wait_ge(lb_exp, 1)
            chain(dve.tensor_tensor(small[:, 20:24], small[:, 8:12], small[:, 12:16], ALU.add))
            chain(dve.reciprocal(small[:, 24:28], small[:, 20:24]))
            chain(dve.tensor_tensor(small[:, 28:32], small[:, 8:12], small[:, 24:28], ALU.mult))
            dve.tensor_scalar(small[:, 32:36], small[:, 28:32], -1.0, 1.0, ALU.mult, ALU.add).then_inc(lb_ready, 1)

            for g in range(10):
                split_lo(2 * g + 2)
                split_lo(2 * g + 3)

            dve.wait_ge(stage_T, 1)
            dve.tensor_copy(qT.rearrange("p (b k) s -> p b (k s)", b=2), ps[:, 0:2, :]).then_inc(sbT_ready, 1)
            dve.wait_ge(stage_T, 2)
            dve.tensor_copy(kT.rearrange("p (b k) s -> p b (k s)", b=2), ps[:, 2:4, :]).then_inc(sbT_ready, 1)
            dve.wait_ge(stage_T, 3)
            dve.tensor_copy(qhT.rearrange("p (b k) s -> p b (k s)", b=2), ps[:, 4:6, :]).then_inc(hgT_ready, 1)
            dve.wait_ge(stage_T, 4)
            dve.wait_ge(bias_stored, 32)
            for ct in range(4):
                dve.tensor_scalar(pre[:, ct, :], ps[:, 6 + ct // 2, (ct % 2) * S:(ct % 2 + 1) * S], small[:, 32 + ct:33 + ct],
                                  small[:, 28 + ct:29 + ct], ALU.mult, ALU.add).then_inc(hgT_ready, 1)

            def softplus(ct):
                dve.wait_ge(ln_ready, ct + 1)
                zb = 2 * (ct % 2)
                dve.scalar_tensor_tensor(out=soft[:, ct % 2], in0=ps[:, zb:zb + 2, 0:384], scalar=0.0, in1=soft[:, ct % 2],
                                         op0=ALU.max, op1=ALU.add).then_inc(sp_ready, 1)

            for ct in range(4):
                softplus(ct)
            dve.wait_ge(ysb_hi, 1)
            dve.tensor_tensor(h_lo[:, 0:4, :].rearrange("p (b k) s -> p b (k s)", b=2), ps[:, 6:8, :],
                              h_hi[:, 0:4, :].rearrange("p (b k) s -> p b (k s)", b=2), ALU.subtract).then_inc(ysb_lo, 1)

            for j in range(3):
                split_lo(U_BRANCH + j)
            dve.tensor_scalar(hk, pre, -1.0, 1.0, ALU.mult, ALU.add).then_inc(zeroed, 1)
            kdec_v = [k_dec[:, b].rearrange("p c s -> p (c s)") for b in range(2)]
            qdec_v = [q_dec[:, b].rearrange("p c s -> p (c s)") for b in range(2)]
            hk_f, qh_f = hk.rearrange("p c s -> p (c s)"), qhT.rearrange("p c s -> p (c s)")
            pre_f, suf_f = pre.rearrange("p c s -> p (c s)"), suf.rearrange("p c s -> p (c s)")
            dve.wait_ge(zeroed, 5)

            def keep(n, mask):
                for b in range(4):
                    dve.wait_ge(level_done, 4 * n + b + 1)
                    if n:
                        dve.wait_ge(level_kept, 4 * (n - 1) + b + 1)
                    dve.copy_predicated(sc_near[:, 4 * b:4 * b + 4, :],
                                        masks[:, mask:mask + 1, :].broadcast_to([P, 4, P]),
                                        ps[:, 4 * (n % 2) + b, :].rearrange("p (c t) -> p c t", c=4)).then_inc(level_kept, 1)

            def halves(v, h):
                return v.rearrange("p (n two h) -> p n two h", two=2, h=h)

            for level in range(LEVELS):
                h, b = 1 << level, level % 2
                if level >= 2:
                    dve.wait_ge(level_done, 4 * level)
                dve.tensor_tensor(halves(qdec_v[b], h)[:, :, 1, :], halves(qh_f, h)[:, :, 1, :], halves(pre_f, h)[:, :, 1, :], ALU.mult)
                dve.tensor_tensor(halves(kdec_v[b], h)[:, :, 0, :], halves(hk_f, h)[:, :, 0, :], halves(suf_f, h)[:, :, 0, :],
                                  ALU.mult).then_inc(qdec_ready, 1)
                n = 4 * S // (2 * h)
                chain(dve.tensor_tensor(halves(suf_f, h)[:, :, 0, :], halves(suf_f, h)[:, :, 0, :],
                                        halves(pre_f, h)[:, :, 1, h - 1:h].broadcast_to([P, n, h]), ALU.mult))
                chain(dve.tensor_tensor(halves(pre_f, h)[:, :, 1, :], halves(pre_f, h)[:, :, 1, :],
                                        halves(pre_f, h)[:, :, 0, h - 1:h].broadcast_to([P, n, h]), ALU.mult))
                if level == 0:
                    keep(0, LEVELS)
                else:
                    keep(level, level - 1)
            dve.wait_ge(level_done, 4 * LEVELS)
            dve.tensor_tensor(q_dec[:, 1, :, P:S], qhT[:, :, P:S], pre[:, :, P:S], ALU.mult)
            dve.tensor_tensor(k_dec[:, 1, :, 0:P], hk[:, :, 0:P], suf[:, :, 0:P], ALU.mult).then_inc(qdec_ready, 1)
            keep(LEVELS, LEVELS - 1)
            dve.wait_ge(far_ready, 1)
            dve.tensor_copy(sc_far.rearrange("p a b t -> p a (b t)"), ps[:, 0:2, :]).then_inc(level_kept, 1)
            dve.wait_ge(osq_ready, 1)
            dve.tensor_reduce(small[:, 48:64], o_sq.rearrange("p t (h d) -> p (t h) d", d=DH), AX, ALU.add).then_inc(orms_in, 1)
            chain(dve.tensor_tensor(o_gated, ps[:, 2:4, :], g_act, ALU.mult))
            dve.wait_ge(orms_ready, 1)
            chain(dve.reciprocal(small[:, 80:96], small[:, 64:80]))
            og = o_gated.rearrange("p t (h d) -> p (t h) d", d=DH)
            dve.tensor_tensor(og, og, small[:, 80:96].unsqueeze(2).broadcast_to([P, TT * HEADS, DH]), ALU.mult).then_inc(og_ready, 1)
            dve.wait_ge(yhg_hi, 1)
            for ct in range(4):
                i = dve.scalar_tensor_tensor(out=h_lo[:, 4 + ct, :], in0=ps[:, 4 + ct // 2, (ct % 2) * S:(ct % 2 + 1) * S],
                                             scalar=cols[:, ROW_HGN + ct:ROW_HGN + ct + 1], in1=h_hi[:, 4 + ct, :],
                                             op0=ALU.mult, op1=ALU.subtract)
            i.then_inc(yhg_lo, 1)

            split_lo(U_BRANCH + 3)
            part = o_sq
            for half in range(2):
                cs = slice(512 * half, 512 * half + 512)
                dve.wait_ge(unit_used, U_BRANCH + 2 * half + 1)
                chain(dve.tensor_tensor(tok[:, :, cs], ps[:, 4 * half:4 * half + 2, :], gates[:, half], ALU.mult))
                dve.wait_ge(unit_used, U_BRANCH + 2 * half + 2)
                chain(dve.tensor_tensor(part, ps[:, 4 * half + 2:4 * half + 4, :], gates[:, 2 + half], ALU.mult))
                dve.tensor_tensor(tok[:, :, cs], tok[:, :, cs], part, ALU.add).then_inc(tok_ready, 1)
                split_lo(U_OUT + half)
            split_lo(U_OUT + 2)
            transposed_lo(1)
            split_lo(U_OUT + 3)
            split_lo(U_MOE)
            dve.wait_ge(wr_split_hi, 1)
            dve.tensor_tensor(wr_lo[:, :, 0:20], wr_raw[:, :, 0:20], wr_hi[:, :, 0:20], ALU.subtract).then_inc(wr_split_lo, 1)

            def residual(u0, scale=None):
                for half in range(2):
                    cs = slice(512 * half, 512 * half + 512)
                    dve.wait_ge(unit_used, u0 + 2 * half + 2)
                    chain(dve.tensor_tensor(x[:, :, cs], ps[:, 4 + 2 * half:6 + 2 * half, :], x[:, :, cs], ALU.add))

            residual(U_OUT)
            square_sums()
            split_lo(U_MOE + 1)
            normalize(1)
            split_lo(U_MOE + 2)
            transposed_lo(2, ROW_LN2)

            def first_best(dst, src, tmp, best):
                b3 = best.unsqueeze(2).broadcast_to([P, TT, 4])
                chain(dve.tensor_tensor(tmp, src, b3, ALU.is_ge))
                chain(dve.tensor_tensor(tmp, tmp, descend, ALU.mult))
                chain(dve.tensor_reduce(sc[:, 16:18], tmp, AX, ALU.max))
                chain(dve.tensor_tensor(dst, tmp, sc[:, 16:18].unsqueeze(2).broadcast_to([P, TT, 4]), ALU.is_equal))

            def v3(o, n, w):
                return sc[:, o:o + n * w].rearrange("p (a b) -> p a b", a=n)

            def wide(v):
                return v.unsqueeze(2).broadcast_to([P, TT, 4])

            descend = v3(20, TT, 4)
            for tt in range(TT):
                for j in range(4):
                    chain(dve.memset(sc[:, 20 + 4 * tt + j:21 + 4 * tt + j], float(4 - j)))
            lg = v3(32, TT, 20)
            e3, oh_g, tmp4, ig, oh1, oh2, inner = (v3(o, TT, 4) for o in (80, 88, 96, 104, 112, 120, 128))
            prod = sc[:, 160:192]
            comb = sc[:, 192:224].rearrange("p (t e) -> p t e", t=TT)
            gmax, gsum, w_grp, m1, m2, dm, e2, w1, w2 = (sc[:, o:o + 2] for o in range(136, 154, 2))

            def route():
                dve.wait_ge(route_T, 1)
                chain(dve.tensor_copy(lg, ps[:, 7, 0:64].rearrange("p (t c) -> p t c", t=TT)[:, :, 0:20]))
                chain(dve.tensor_reduce(gmax, lg[:, :, 0:4], AX, ALU.max))
                dve.tensor_tensor(e3, lg[:, :, 0:4], wide(gmax), ALU.subtract).then_inc(route_sub, 1)
                first_best(oh_g, lg[:, :, 0:4], tmp4, gmax)
                for tt in range(TT):
                    pv = prod[:, 16 * tt:16 * tt + 16].rearrange("p (g j) -> p g j", g=4)
                    chain(dve.tensor_tensor(pv, lg[:, tt, 4:20].rearrange("p (g j) -> p g j", g=4),
                                            oh_g[:, tt, :].unsqueeze(2).broadcast_to([P, 4, 4]), ALU.mult))
                chain(dve.tensor_reduce(ig, prod.rearrange("p (t g j) -> p t j g", t=TT, g=4), AX, ALU.add))
                chain(dve.tensor_reduce(m1, ig, AX, ALU.max))
                first_best(oh1, ig, tmp4, m1)
                chain(dve.scalar_tensor_tensor(out=tmp4, in0=oh1, scalar=-3e38, in1=ig, op0=ALU.mult, op1=ALU.add))
                chain(dve.tensor_reduce(m2, tmp4, AX, ALU.max))
                chain(dve.tensor_copy(ig, tmp4))
                first_best(oh2, ig, tmp4, m2)
                dve.tensor_tensor(dm, m2, m1, ALU.subtract).then_inc(route_sub, 1)
                dve.wait_ge(route_exp, 2)
                chain(dve.tensor_reduce(gsum, e3, AX, ALU.add))
                chain(dve.reciprocal(w_grp, gsum))
                chain(dve.tensor_scalar(w1, e2, 1.0, None, ALU.add))
                chain(dve.reciprocal(w1, w1))
                chain(dve.tensor_tensor(w2, e2, w1, ALU.mult))
                chain(dve.tensor_tensor(w1, w1, w_grp, ALU.mult))
                chain(dve.tensor_tensor(w2, w2, w_grp, ALU.mult))
                chain(dve.tensor_tensor(oh1, oh1, wide(w1), ALU.mult))
                chain(dve.tensor_tensor(oh2, oh2, wide(w2), ALU.mult))
                chain(dve.tensor_tensor(inner, oh1, oh2, ALU.add))
                for tt in range(TT):
                    chain(dve.tensor_tensor(comb[:, tt, :].rearrange("p (g j) -> p g j", g=4),
                                            oh_g[:, tt, :].unsqueeze(2).broadcast_to([P, 4, 4]),
                                            inner[:, tt, :].unsqueeze(1).broadcast_to([P, 4, 4]), ALU.mult))

            coef = sc[:, 8:10]

            def gated(c, u_up, width=512):
                dve.wait_ge(silu_done, c + 1)
                dve.wait_ge(unit_used, u_up + 1)
                if not (isinstance(c, int) and c == 0):
                    dve.wait_ge(aT_done, 2 * c)
                dve.tensor_tensor(act_a[:, :, 0:width], ps[:, 2:4, 0:width], act_s[:, :, 0:width], ALU.mult).then_inc(a_done, 1)

            def aT_lo_out(c, n_f=4):
                for tt in range(TT):
                    dve.wait_ge(aT_hi_r, 2 * c + (tt + 1))
                    dve.tensor_tensor(aT_lo[:, 0:n_f, tt * P:(tt + 1) * P],
                                      ps[:, 2 + tt, 0:n_f * P].rearrange("p (f t) -> p f t", f=n_f),
                                      aT_hi[:, 0:n_f, tt * P:(tt + 1) * P], ALU.subtract).then_inc(aT_lo_r, 1)

            def add_down(half, before, u_down):
                cs = slice(512 * half, 512 * half + 512)
                dve.wait_ge(unit_used, u_down + 1)
                dve.wait_ge(down_added, before)
                for tt in range(TT):
                    dve.scalar_tensor_tensor(out=x[:, tt, cs], in0=ps[:, 4 + 2 * half + tt, :], scalar=coef[:, tt:tt + 1],
                                             in1=x[:, tt, cs], op0=ALU.mult, op1=ALU.add).then_inc(down_added, 1)

            def chunks(u0, c0, n, adds0, between=None, each=None):
                split_lo(u0 + 3)
                split_lo(u0 + 4)
                if between is not None:
                    between()
                gated(c0, u0 + 3)
                split_lo(u0 + 5)
                aT_lo_out(c0)
                split_lo(u0 + 6)
                s0 = u0 + 4
                with dve.Fori(0, n - 1) as i:
                    split_lo(s0 + 3, i)
                    split_lo(s0 + 4, i)
                    split_lo(s0 + 5, i)
                    gated(i + (c0 + 1), STEP * i + (s0 + 3))
                    split_lo(s0 + 6, i)
                    add_down(0, 4 * i + adds0, STEP * i + (s0 + 4))
                    split_lo(s0 + 7, i)
                    aT_lo_out(i + (c0 + 1))
                    split_lo(s0 + 8, i)
                    add_down(1, 4 * i + adds0, STEP * i + (s0 + 5))
                    if each is not None:
                        each(i)
                return s0 + STEP * (n - 1)

            def next_coef(i):
                dve.wait_ge(down_added, 4 * i + 8)
                dve.tensor_copy(coef.unsqueeze(2), comb[:, :, bass.ds(i + 1, 1)]).then_inc(coef_set, 1)
                dve.wait_ge(coef_set, i + 2)

            def first_coef():
                route()
                dve.tensor_copy(coef.unsqueeze(2), comb[:, :, 0:1]).then_inc(coef_set, 1)
                dve.wait_ge(coef_set, 1)
                dve.tensor_copy(sc[:, 10:12], coef).then_inc(down_added, 4)

            u = chunks(U_MOE, 0, N_EXP, 4, first_coef, next_coef)
            adds = 4 + 4 * (N_EXP - 1)
            add_down(0, adds, u)
            split_lo(U_FFN1 + 1)
            add_down(1, adds, u + 1)
            dve.wait_ge(down_added, adds + 4)
            square_sums()
            split_lo(U_FFN1 + 2)
            dve.wait_ge(rms_ready, 3)
            chain(dve.reciprocal(sc[:, 6:8], sc[:, 4:6]))
            dve.wait_ge(fg_in, 16)
            for t in range(TT):
                i = dve.scalar_tensor_tensor(out=x[:, t, :], in0=x[:, t, :], scalar=sc[:, 6 + t:7 + t], in1=final_g,
                                             op0=ALU.mult, op1=ALU.mult)
            chain(i)
            square_sums()
            normalize(3)
            transposed_lo(3, ROW_FFN1)

            def ffn(u0, c0, phase, adds):
                dve.wait_ge(down_added, adds)
                chain(dve.memset(coef, 0.5))
                dve.tensor_copy(sc[:, 10:12], coef).then_inc(down_added, 4)
                adds += 4
                u = chunks(u0, c0, FFN_FULL, adds)
                adds += 4 * (FFN_FULL - 1)
                c = c0 + FFN_FULL
                split_lo(u + 3)
                gated(c, u + 1, 256)
                split_lo(u + 4)
                split_lo(u + 5)
                add_down(0, adds, u + 2)
                split_lo(u + 6)
                add_down(1, adds, u + 3)
                aT_lo_out(c, 2)
                split_lo(u + 7)
                adds += 4
                add_down(0, adds, u + 4)
                add_down(1, adds, u + 4)
                return adds + 4

            adds = ffn(U_FFN1, N_EXP, 1, adds + 4)
            dve.wait_ge(down_added, adds)

            dve.wait_ge(wr_split_hi, 2)
            dve.tensor_tensor(wr_lo[:, :, :], wr_raw[:, :, :], wr_hi[:, :, :], ALU.subtract).then_inc(wr_split_lo, 1)
            square_sums()
            normalize(4)
            transposed_lo(4, ROW_MIX)
            ss = blk_ss.rearrange("p (t b) -> p t b", t=TT)
            for g in range(4):
                split_lo(U_MIX + 2 * g + 3)
                split_lo(U_MIX + 2 * g + 4)
                dve.wait_ge(mix_out, 2 * g + 2)
                for t in range(TT):
                    i = dve.tensor_reduce(ss[:, t, 8 * g:8 * g + 8], sq[:, t, 512 * g:512 * g + 512].rearrange("p (b d) -> p b d", d=DH), AX, ALU.add)
            i.then_inc(blk_summed, 1)
            dve.wait_ge(pos_set, 1)
            pos = kvT[:, :, 2, 0:2 * PAIRS].rearrange("p k (q two) -> p k q two", two=2)[:, :, :, 0]
            dve.tensor_copy(pos, cols[:, ROW_POS:ROW_POS + 2 * PAIRS].rearrange("p (k q) -> p k q", k=2)).then_inc(kvT_ready, 1)
            dve.wait_ge(kv_T, 1)
            kvp = ps[:, 1, :].rearrange("p (k s) -> p k s", k=2)
            for g in range(2):
                src = kvp[g * DH:(g + 1) * DH]
                dve.tensor_copy(kvT[0:DH, :, g, :], src).then_inc(kvT_ready, 1)
                dve.tensor_copy(kvT[DH:P, :, g, 0:S - 1], src[:, :, 1:S]).then_inc(kvT_ready, 1)
            dve.wait_ge(blk_rms, 1)
            chain(dve.reciprocal(blk_ss, blk_r))
            for c0 in (0, OFF_QB):
                v = proj[:, :, c0:c0 + 512].rearrange("p t (b d) -> p t b d", d=DH)
                dve.tensor_tensor(v, v, ss[:, :, c0 // DH:c0 // DH + 8].unsqueeze(3).broadcast_to([P, TT, 8, DH]), ALU.mult).then_inc(q_normed, 1)
            for n, c0 in enumerate((OFF_KA, OFF_KS, OFF_KW)):
                v = proj[:, :, c0:c0 + P].rearrange("p t (b d) -> p t b d", d=DH)
                for dup in range(2):
                    dve.tensor_tensor(k_dup[:, :, 2 * n:2 * n + 2, dup * DH:(dup + 1) * DH], v,
                                      ss[:, :, c0 // DH:c0 // DH + 2].unsqueeze(3).broadcast_to([P, TT, 2, DH]), ALU.mult).then_inc(k_normed, 1)
            dve.tensor_scalar(gain8[:, 0:1], cols[:, ROW_QA:ROW_QA + 1], DH ** -0.5, None, ALU.mult)
            chain(dve.tensor_scalar(gain8[:, 1:2], cols[:, ROW_QB:ROW_QB + 1], DH ** -0.5, None, ALU.mult))
            dve.wait_ge(small_in, 64)
            chain(dve.tensor_scalar(nsink, sink, -1.0, None, ALU.mult))
            dve.wait_ge(pre_T, 1)
            pos_cols = ps[:, 2, 0:P].rearrange("p (k c) -> p k c", k=2)[:, :, 30]
            dve.tensor_tensor(bias2, pos_cols, cols[:, ROW_B1:ROW_B1 + 2], ALU.add).then_inc(bias2_set, 1)
            for n in range(2):
                dve.wait_ge(qk_T, n + 1)
                dve.tensor_scalar(qqT[:, n].rearrange("p (b k) s -> p b (k s)", b=2), ps[:, 4 + 2 * n:6 + 2 * n, :], gain8[:, n:n + 1], None,
                                  ALU.mult).then_inc(qk_set, 1)
            dve.wait_ge(kcsq_ready, 1)
            dve.tensor_reduce(kc_ss[0:N_CMP], kc_sq[0:N_CMP].rearrange("p (g d) -> p g d", g=2), AX, ALU.add).then_inc(kcss_ready, 1)
            dve.tensor_copy(v_c[0:N_CMP], ps[0:N_CMP, 3, P:2 * P]).then_inc(kcT_set, 1)
            for n in range(3):
                dve.wait_ge(qk_T, n + 3)
                gain = ROW_KA if n == 0 else ROW_KB
                bank = (0, 1, 4)[n]
                dve.tensor_scalar(kkT[:, 2 * n:2 * n + 2, :].rearrange("p k s -> p (k s)"), ps[:, bank, :], cols[:, gain:gain + 1], None,
                                  ALU.mult).then_inc(qk_set, 1)
            dve.wait_ge(kcr_ready, 1)
            chain(dve.reciprocal(kc_ss[0:N_CMP], kc_r[0:N_CMP]))
            for g in range(2):
                for dup in range(2):
                    dve.tensor_scalar(kc_n[0:N_CMP, g, dup], ps[0:N_CMP, 3, g * DH:(g + 1) * DH], kc_ss[0:N_CMP, g:g + 1], None,
                                      ALU.mult).then_inc(kcn_ready, 1)
            dve.wait_ge(kcT_T, 1)
            dve.tensor_scalar(kcT[:, :, 0:N_CMP], ps[:, 5, 0:32].rearrange("p (g c) -> p g c", g=2)[:, :, 0:N_CMP],
                              cols[:, ROW_KB:ROW_KB + 1], None, ALU.mult).then_inc(kcT_set, 1)

            def neg_logits(n):
                kind, h = n // HEADS, n % HEADS
                dve.wait_ge(lg_ready, n + 1)
                if n >= 4:
                    dve.wait_ge(pT_ready, n - 3)
                for qt in range(TT):
                    cs = key_cols(kind, qt)
                    k = 16 * kind + 8 * qt + h
                    b = bias_t[:, KINDS[kind][3], h]
                    if kind < 3:
                        b = b[:, P:S] if qt == 0 else b
                    else:
                        b = b[:, (P + CMP_LEN - 1 if qt == 0 else CMP_LEN - 1)::CMP_STRIDE]
                    start = nsink[:, h:h + 1] if kind == 0 else (3e38 if kind < 3 else FAR)
                    i = dve.tensor_tensor_reduce(out=prob[:, n % 4, cs], in0=ps[:, n % 4, cs], in1=b, scale=-1.0, scalar=start,
                                                 op0=ALU.add, op1=ALU.min, accum_out=negm[:, k:k + 1])
                i.then_inc(neg_ready, 1)

            def probs_T(n):
                dve.wait_ge(pT_ready, n + 1)
                if n >= 2:
                    dve.wait_ge(pv_done, n - 1)
                if n < 3 * HEADS:
                    dve.tensor_copy(probT[:, n % 2], ps[:, 4 + n % 2, 0:384]).then_inc(pT_set, 1)
                else:
                    dve.tensor_copy(probT[0:7, n % 2, 0:P], ps[0:7, 4 + n % 2, 0:P])
                    dve.tensor_copy(probT[0:N_CMP, n % 2, P:S], ps[0:N_CMP, 4 + n % 2, P:S]).then_inc(pT_set, 1)

            def sink_diff():
                dve.wait_ge(neg_ready, HEADS)
                dve.tensor_tensor(sink_t.rearrange("p (t h) -> p t h", t=TT), negm[:, 0:16].rearrange("p (t h) -> p t h", t=TT),
                                  sink.unsqueeze(1).broadcast_to([P, TT, HEADS]), ALU.add).then_inc(sink_ready, 1)

            def keep_kind(kind):
                sl = slice(16 * kind, 16 * kind + 16)
                dve.wait_ge(p_ready, HEADS * (kind + 1))
                if kind == 0:
                    dve.wait_ge(sinkexp, 1)
                    chain(dve.tensor_tensor(sums[:, sl], sums[:, sl], sink_t, ALU.add))
                if kind == 3:
                    chain(dve.tensor_scalar(sums[:, sl], sums[:, sl], TINY, None, ALU.max))
                chain(dve.reciprocal(o_scale[:, sl], sums[:, sl]))
                if kind:
                    gi = (None, 1, 2, 0)[kind]
                    v = o_scale[:, sl].rearrange("p (t h) -> p t h", t=TT)
                    dve.wait_ge(gsig_ready, 1)
                    chain(dve.tensor_tensor(v, v, gate_sig[:, :, HEADS * gi:HEADS * gi + HEADS], ALU.mult))
                dve.wait_ge(pv_done, HEADS * (kind + 1))
                o = ps[:, 6:8, :].rearrange("p t (h d) -> p t h d", d=DH)
                sv = o_scale[:, sl].rearrange("p (t h) -> p t h", t=TT).unsqueeze(3).broadcast_to([P, TT, HEADS, DH])
                dst = tok[:, :, 0:512] if kind == 0 else tok[:, :, 512:D]
                if kind < 2:
                    i = dve.tensor_tensor(dst.rearrange("p t (h d) -> p t h d", d=DH), o, sv, ALU.mult)
                    i.then_inc(o_used, 1)
                else:
                    dve.tensor_tensor(o_part.rearrange("p t (h d) -> p t h d", d=DH), o, sv, ALU.mult).then_inc(o_used, 1)
                    dve.wait_ge(o_used, kind + 1)
                    chain(dve.tensor_tensor(dst, dst, o_part, ALU.add))

            dve.wait_ge(bias_in, 32)
            for s in range(4 * HEADS + 4):
                if s < 4 * HEADS:
                    neg_logits(s)
                if s == HEADS:
                    sink_diff()
                if 2 <= s < 4 * HEADS + 2:
                    probs_T(s - 2)
                if s >= HEADS + 3 and (s - 3) % HEADS == 0:
                    keep_kind((s - 3) // HEADS - 1)
            dve.tensor_copy(sc[:, 12:14], sc[:, 8:10]).then_inc(tok_ready, 2)
            transposed_lo(5)
            split_lo(U_MIXOUT + 3)
            split_lo(U_FFN2)
            residual(U_MIXOUT)
            square_sums()
            split_lo(U_FFN2 + 1)
            normalize(5)
            split_lo(U_FFN2 + 2)
            transposed_lo(6, ROW_FFN2)
            adds = ffn(U_FFN2, N_EXP + FFN_FULL + 1, 2, adds)
            dve.wait_ge(down_added, adds)
            dve.tensor_copy(sc[:, 12:14], sc[:, 8:10]).then_inc(out_ready, 2)

        @block.tensor
        def _(pe):
            pe.wait_ge(const_in, 32)
            pe.wait_ge(rows_in, 16 * 17)
            pe.transpose(ps[:, 7, 0:N_ROWS], rows[:, :], ident[0:N_ROWS, 0:N_ROWS]).then_inc(cols_T, 1)

            pe.wait_ge(tbl_in, 16)
            pe.wait_ge(onehot_in, 16)
            pe.wait_ge(ones_ready, 2)
            for n in range(2):
                i = pe.matmul(ps[0:HEADS, 5 + n, 0:REL_W], tbl[:, n * HEADS:(n + 1) * HEADS], onehot[0:33, n], start=True, stop=True)
            i.then_inc(bias_done, 1)

            def transpose_tok(t):
                pe.wait_ge(tok_ready, 2 * (t + 1))
                for b in range(4):
                    for k in (2 * b, 2 * b + 1):
                        for tt in range(TT):
                            c0 = (k % 2) * S + tt * P
                            ins = pe.transpose(ps[:, b, c0:c0 + P], tok[:, tt, k * P:(k + 1) * P], ident)
                    ins.then_inc(xT_ready, 1)

            def product(out, hi, lo, w_h, w_l, first, last):
                pe.matmul(out, hi, w_h, start=first, stop=False)
                pe.matmul(out, hi, w_l, start=False, stop=False)
                return pe.matmul(out, lo, w_h, start=False, stop=last)

            def unit(u, banks, k0, first, last, i=None, n_k=4, src=(h_hi, h_lo)):
                pe.wait_ge(lo_ready, u + 1 if i is None else STEP * i + (u + 1))
                width = UNIT // n_k
                for k in range(n_k):
                    for tt in range(TT):
                        c = slice(tt * P, (tt + 1) * P)
                        wc = slice(k * width, k * width + 512)
                        ins = product(ps[:, banks[tt], :], src[0][:, k0 + k, c], src[1][:, k0 + k, c],
                                      w_hi[:, u % SPLIT, wc], w_lo[:, u % SPLIT, wc],
                                      first and k == 0, last and k == n_k - 1)
                ins.then_inc(unit_used, 1)

            transpose_tok(0)
            pe.wait_ge(hT_lo, 4)
            for g in range(11):
                if g >= 4:
                    pe.wait_ge(proj_out, g - 3)
                banks = (2 * (g % 4), 2 * (g % 4) + 1)
                unit(2 * g, banks, 0, True, False)
                unit(2 * g + 1, banks, 4, False, True)

            pe.wait_ge(proj_out, 11)
            for n in range(4):
                for ct in range(4):
                    for tt in range(TT):
                        c0 = (ct % 2) * S + tt * P
                        i = pe.transpose(ps[:, 2 * n + ct // 2, c0:c0 + P], stage[:, n, tt, ct * P:(ct + 1) * P], ident)
                i.then_inc(stage_T, 1)

            def z_of(ct, par, bank, first, last):
                r = slice(par * DH, (par + 1) * DH)
                if first:
                    pe.matmul(ps[:, bank, 0:S], kT[r, ct, 0:P], qT[r, ct, :], start=True, stop=True)
                    return pe.matmul(ps[:, bank, S:S + P], kT[r, ct, P:S], qT[r, ct, P:S], start=True, stop=True)

            def logits(ct):
                if ct >= 2:
                    pe.wait_ge(sp_ready, ct - 1)
                for par in range(2):
                    i = z_of(ct, par, 2 * (ct % 2) + par, True, True)
                i.then_inc(z_ready, 1)

            def survive(ct):
                pe.wait_ge(spm_ready, ct + 1)
                if ct >= 1:
                    pe.wait_ge(a_ready, ct)
                for par in range(2):
                    r = slice(par * DH, (par + 1) * DH)
                    s_ = soft[:, ct % 2, par]
                    bank = ps[:, 4 + par, :]
                    pe.matmul(bank[:, 0:S], kT[r, ct, 0:P], qT[r, ct, :], start=True, stop=False, skip_group_check=True)
                    pe.matmul(bank[:, 0:S], neg_tri, s_[:, 0:S], start=False, stop=False, skip_group_check=True)
                    pe.matmul(bank[:, P:S], neg_ones, s_[:, S:S + P], start=False, stop=True, skip_group_check=True)
                    pe.matmul(bank[:, S:S + P], kT[r, ct, P:S], qT[r, ct, P:S], start=True, stop=False, skip_group_check=True)
                    i = pe.matmul(bank[:, S:S + P], neg_tri, s_[:, S:S + P], start=False, stop=True, skip_group_check=True)
                i.then_inc(s_ready, 1)

            def values(ct):
                pe.wait_ge(am_ready, ct + 1)
                for par in range(2):
                    r = slice(par * DH, (par + 1) * DH)
                    hc = slice((2 * ct + par) * DH, (2 * ct + par + 1) * DH)
                    o = ps[r, 6 + ct // 2, (ct % 2) * S:(ct % 2 + 1) * S]
                    w = att[:, ct % 2, par]
                    pe.matmul(o, v_sb[:, 0, hc], w[:, 0:S], start=True, stop=False, skip_group_check=True)
                    i = pe.matmul(o[:, P:S], v_sb[:, 1, hc], w[:, S:S + P], start=False, stop=True, skip_group_check=True)
                i.then_inc(y_ready, 1)

            pe.wait_ge(sbT_ready, 2)
            logits(0)
            logits(1)
            pe.wait_ge(hgT_ready, 5)
            for ct in range(4):
                survive(ct)
                if ct + 2 < 4:
                    logits(ct + 2)
                values(ct)

            def scores(n, k, q):
                pe.wait_ge(qdec_ready, n) if n else pe.wait_ge(zeroed, 5)
                if n >= 2:
                    pe.wait_ge(level_kept, 4 * (n - 1))
                for b in range(4):
                    par, tt = b // 2, b % 2
                    r = slice(par * DH, (par + 1) * DH)
                    for ct in range(4):
                        i = pe.matmul(ps[:, 4 * (n % 2) + b, ct * P:(ct + 1) * P], k[r, ct, tt * P:(tt + 1) * P],
                                      q[r, ct, tt * P:(tt + 1) * P], start=True, stop=True)
                    i.then_inc(level_done, 1)

            scores(0, hk, qhT)
            for level in range(LEVELS):
                scores(level + 1, k_dec[:, level % 2], q_dec[:, level % 2])
            pe.wait_ge(qdec_ready, LEVELS + 1)
            pe.wait_ge(level_kept, 4 * LEVELS)
            for par in range(2):
                r = slice(par * DH, (par + 1) * DH)
                for ct in range(4):
                    i = pe.matmul(ps[:, par, ct * P:(ct + 1) * P], k_dec[r, 1, ct, 0:P], q_dec[r, 1, ct, P:S], start=True, stop=True)
            i.then_inc(far_ready, 1)
            pe.wait_ge(level_kept, 4 * (LEVELS + 1) + 1)
            for tt in range(TT):
                for h in range(HEADS):
                    par, ct = h % 2, h // 2
                    o = ps[:, 2 + tt, h * DH:(h + 1) * DH]
                    i = pe.matmul(o, sc_near[:, (par * 2 + tt) * 4 + ct, :], v_hg[:, tt, h * DH:(h + 1) * DH], start=True, stop=(tt == 0))
                    if tt == 1:
                        i = pe.matmul(o, sc_far[:, par, ct, :], v_hg[:, 0, h * DH:(h + 1) * DH], start=False, stop=True)
            i.then_inc(o_ready, 1)
            pe.wait_ge(og_ready, 1)
            for ct in range(4):
                for tt in range(TT):
                    c0 = (ct % 2) * S + tt * P
                    i = pe.transpose(ps[:, 4 + ct // 2, c0:c0 + P], o_gated[:, tt, ct * P:(ct + 1) * P], ident)
            i.then_inc(oT_ready, 1)

            pe.wait_ge(yhg_lo, 1)
            pe.wait_ge(ysb_lo, 1)
            for half in range(2):
                unit(U_BRANCH + 2 * half, (4 * half, 4 * half + 1), 0, True, True)
                unit(U_BRANCH + 2 * half + 1, (4 * half + 2, 4 * half + 3), 4, True, True)
            transpose_tok(1)

            def square_product(u0):
                for half in range(2):
                    banks = (4 + 2 * half, 5 + 2 * half)
                    unit(u0 + 2 * half, banks, 0, True, False)
                    unit(u0 + 2 * half + 1, banks, 4, False, True)

            pe.wait_ge(hT_lo, 8)
            square_product(U_OUT)
            transpose_tok(2)
            pe.wait_ge(hT_lo, 12)

            pe.wait_ge(wr_split_lo, 1)
            pe.wait_ge(small_in, 64)
            pe.wait_ge(ones_ready, 1)
            for tt in range(TT):
                c = slice(tt * P, (tt + 1) * P)
                o = ps[:, 7, 32 * tt:32 * tt + 20]
                for k in range(KT):
                    product(o, h_hi[:, k, c], h_lo[:, k, c], wr_hi[:, k, 0:20], wr_lo[:, k, 0:20], k == 0, False)
                i = pe.matmul(o, one_row[:, :], rb_row[:, 0:20], start=False, stop=True)
            i.then_inc(route_T, 1)

            down = (aT_hi, aT_lo)

            def transpose_a(c, n_f=4):
                pe.wait_ge(a_done, c + 1)
                for tt in range(TT):
                    for f in range(n_f):
                        i = pe.transpose(ps[:, 2 + tt, f * P:(f + 1) * P], act_a[:, tt, f * P:(f + 1) * P], ident)
                    i.then_inc(aT_done, 1)

            def chunks(u0, c0, n, adds0):
                unit(u0, (0, 1), 0, True, False)
                unit(u0 + 1, (0, 1), 4, False, True)
                if c0:
                    pe.wait_ge(aT_lo_r, 2 * c0)
                unit(u0 + 2, (2, 3), 0, True, False)
                unit(u0 + 3, (2, 3), 4, False, True)
                transpose_a(c0)
                s0 = u0 + 4
                with pe.Fori(0, n - 1) as i:
                    c = i + (c0 + 1)
                    unit(s0, (0, 1), 0, True, False, i)
                    unit(s0 + 1, (0, 1), 4, False, True, i)
                    pe.wait_ge(aT_lo_r, 2 * i + 2 * (c0 + 1))
                    unit(s0 + 2, (2, 3), 0, True, False, i)
                    unit(s0 + 3, (2, 3), 4, False, True, i)
                    pe.wait_ge(down_added, 4 * i + (adds0 - 2))
                    unit(s0 + 4, (4, 5), 0, True, True, i, src=down)
                    pe.wait_ge(down_added, 4 * i + adds0)
                    unit(s0 + 5, (6, 7), 0, True, True, i, src=down)
                    transpose_a(c)
                return s0 + STEP * (n - 1)

            u = chunks(U_MOE, 0, N_EXP, 4)
            adds = 4 + 4 * (N_EXP - 1)

            def last_down(u, c, adds):
                pe.wait_ge(aT_lo_r, 2 * (c + 1))
                pe.wait_ge(down_added, adds - 2)
                unit(u, (4, 5), 0, True, True, src=down)
                pe.wait_ge(down_added, adds)
                unit(u + 1, (6, 7), 0, True, True, src=down)

            last_down(u, N_EXP - 1, adds)
            transpose_tok(3)
            pe.wait_ge(hT_lo, 16)

            def narrow(u, banks):
                pe.wait_ge(lo_ready, u + 1)
                for k in range(KT):
                    for tt in range(TT):
                        c = slice(tt * P, (tt + 1) * P)
                        wc = slice(k * 256, (k + 1) * 256)
                        i = product(ps[:, banks[tt], 0:256], h_hi[:, k, c], h_lo[:, k, c], w_hi[:, u % SPLIT, wc],
                                    w_lo[:, u % SPLIT, wc], k == 0, k == KT - 1)
                i.then_inc(unit_used, 1)

            def ffn(u0, c0, adds):
                u = chunks(u0, c0, FFN_FULL, adds)
                adds += 4 * (FFN_FULL - 1)
                c = c0 + FFN_FULL
                narrow(u, (0, 1))
                pe.wait_ge(aT_lo_r, 2 * c)
                narrow(u + 1, (2, 3))
                last_down(u + 2, c - 1, adds)
                transpose_a(c, 2)
                pe.wait_ge(lo_ready, u + 5)
                pe.wait_ge(aT_lo_r, 2 * (c + 1))
                for half in range(2):
                    pe.wait_ge(down_added, adds + 2 * half + 2)
                    for k in range(2):
                        for tt in range(TT):
                            t = slice(tt * P, (tt + 1) * P)
                            wc = slice(k * D + half * 512, k * D + half * 512 + 512)
                            i = product(ps[:, 4 + 2 * half + tt, :], aT_hi[:, k, t], aT_lo[:, k, t], w_hi[:, (u + 4) % SPLIT, wc],
                                        w_lo[:, (u + 4) % SPLIT, wc], k == 0, k == 1)
                i.then_inc(unit_used, 1)
                return adds + 8

            adds = ffn(U_FFN1, N_EXP, adds + 8)

            transpose_tok(4)
            pe.wait_ge(hT_lo, 20)
            for g in range(4):
                unit(U_MIX + 2 * g, (2 * g, 2 * g + 1), 0, True, False)
                unit(U_MIX + 2 * g + 1, (2 * g, 2 * g + 1), 4, False, True)
            pe.wait_ge(wr_split_lo, 2)
            pe.wait_ge(mix_out, 2)
            for tt in range(TT):
                c = slice(tt * P, (tt + 1) * P)
                for k in range(KT):
                    i = product(ps[:, 0, 32 * tt:32 * tt + GATE_COLS], h_hi[:, k, c], h_lo[:, k, c], wr_hi[:, k, :], wr_lo[:, k, :],
                                k == 0, k == KT - 1)
            i.then_inc(gates_T, 1)
            pe.wait_ge(mix_out, 8)
            for kv in range(2):
                for tt in range(TT):
                    i = pe.transpose(ps[:, 1, kv * S + tt * P:kv * S + (tt + 1) * P], proj[:, tt, OFF_KC + kv * P:OFF_KC + (kv + 1) * P], ident)
            i.then_inc(kv_T, 1)
            pe.wait_ge(cmp_in, 32)
            pe.wait_ge(kvT_ready, 5)
            for kv in range(2):
                for pp in range(PAIRS):
                    i = pe.matmul(ps[:, 2, 64 * kv:64 * kv + 3 * N_CMP], cmp_w1[:, kv, pp, :],
                                  kvT[:, kv, :, 2 * pp:2 * pp + CMP_STRIDE * (N_CMP - 1) + 1:CMP_STRIDE],
                                  start=(pp == 0), stop=(pp == PAIRS - 1))
            i.then_inc(pre_T, 1)
            for n, c0 in enumerate((0, OFF_QB)):
                pe.wait_ge(q_normed, n + 1)
                for ct in range(4):
                    for tt in range(TT):
                        o = (ct % 2) * S + tt * P
                        i = pe.transpose(ps[:, 4 + 2 * n + ct // 2, o:o + P], proj[:, tt, c0 + ct * P:c0 + (ct + 1) * P], ident)
                i.then_inc(qk_T, 1)
            pe.wait_ge(hid_ready, 1)
            for kv in range(2):
                for g in range(2):
                    o = ps[0:N_CMP, 3, kv * P + g * DH:kv * P + (g + 1) * DH]
                    pe.matmul(o, hidT[:, kv, g * N_CMP:(g + 1) * N_CMP], cmp_w2[:, kv, :], start=True, stop=False)
                    i = pe.matmul(o, one_row[:, 0:N_CMP], b2_row[:, kv, :], start=False, stop=True)
            i.then_inc(kvc_ready, 1)
            pe.wait_ge(gsig_ready, 1)
            for n in range(3):
                pe.wait_ge(k_normed, 2 * n + 2)
                if n == 2:
                    pe.wait_ge(qk_set, 1)
                for g in range(2):
                    for tt in range(TT):
                        i = pe.transpose(ps[:, (0, 1, 4)[n], g * S + tt * P:g * S + (tt + 1) * P], k_dup[:, tt, 2 * n + g, :], ident)
                i.then_inc(qk_T, 1)
            pe.wait_ge(kcn_ready, 4)
            for g in range(2):
                i = pe.transpose(ps[:, 5, 16 * g:16 * g + N_CMP], kc_n[0:N_CMP, g].rearrange("p a d -> p (a d)"), ident[0:N_CMP, 0:N_CMP])
            i.then_inc(kcT_T, 1)

            def logits_of(n):
                kind, h = n // HEADS, n % HEADS
                qi, k0, _, _ = KINDS[kind]
                ct, g = h // 2, h // (HEADS // 2)
                r = slice((h % 2) * DH, (h % 2 + 1) * DH)
                if n >= 4:
                    pe.wait_ge(neg_ready, n - 3)
                for qt in range(TT):
                    o = ps[:, n % 4, key_cols(kind, qt)]
                    w = o.shape[-1]
                    keys = kkT[r, k0 + g, 0:w] if kind < 3 else kcT[r, g, 0:w]
                    i = pe.matmul(o, qqT[r, qi, ct, qt * P:(qt + 1) * P], keys, start=True, stop=True)
                i.then_inc(lg_ready, 1)

            def transpose_p(n):
                kind = n // HEADS
                w = prob[:, n % 4]
                pe.wait_ge(p_ready, n + 1)
                if n >= 2:
                    pe.wait_ge(pT_set, n - 1)
                if kind < 3:
                    for b in range(3):
                        i = pe.transpose(ps[:, 4 + n % 2, b * P:(b + 1) * P], w[:, b * P:(b + 1) * P], ident)
                else:
                    for qt in range(TT):
                        cs = key_cols(3, qt)
                        i = pe.transpose(ps[0:cs.stop - cs.start, 4 + n % 2, qt * P:(qt + 1) * P], w[:, cs], ident)
                i.then_inc(pT_ready, 1)

            def weighted(n):
                kind, h = n // HEADS, n % HEADS
                g = h // (HEADS // 2)
                pe.wait_ge(pT_set, n + 1)
                if kind and h == 0:
                    pe.wait_ge(o_used, kind)
                cs = slice(h * DH, (h + 1) * DH)
                if kind < 3:
                    vc = slice(KINDS[kind][2] + g * DH, KINDS[kind][2] + (g + 1) * DH)
                    pe.matmul(ps[:, 6, cs], probT[:, n % 2, 0:P], proj[:, 0, vc], start=True, stop=True)
                    pe.matmul(ps[:, 7, cs], probT[:, n % 2, P:2 * P], proj[:, 0, vc], start=True, stop=False)
                    i = pe.matmul(ps[:, 7, cs], probT[:, n % 2, 2 * P:3 * P], proj[:, 1, vc], start=False, stop=True)
                else:
                    vc = slice(g * DH, (g + 1) * DH)
                    for qt in range(TT):
                        w = key_cols(3, qt)
                        w = w.stop - w.start
                        i = pe.matmul(ps[:, 6 + qt, cs], probT[0:w, n % 2, qt * P:(qt + 1) * P], v_c[0:w, vc], start=True, stop=True)
                i.then_inc(pv_done, 1)

            pe.wait_ge(qk_set, 5)
            pe.wait_ge(kcT_set, 2)
            for s in range(4 * HEADS + 3):
                if s < 4 * HEADS:
                    logits_of(s)
                if 2 <= s < 4 * HEADS + 2:
                    transpose_p(s - 2)
                if s >= 3:
                    weighted(s - 3)

            transpose_tok(5)
            pe.wait_ge(hT_lo, 24)
            square_product(U_MIXOUT)
            transpose_tok(6)
            pe.wait_ge(hT_lo, 28)
            ffn(U_FFN2, N_EXP + FFN_FULL + 1, adds + 4)

        @block.gpsimd
        def _(pool):

            pool.memset(one_row[:, :], 1.0).then_inc(ones_ready, 1)
            pool.memset(tbl[32:33, :], 1.0).then_inc(ones_ready, 1)

            def causal(buf):
                for block_cols in (slice(0, P), slice(2 * P, 3 * P)):
                    v = buf[:, :, block_cols]
                    i = pool.affine_select(out=v, in_=v, compare_op=ALU.is_gt, fill=0.0, base=0,
                                           pattern=[[0, 2], [1, P]], channel_multiplier=-1)
                return i

            def mask_soft(ct):
                pool.wait_ge(sp_ready, ct + 1)
                causal(soft[:, ct % 2]).then_inc(spm_ready, 1)

            mask_soft(0)
            mask_soft(1)
            for ct in range(4):
                pool.wait_ge(a_ready, ct + 1)
                causal(att[:, ct % 2]).then_inc(am_ready, 1)
                if ct + 2 < 4:
                    mask_soft(ct + 2)
            pool.wait_ge(y_ready, 4)
            pool.memset(sc_near, 0.0).then_inc(zeroed, 1)
            pool.memset(q_dec, 0.0).then_inc(zeroed, 1)
            pool.memset(k_dec, 0.0).then_inc(zeroed, 1)
            pool.memset(suf, 1.0).then_inc(zeroed, 1)
            pool.wait_ge(level_kept, 4 * (LEVELS + 1))
            pool.dma_start(final_g, a["final_g"].rearrange("(o d) -> o d", o=1).broadcast_to([P, D])).then_inc(fg_in, 16)

            pool.wait_ge(wr_split_lo, 1)
            pool.dma_start(wr_raw[:, :, 0:GATE_COLS], a["w_mix_in_2"][0][:, 2048:D_MIX].rearrange("(k p) n -> p k n", p=P)).then_inc(wr2_in, 16)
            pool.wait_ge(tok_ready, 4)
            pool.memset(kvT[:, :, 2, :], 0.0).then_inc(pos_set, 1)




_INS = ["x", "ln1_g", "w_in", "w_branch_sb", "w_branch_hg", "hg_norm_g", "hg_lb_logits", "w_out", "ln2_g",
        "w_router_group", "b_router_group", "w_router_expert", "b_router_expert", "w_exp_gate", "w_exp_up",
        "w_exp_down", "final_g", "rel_bias_table_2", "ffn1_norm_2", "ffn1_w_in_2", "ffn1_w_out_2", "mix_norm_2",
        "w_mix_in_2", "w_mix_out_2", "q_norm_a_2", "k_norm_a_2", "sinks_a_2", "q_norm_b_2", "k_norm_b_2",
        "cmp_pos_2", "cmp_w1_2", "cmp_b1_2", "cmp_w2_2", "cmp_b2_2", "ffn2_norm_2", "ffn2_w_in_2", "ffn2_w_out_2"]


def kernel(**inputs):
    import concourse.bacc as bacc
    from concourse.bass_utils import run_bass_kernel_spmd

    nc = bacc.Bacc("TRN2", target_bir_lowering=False, num_devices=1, dynamic_dma_scratch_size=2048)
    arrays, handles = {}, {}
    for name in _INS:
        arr = np.ascontiguousarray(inputs[name])
        arrays[f"in_{name}"] = arr
        handles[name] = nc.dram_tensor(f"in_{name}", arr.shape, F32, kind="ExternalInput").ap()
    out = nc.dram_tensor("out_x", (1, S, D), F32, kind="ExternalOutput").ap()
    two_blocks_kernel(nc, handles, out)
    result = run_bass_kernel_spmd(nc, [arrays], core_ids=[0])
    return result.results[0]["out_x"]
```

```python
from contextlib import ExitStack

import numpy as np

import concourse.bass as bass
from concourse import mybir

F32 = mybir.dt.float32
F32R = mybir.dt.float32r
I32 = mybir.dt.int32
ALU = mybir.AluOpType
ACT = mybir.ActivationFunctionType
AX = mybir.AxisListType.X

P = 128
D = 1024
S = 256
TT = S // P
KT = D // P
EPS = 1e-6
HEADS = 8
DH = 64
SBW = HEADS * DH
GROUPS, PER_GROUP = 4, 4
N_EXP = GROUPS * PER_GROUP
D_EXP = 512
D_FF = 2816
D_MIX = 2072
GATE_COLS = 3 * HEADS
NEG = -1e9
TINY = float(np.finfo(np.float32).tiny)
CMP_LEN, CMP_STRIDE = 32, 16
N_CMP = (S - CMP_LEN) // CMP_STRIDE + 1
PAIRS = CMP_LEN // 2
REL_W = 384

UNIT = 2048
RAW, SPLIT = 6, 3
STEP = 6
LEVELS = 7

U_IN, N_IN = 0, 22
U_BRANCH = U_IN + N_IN
U_OUT = U_BRANCH + 4
U_MOE = U_OUT + 4
U_FFN1 = U_MOE + N_EXP * STEP
FFN_FULL = D_FF // 512
FFN_UNITS = FFN_FULL * STEP + 3
U_MIX = U_FFN1 + FFN_UNITS
U_MIXOUT = U_MIX + 8
U_FFN2 = U_MIXOUT + 4
U_END = U_FFN2 + FFN_UNITS

OFF_KA, OFF_VA, OFF_QB, OFF_KC, OFF_KS, OFF_VS, OFF_KW, OFF_VW = 512, 640, 768, 1280, 1536, 1664, 1792, 1920
MIX_BLOCKS = 2048 // DH
FAR = 1e8

IN_COLS = dict(q_sb=0, k_sb=512, v_sb=1024, q_hg=1536, f_hg=2048, i_hg=2560, g_hg=3072,
               gate_sb0=3584, gate_sb1=4096, gate_hg0=4608, gate_hg1=5120)
IN_ORDER = ["q_sb", "k_sb", "v_sb", "i_hg", "q_hg", "g_hg", "f_hg", "gate_sb0", "gate_sb1", "gate_hg0", "gate_hg1"]

ROW_LN1, ROW_LN2, ROW_FFN1, ROW_MIX, ROW_FFN2 = 0, 8, 16, 24, 32
ROW_HGN, ROW_LB, ROW_QA, ROW_KA, ROW_QB, ROW_KB, ROW_B1 = 40, 44, 52, 53, 54, 55, 56
ROW_POS = 58
N_ROWS = 90


def shape_constants():
    k = np.arange(P)[:, None]
    q = np.arange(P)[None, :]
    ident = (k == q).astype(np.float32)
    neg_tri = -(k >= q).astype(np.float32)
    neg_ones = -np.ones((P, P), np.float32)
    dense = np.stack([ident, neg_tri, neg_ones], 1)
    slots = np.broadcast_to(np.arange(P, dtype=np.float32), (P, P)).copy()
    masks = []
    for level in range(LEVELS):
        h = 1 << level
        masks.append((k // (2 * h) == q // (2 * h)) & (k % (2 * h) < h) & (q % (2 * h) >= h))
    masks.append(k == q)
    masks = np.stack(masks, 1).astype(np.int32)
    rel = 255 - np.arange(REL_W)
    n = np.maximum(rel, 0)
    nf = np.maximum(n, 1).astype(np.float32)
    large = 16 + (np.log(nf / np.float32(16)) / np.float32(np.log(8.0)) * np.float32(16)).astype(np.int32)
    bucket = np.where(n < 16, n, np.minimum(large, 31))
    hot = (np.arange(32)[:, None] == bucket[None, :]).astype(np.float32)
    off_a = np.where((rel < 0) | (rel >= 128), np.float32(NEG), np.float32(0))[None, :]
    off_b = np.where(rel < 0, np.float32(NEG), np.float32(0))[None, :]
    bias = np.stack([np.concatenate([hot, off_a]), np.concatenate([hot, off_b])], 1).astype(np.float32)
    return dense, masks, bias, slots


def two_blocks_kernel(nc, a, out):
    dense_np, masks_np, bias_np, slots_np = shape_constants()
    dense_dram = nc.inline_tensor(dense_np, name="dense_const").ap()
    masks_dram = nc.inline_tensor(masks_np, name="masks_const").ap()
    slots_dram = nc.inline_tensor(slots_np, name="slots_const").ap()
    onehot_dram = nc.inline_tensor(bias_np, name="bucket_const").ap()
    bias_rows = nc.dram_tensor("bias_rows", (2, HEADS, P, REL_W), F32, kind="Internal")

    with ExitStack() as ctx:
        def sb(name, shape, dt=F32):
            return ctx.enter_context(nc.sbuf_tensor(name, shape, dt))

        x = sb("x_res", [P, TT, D])
        tok = sb("tok", [P, TT, D])
        h_hi = sb("h_hi", [P, KT, S], F32R)
        h_lo = sb("h_lo", [P, KT, S], F32R)
        w_raw = sb("w_raw", [P, RAW, UNIT])
        w_hi = sb("w_hi", [P, SPLIT, UNIT], F32R)
        w_lo = sb("w_lo", [P, SPLIT, UNIT], F32R)
        aT_hi = sb("aT_hi", [P, 4, S], F32R)
        aT_lo = sb("aT_lo", [P, 4, S], F32R)
        dense = sb("dense", [P, 3, P])
        masks = sb("masks", [P, LEVELS + 1, P], I32)
        rows = sb("rows", [N_ROWS, P])
        cols = sb("cols", [P, N_ROWS])
        final_g = masks[:, :, :].rearrange("p a b -> p (a b)").bitcast(F32)
        arena_at = -(-nc.sbuf_base // 32) * 32
        arena = sb("arena", [P, 16384])
        sc = sb("scalars", [P, 1024])
        wr_raw = sb("wr_raw", [P, KT, 24])
        wr_hi = sb("wr_hi", [P, KT, 24], F32R)
        wr_lo = sb("wr_lo", [P, KT, 24], F32R)
        small = sb("small", [P, 512])
        one_row = sb("one_row", [1, P])
        rb_row = sb("rb_row", [1, 24])
        few_i = sb("few_i", [P, 1], I32)
        tbl = sb("tbl", [33, 2 * HEADS])
        b2_row = sb("b2_row", [1, 2, DH])
        ps = ctx.enter_context(nc.psum_tensor("ps", [P, 8, 512], F32))

        ident, neg_tri, neg_ones = dense[:, 0, :], dense[:, 1, :], dense[:, 2, :]

        def region(off, *dims):
            n = int(np.prod(dims))
            v = arena[:, off:off + n]
            names = "abcd"[:len(dims)]
            if len(dims) == 1:
                return v
            return v.rearrange(f"p ({' '.join(names)}) -> p {' '.join(names)}",
                               **{names[i]: dims[i] for i in range(len(dims))})

        v_sb = region(0, TT, 512)
        v_hg = region(1024, TT, 512)
        g_act = region(2048, TT, 512)
        gates = region(3072, 4, TT, 512)
        stage = region(7168, 4, TT, 512)
        qT = region(11264, 4, S)
        kT = region(12288, 4, S)
        qhT = region(13312, 4, S)
        pre = region(14336, 4, S)
        soft = region(7168, 2, 2, 384)
        att = region(8704, 2, 2, 384)
        hk = region(11264, 4, S)
        suf = region(12288, 4, S)
        chunks_1k = arena[:, :].rearrange("p (c x) -> p c x", x=4 * S)
        q_dec = [chunks_1k[:, 7:9, :], chunks_1k[:, 0::15, :]]
        k_dec = region(9216, 2, 4, S)
        sc_far = region(15360, 4, 2, P)
        sc_near = tok[:, :, :].rearrange("p t (c e q) -> p t c e q", c=4, e=2)
        o_gated = region(7168, TT, 512)
        o_sq = region(9216, TT, 512)
        merged_part = [region(9216 + 1024 * half, TT, 512) for half in range(2)]
        act_s = region(0, TT, 512)
        act_a = region(1024, TT, 512)

        route_sb = arena[0:20, 0:S]
        def region_r(name, off, *dims):
            return nc.alloc_sbuf_tensor_at(name, [P, *dims], F32R, offset=arena_at + 4 * off).ap()

        pick = region_r("pick", 4096, TT, P)
        pick_f = pick.bitcast(F32)
        slot_no = region(4352, P)
        zero_r = region_r("zero_r", 4608, 512)
        y_hi = region_r("y_hi", 2048, D)
        y_lo = region_r("y_lo", 3072, D)
        pickT_now = region_r("pickT_now", 5120, S)
        h2_hi = region_r("h2_hi", 8192, TT, D)
        h2_lo = region_r("h2_lo", 10240, TT, D)
        pickT = region_r("pickT", 12288, N_EXP, S)
        proj = region(0, TT, 2048)
        cmp_w1 = region(4096, 2, PAIRS, P)
        qqT_even = region(4096, 2, 4, S)
        qqT_odd = [proj[:, :, c:c + 512].rearrange("p b (k s) -> p b k s", s=S) for c in (0, OFF_QB)]
        kkT = region(6144, 6, S)
        sq = region(8192, TT, 2048)
        bias_t = region(8192, 2, HEADS, S)
        k_dup = region(12288, TT, 6, P)
        prob = region(12288, 4, 384)
        kvT = region(13824, 2, 3, S)
        probT = region(13824, 2, 384)
        cmp_w2 = region(15360, 2, DH)
        hidT = region(15488, 2, 32)
        kc_sq = region(15552, P)
        kc_n = region(15680, 2, 2, DH)
        v_c = region(15936, P)
        kcT = region(16064, 2, 16)
        onehot = region(15360, 2, REL_W)
        bias_out = region(14336, 2, REL_W)
        gate_sig = sc[:, 256:304].rearrange("p (t c) -> p t c", t=TT)
        blk_ss, blk_r = sc[:, 320:384], sc[:, 384:448]
        sums, negm = sc[:, 448:512], sc[:, 512:576]
        sink, nsink = sc[:, 576:584], sc[:, 584:592]
        o_scale, sink_t = sc[:, 592:656], sc[:, 656:672]
        gain8, bias2 = sc[:, 756:760], sc[:, 674:676]
        half_rows = sc[:, 754:756]
        kc_ss, kc_r = sc[:, 676:678], sc[:, 678:680]
        o_part = region(14592, TT, 512)
        sel, few, cur, slot_w, slot_w_now = sc[:, 688:720], sc[:, 720:722], sc[:, 724:728], sc[:, 736:752], sc[:, 752:753]
        post = sc[:, 760:762]
        KINDS = [(0, 0, OFF_VA, 0), (1, 2, OFF_VS, 1), (1, 4, OFF_VW, 1), (1, None, None, 1)]

        def halves(v, h):
            return v.rearrange("p (n two h) -> p n two h", two=2, h=h)

        def sem(name):
            return ctx.enter_context(nc.semaphore(name))

        raw_in = [sem(f"raw_in{i}") for i in range(RAW)]
        hi_ready, lo_ready, unit_used = sem("hi_ready"), sem("lo_ready"), sem("unit_used")
        x_in, rows_in, const_in, small_in, tbl_in, wr_in = (sem(n) for n in
            ("x_in", "rows_in", "const_in", "small_in", "tbl_in", "wr_in"))
        ss_ready, rms_ready, tok_ready = sem("ss_ready"), sem("rms_ready"), sem("tok_ready")
        xT_ready, hT_hi, hT_lo = sem("xT_ready"), sem("hT_hi"), sem("hT_lo")
        cols_T, cols_ready = sem("cols_T"), sem("cols_ready")
        lb_diff, lb_exp, lb_ready = sem("lb_diff"), sem("lb_exp"), sem("lb_ready")
        proj_out = sem("proj_out")
        stage_T, sbT_ready, hgT_ready = sem("stage_T"), sem("sbT_ready"), sem("hgT_ready")
        z_ready, ln_ready, sp_ready, spm_ready = sem("z_ready"), sem("ln_ready"), sem("sp_ready"), sem("spm_ready")
        s_ready, a_ready, am_ready, y_ready = sem("s_ready"), sem("a_ready"), sem("am_ready"), sem("y_ready")
        ysb_hi, ysb_lo = sem("ysb_hi"), sem("ysb_lo")
        zeroed, hk_ready, qdec_ready, kdec_ready, pre_ready, suf_done = (sem(n) for n in
            ("zeroed", "hk_ready", "qdec_ready", "kdec_ready", "pre_ready", "suf_done"))
        x_ready, eps_set, post_ready = sem("x_ready"), sem("eps_set"), sem("post_ready")
        half_set, masks_in = sem("half_set"), sem("masks_in")
        route_done, route_out = sem("route_done"), sem("route_out")
        level_done, level_kept, far_ready = sem("level_done"), sem("level_kept"), sem("far_ready")
        o_ready, osq_ready, orms_in, orms_ready, og_ready, oT_ready, yhg_hi, yhg_lo = (sem(n) for n in
            ("o_ready", "osq_ready", "orms_in", "orms_ready", "og_ready", "oT_ready", "yhg_hi", "yhg_lo"))
        resid_ready = sem("resid_ready")
        act_seq, dve_seq, pool_seq = sem("act_seq"), sem("dve_seq"), sem("pool_seq")
        wr_split_hi, wr_split_lo, route_T, route_sub, route_exp, route_ready = (sem(n) for n in
            ("wr_split_hi", "wr_split_lo", "route_T", "route_sub", "route_exp", "route_ready"))
        gate_done, up_done, silu_done, a_done, aT_done, aT_hi_r, aT_lo_r, down_done, down_added = (sem(n) for n in
            ("gate_done", "up_done", "silu_done", "a_done", "aT_done", "aT_hi_r", "aT_lo_r", "down_done", "down_added"))
        stored = sem("stored")
        mix_out, gates_T, gsig_ready, blk_summed, blk_rms, q_normed, k_normed = (sem(n) for n in
            ("mix_out", "gates_T", "gsig_ready", "blk_summed", "blk_rms", "q_normed", "k_normed"))
        out_ready = sem("out_ready")
        bias_done, bias_sb, bias_stored, bias_in, onehot_in, cmp_in, wr2_in, pos_set = (sem(n) for n in
            ("bias_done", "bias_sb", "bias_stored", "bias_in", "onehot_in", "cmp_in", "wr2_in", "pos_set"))
        kv_T, kvT_ready, pre_T, bias2_set, hid_ready, kvc_ready, kcsq_ready, kcss_ready, kcr_ready, kcn_ready, kcT_T, kcT_set = (sem(n) for n in
            ("kv_T", "kvT_ready", "pre_T", "bias2_set", "hid_ready", "kvc_ready", "kcsq_ready", "kcss_ready", "kcr_ready",
             "kcn_ready", "kcT_T", "kcT_set"))
        qk_T, qk_set, lg_ready, neg_ready, p_ready, pT_ready, pT_set, pv_done, o_used, sink_ready, sinkexp = (sem(n) for n in
            ("qk_T", "qk_set", "lg_ready", "neg_ready", "p_ready", "pT_ready", "pT_set", "pv_done", "o_used", "sink_ready", "sinkexp"))
        ones_ready = sem("ones_ready")
        h2_hi_set, h2_lo_set, sel_ready, count_T, few_ready, slots_in, zero_set = (sem(n) for n in
            ("h2_hi_set", "h2_lo_set", "sel_ready", "count_T", "few_ready", "slots_in", "zero_set"))
        pick_ready, gathered, gath_hi, gath_lo, pick_T, pickT_set, pickT_moved, y_half_hi, y_used = (sem(n) for n in
            ("pick_ready", "gathered", "gath_hi", "gath_lo", "pick_T", "pickT_set", "pickT_moved", "y_half_hi", "y_used"))
        fg_in, coef_set = sem("fg_in"), sem("coef_set")

        def key_cols(kind, qt):
            if kind < 3:
                return slice(0, P) if qt == 0 else slice(P, P + S)
            return slice(0, (P - CMP_LEN) // CMP_STRIDE + 1) if qt == 0 else slice(16, 16 + N_CMP)

        class Chain:

            def __init__(self, eng, s):
                self.eng, self.s, self.n = eng, s, 0

            def __call__(self, ins):
                ins.then_inc(self.s, 1)
                self.n = self.n + 1
                self.eng.wait_ge(self.s, self.n)

            def mark(self, ins):
                ins.then_inc(self.s, 1)
                self.n = self.n + 1

            def settle(self):
                self.eng.wait_ge(self.s, self.n)

        w_in, w_out = a["w_in"][0], a["w_out"][0]

        def unit_src(w, r0, c0, width=512):
            n = UNIT // width
            return w[r0:r0 + n * P, c0:c0 + width].rearrange("(k p) n -> p k n", p=P)

        def slot(u):
            return u % RAW, u % SPLIT

        def moe_src(e, j):
            if j < 4:
                w = a["w_exp_gate"] if j < 2 else a["w_exp_up"]
                v = w[0].rearrange("e (k p) n -> e p k n", p=P)
                return v[e, :, 4 * (j % 2):4 * (j % 2) + 4, :] if isinstance(e, int) else \
                    v[bass.ds(e, 1), :, 4 * (j % 2):4 * (j % 2) + 4, :].rearrange("e p k n -> p (e k) n")
            v = a["w_exp_down"][0].rearrange("e (k p) n -> e p k n", p=P)
            c0 = 512 * (j - 4)
            return v[e, :, :, c0:c0 + 512] if isinstance(e, int) else \
                v[bass.ds(e, 1), :, :, c0:c0 + 512].rearrange("e p k n -> p (e k) n")

        def ffn_src(w1, w2, c, j):
            w1, w2 = w1[0], w2[0]
            if j < 4:
                c0 = (0 if j < 2 else D_FF) + 512 * c
                r0 = 512 * (j % 2)
                return w1[r0:r0 + 512, c0:c0 + 512].rearrange("(k p) n -> p k n", p=P) if isinstance(c, int) else \
                    w1[r0:r0 + 512, bass.ds(c0, 512)].rearrange("(k p) n -> p k n", p=P)
            c0 = 512 * (j - 4)
            return w2[512 * c:512 * c + 512, c0:c0 + 512].rearrange("(k p) n -> p k n", p=P) if isinstance(c, int) else \
                w2[bass.ds(512 * c, 512), c0:c0 + 512].rearrange("(k p) n -> p k n", p=P)

        block = ctx.enter_context(nc.Block())

        @block.sync
        def _(sp):
            sp.dma_start(x[:, :, :], a["x"][0].rearrange("(t p) d -> p t d", p=P)).then_inc(x_in, 16)

            def load(u, src, i=None, k=4):
                r = u % RAW
                if u >= RAW:
                    sp.wait_ge(lo_ready, u - RAW + 1 if i is None else STEP * i + (u - RAW + 1))
                dst = w_raw[:, r, :].rearrange("p (k n) -> p k n", k=k)
                sp.dma_start(dst, src).then_inc(raw_in[r], 16)

            u = U_IN
            for name in IN_ORDER:
                for kh in range(2):
                    if u == 2:
                        sp.wait_ge(rows_in, 16 * 13)
                    load(u, unit_src(w_in, 512 * kh, IN_COLS[name]))
                    u += 1
                    if u == RAW:
                        sp.dma_start(tbl[0:32, :], a["rel_bias_table_2"]).then_inc(tbl_in, 16)
                        sp.dma_start(onehot[0:33], onehot_dram).then_inc(onehot_in, 16)
                        sp.dma_start(wr_raw[:, :, 0:4], a["w_router_group"][0].rearrange("(k p) n -> p k n", p=P)).then_inc(wr_in, 16)
                        sp.dma_start(wr_raw[:, :, 4:20], a["w_router_expert"][0].rearrange("(k p) n -> p k n", p=P)).then_inc(wr_in, 16)
                        sp.dma_start(rb_row[:, 0:4], a["b_router_group"]).then_inc(small_in, 16)
                        sp.dma_start(rb_row[:, 4:20], a["b_router_expert"]).then_inc(small_in, 16)
                        sp.dma_start(b2_row[:, :, :], a["cmp_b2_2"]).then_inc(small_in, 16)
                        sp.dma_start(sink, a["sinks_a_2"].broadcast_to([P, HEADS])).then_inc(small_in, 16)
                        sp.dma_start(masks[:, :, :], masks_dram).then_inc(masks_in, 16)
                    if u == 12:
                        sp.wait_ge(bias_sb, 1)
                        for n in range(2):
                            sp.dma_start(bias_rows.ap()[n], bias_out[0:HEADS, n:n + 1, :].broadcast_to((HEADS, P, REL_W))
                                         ).then_inc(bias_stored, 16)
            for w in ("w_branch_sb", "w_branch_hg"):
                for half in range(2):
                    load(u, unit_src(a[w][0], 0, 512 * half))
                    u += 1
            for half in range(2):
                for kh in range(2):
                    load(u, unit_src(w_out, 512 * kh, 512 * half))
                    u += 1

            def chunks(u0, n, src):
                for j in range(4):
                    load(u0 + j, src(0, j))
                with sp.Fori(0, n - 1) as i:
                    for j in range(STEP):
                        load(u0 + 4 + j, src(i + 1, j) if j < 4 else src(i, j), i)

            chunks(U_MOE, N_EXP, moe_src)
            for j in (4, 5):
                load(U_MOE + 4 + STEP * (N_EXP - 1) + j - 4, moe_src(N_EXP - 1, j))

            def ffn(u0, w1, w2):
                src = lambda c, j: ffn_src(a[w1], a[w2], c, j)
                chunks(u0, FFN_FULL, src)
                u = u0 + 4 + STEP * (FFN_FULL - 1)
                w1_, w2_ = a[w1][0], a[w2][0]
                c0 = 512 * FFN_FULL
                load(u, w1_[:, c0:c0 + 256].rearrange("(k p) n -> p k n", p=P), k=KT)
                load(u + 1, w1_[:, D_FF + c0:D_FF + c0 + 256].rearrange("(k p) n -> p k n", p=P), k=KT)
                load(u + 2, src(FFN_FULL - 1, 4))
                load(u + 3, src(FFN_FULL - 1, 5))
                load(u + 4, w2_[c0:c0 + 256, :].rearrange("(k p) n -> p k n", p=P), k=2)

            ffn(U_FFN1, "ffn1_w_in_2", "ffn1_w_out_2")
            sp.wait_ge(ss_ready, 3)
            sp.dma_start(cmp_w1, a["cmp_w1_2"][0].rearrange("k (pp q) h -> q k pp h", q=P)).then_inc(cmp_in, 16)
            sp.dma_start(cmp_w2, a["cmp_w2_2"][0].rearrange("k q d -> q k d")).then_inc(cmp_in, 16)

            def mix_load(u):
                g, kh = (u - U_MIX) // 2, (u - U_MIX) % 2
                load(u, unit_src(a["w_mix_in_2"][0], 512 * kh, 512 * g))


            for j in range(8):
                mix_load(U_MIX + j)
            for half in range(2):
                for kh in range(2):
                    load(U_MIXOUT + 2 * half + kh, unit_src(a["w_mix_out_2"][0], 512 * kh, 512 * half))
            sp.wait_ge(blk_summed, 1)
            sp.wait_ge(bias_stored, 32)
            for n in range(2):
                sp.dma_start(bias_t[:, n], bass.AP(bias_rows, n * HEADS * P * REL_W + P - 1,
                                                   [[REL_W - 1, P], [P * REL_W, HEADS], [1, S]])).then_inc(bias_in, 16)
            ffn(U_FFN2, "ffn2_w_in_2", "ffn2_w_out_2")
            for tt in range(TT):
                sp.wait_ge(out_ready, tt + 1)
                sp.dma_start(out[0, tt * P:(tt + 1) * P, :], x[:, tt, :]).then_inc(stored, 16)
            sp.wait_ge(stored, 16 * TT)

        @block.scalar
        def _(act):
            chain = Chain(act, act_seq)
            act.dma_start(dense[:, :, :], dense_dram).then_inc(const_in, 16)
            per_row = [("ln1_g", ROW_LN1, 8), ("ln2_g", ROW_LN2, 8), ("ffn1_norm_2", ROW_FFN1, 8), ("mix_norm_2", ROW_MIX, 8),
                       ("ffn2_norm_2", ROW_FFN2, 8), ("hg_norm_g", ROW_HGN, 4), ("hg_lb_logits", ROW_LB, 8)]
            for name, r0, n in per_row:
                act.dma_start(rows[r0:r0 + n, :], a[name].rearrange("a (b p) -> (a b) p", p=P)).then_inc(rows_in, 16)
            for name, r in (("q_norm_a_2", ROW_QA), ("k_norm_a_2", ROW_KA), ("q_norm_b_2", ROW_QB), ("k_norm_b_2", ROW_KB)):
                act.dma_start(rows[r:r + 1, :].rearrange("o (c d) -> o c d", c=2),
                              a[name].unsqueeze(1).broadcast_to([1, 2, DH])).then_inc(rows_in, 16)
            act.dma_start(rows[ROW_B1:ROW_B1 + 2, :], a["cmp_b1_2"][0]).then_inc(rows_in, 16)
            act.dma_start(rows[ROW_POS:ROW_POS + 2 * PAIRS, :],
                          a["cmp_pos_2"][0].rearrange("k (pp two) d -> (k pp) (two d)", two=2)).then_inc(rows_in, 16)

            def split_hi(u, i=None):
                if u >= U_END:
                    return
                act.wait_ge(raw_in[u % RAW], 16 * (u // RAW + 1) if i is None else 16 * i + 16 * (u // RAW + 1))
                if u >= SPLIT:
                    act.wait_ge(unit_used, u - SPLIT + 1 if i is None else STEP * i + (u - SPLIT + 1))
                act.activation(w_hi[:, u % SPLIT, :], w_raw[:, u % RAW, :], ACT.Copy).then_inc(hi_ready, 1)

            def rms(m):
                act.wait_ge(eps_set, 1)
                chain(act.activation(small[:, 104:105], sc[:, 0:1], ACT.Sqrt))
                act.wait_ge(x_ready, m + 1)
                chain(act.activation(tok[:, 1, :], x[:, 1, :], ACT.Square, accum_out=sc[:, 3:4]))
                act.wait_ge(ss_ready, m + 1)
                act.activation(sc[:, 4:6], sc[:, 2:4], ACT.Sqrt, scale=1.0 / D, bias=sc[:, 0:1]).then_inc(rms_ready, 1)

            def transposed_hi(t, gain=None):
                for b in range(4):
                    act.wait_ge(xT_ready, 4 * t + b + 1)
                    for k in (2 * b, 2 * b + 1):
                        src = ps[:, b, (k % 2) * S:(k % 2 + 1) * S]
                        if gain is None:
                            ins = act.activation(h_hi[:, k, :], src, ACT.Copy)
                        else:
                            ins = act.activation(h_hi[:, k, :], src, ACT.Copy, scale=cols[:, gain + k:gain + k + 1])
                    ins.then_inc(hT_hi, 1)

            split_hi(0)
            act.wait_ge(cols_ready, 1)
            transposed_hi(0, ROW_LN1)
            split_hi(1)
            rms(0)
            act.wait_ge(lb_diff, 1)
            act.activation(small[:, 8:16], small[:, 0:8], ACT.Exp).then_inc(lb_exp, 1)

            def leave_proj(g):
                act.wait_ge(unit_used, U_IN + 2 * g + 2)
                act.wait_ge(post_ready, 1)
                dst, func = {"q_sb": (stage[:, 0], ACT.Copy), "k_sb": (stage[:, 1], ACT.Copy), "v_sb": (v_sb, ACT.Copy),
                             "i_hg": (v_hg, ACT.Copy), "q_hg": (stage[:, 2], ACT.Silu), "g_hg": (g_act, ACT.Silu),
                             "f_hg": (stage[:, 3], ACT.Sigmoid)}.get(IN_ORDER[g]) or (gates[:, g - 7], ACT.Sigmoid)
                for tt in range(TT):
                    ins = act.activation(dst[:, tt, :], ps[:, 2 * (g % 4) + tt, :], func, scale=post[:, tt:tt + 1])
                ins.then_inc(proj_out, 1)

            for g in range(11):
                if g < 10:
                    split_hi(2 * g + 2)
                    split_hi(2 * g + 3)
                leave_proj(g)

            def softplus_parts(ct):
                act.wait_ge(z_ready, ct + 1)
                if ct >= 2:
                    act.wait_ge(s_ready, ct - 1)
                zb = 2 * (ct % 2)
                chain(act.activation(soft[:, ct % 2], ps[:, zb:zb + 2, 0:384], ACT.Abs))
                chain(act.activation(soft[:, ct % 2], soft[:, ct % 2], ACT.Exp, scale=-1.0))
                act.activation(soft[:, ct % 2], soft[:, ct % 2], ACT.Ln, bias=1.0).then_inc(ln_ready, 1)

            def weights(ct):
                act.wait_ge(s_ready, ct + 1)
                if ct >= 2:
                    act.wait_ge(y_ready, ct - 1)
                act.activation(att[:, ct % 2], ps[:, 4:6, 0:384], ACT.Exp).then_inc(a_ready, 1)

            chain(act.activation(small[:, 100:101], sc[:, 0:1], ACT.Ln))
            act.wait_ge(sbT_ready, 2)
            act.wait_ge(hgT_ready, 5)
            softplus_parts(0)
            softplus_parts(1)
            split_hi(U_BRANCH)
            for ct in range(4):
                weights(ct)
                if ct + 2 < 4:
                    softplus_parts(ct + 2)
                if ct in (1, 2):
                    split_hi(U_BRANCH + ct)
            act.wait_ge(y_ready, 4)
            act.activation(h_hi[:, 0:4, :].rearrange("p (b k) s -> p b (k s)", b=2), ps[:, 6:8, :], ACT.Copy).then_inc(ysb_hi, 1)

            act.wait_ge(o_ready, 1)
            act.activation(o_sq, ps[:, 2:4, :], ACT.Square).then_inc(osq_ready, 1)
            act.wait_ge(orms_in, 1)
            act.activation(small[:, 64:80], small[:, 48:64], ACT.Sqrt, scale=1.0 / DH, bias=sc[:, 0:1]).then_inc(orms_ready, 1)
            act.wait_ge(oT_ready, 1)
            for ct in range(4):
                i = act.activation(h_hi[:, 4 + ct, :], ps[:, 4 + ct // 2, (ct % 2) * S:(ct % 2 + 1) * S], ACT.Copy,
                                   scale=cols[:, ROW_HGN + ct:ROW_HGN + ct + 1])
            i.then_inc(yhg_hi, 1)

            split_hi(U_BRANCH + 3)
            for j in range(3):
                split_hi(U_OUT + j)
            transposed_hi(1)
            split_hi(U_OUT + 3)
            split_hi(U_MOE)
            act.wait_ge(wr_in, 32)
            act.activation(wr_hi[:, :, 0:20], wr_raw[:, :, 0:20], ACT.Copy).then_inc(wr_split_hi, 1)
            split_hi(U_MOE + 1)
            rms(1)
            split_hi(U_MOE + 2)
            transposed_hi(2, ROW_LN2)
            act.activation(h2_hi, tok[:, :, :], ACT.Copy).then_inc(h2_hi_set, 1)

            def route_exps():
                act.wait_ge(route_sub, 1)
                chain(act.activation(sc[:, 80:88], sc[:, 80:88], ACT.Exp))
                act.wait_ge(route_sub, 2)
                act.activation(sc[:, 148:150], sc[:, 146:148], ACT.Exp).then_inc(route_exp, 2)

            def silu(c, u_gate, posts, width=512):
                act.wait_ge(unit_used, u_gate + 1)
                if not (isinstance(c, int) and c == 0):
                    act.wait_ge(a_done, c)
                act.wait_ge(post_ready, posts)
                for tt in range(TT):
                    ins = act.activation(act_s[:, tt, 0:width], ps[:, tt, 0:width], ACT.Silu, scale=post[:, tt:tt + 1])
                ins.then_inc(silu_done, 1)

            def aT_hi_out(c, n_f=4):
                for tt in range(TT):
                    act.wait_ge(aT_done, 2 * c + (tt + 1))
                    act.activation(aT_hi[:, 0:n_f, tt * P:(tt + 1) * P],
                                   ps[:, 2 + tt, 0:n_f * P].rearrange("p (f t) -> p f t", f=n_f), ACT.Copy).then_inc(aT_hi_r, 1)

            def chunks(u0, c0, n, posts):
                split_hi(u0 + 3)
                silu(c0, u0 + 1, posts)
                split_hi(u0 + 4)
                split_hi(u0 + 5)
                aT_hi_out(c0)
                split_hi(u0 + 6)
                s0 = u0 + 4
                with act.Fori(0, n - 1) as i:
                    split_hi(s0 + 3, i)
                    split_hi(s0 + 4, i)
                    silu(i + (c0 + 1), STEP * i + (s0 + 1), posts)
                    split_hi(s0 + 5, i)
                    split_hi(s0 + 6, i)
                    split_hi(s0 + 7, i)
                    aT_hi_out(i + (c0 + 1))
                    split_hi(s0 + 8, i)
                return s0 + STEP * (n - 1)

            def gather_hi(n, half):
                act.wait_ge(gathered, 2 * n + (half + 1))
                for k in range(4 * half, 4 * half + 4):
                    ins = act.activation(h_hi[:, k, 0:P], ps[:, 0, (k % 4) * P:(k % 4 + 1) * P], ACT.Copy,
                                         scale=cols[:, ROW_LN2 + k:ROW_LN2 + k + 1])
                ins.then_inc(gath_hi, 1)

            def silu_few(c, u_gate):
                act.wait_ge(unit_used, u_gate + 1)
                if not (isinstance(c, int) and c == 0):
                    act.wait_ge(a_done, c)
                act.activation(act_s[:, 0, :], ps[:, 0, :], ACT.Silu).then_inc(silu_done, 1)

            def aT_few(c, u_down=None):
                act.wait_ge(aT_done, 2 * c + 2)
                if u_down is not None:
                    act.wait_ge(unit_used, u_down + 1)
                act.activation(aT_hi[:, :, 0:P], ps[:, 1, :].rearrange("p (f t) -> p f t", f=4), ACT.Copy).then_inc(aT_hi_r, 2)

            def y_out(p, half, u_down):
                act.wait_ge(unit_used, u_down + 1)
                act.wait_ge(pickT_moved, p + 1)
                act.activation(y_hi[:, 512 * half:512 * half + 512], ps[:, 2 + half, :], ACT.Copy, scale=slot_w_now).then_inc(y_half_hi, 1)

            def few_experts():
                u = U_MOE
                gather_hi(0, 0)
                gather_hi(0, 1)
                split_hi(u + 3)
                silu_few(0, u + 1)
                split_hi(u + 4)
                split_hi(u + 5)
                gather_hi(1, 0)
                split_hi(u + 6)
                aT_few(0)
                gather_hi(1, 1)
                s0 = u + 4
                with act.Fori(0, N_EXP - 2) as i:
                    split_hi(s0 + 3, i)
                    split_hi(s0 + 4, i)
                    silu_few(i + 1, STEP * i + (s0 + 1))
                    split_hi(s0 + 5, i)
                    gather_hi(i + 2, 0)
                    split_hi(s0 + 6, i)
                    y_out(i, 0, STEP * i + (s0 + 4))
                    split_hi(s0 + 7, i)
                    y_out(i, 1, STEP * i + (s0 + 5))
                    gather_hi(i + 2, 1)
                    aT_few(i + 1, STEP * i + (s0 + 5))
                    split_hi(s0 + 8, i)
                s, p = s0 + STEP * (N_EXP - 2), N_EXP - 2
                split_hi(s + 3)
                split_hi(s + 4)
                silu_few(p + 1, s + 1)
                split_hi(s + 5)
                split_hi(s + 6)
                y_out(p, 0, s + 4)
                split_hi(s + 7)
                y_out(p, 1, s + 5)
                aT_few(p + 1, s + 5)
                split_hi(s + 8)
                y_out(p + 1, 0, s + 6)
                y_out(p + 1, 1, s + 7)

            route_exps()
            act.wait_ge(few_ready, 1)
            is_few = act.value_load(few_i[0:1, 0:1], min_val=0, max_val=1)
            with act.If(is_few > 0):
                few_experts()
            with act.Else():
                chunks(U_MOE, 0, N_EXP, 2)
            split_hi(U_FFN1 + 1)
            rms(2)
            split_hi(U_FFN1 + 2)
            transposed_hi(3, ROW_FFN1)
            rms(3)

            def ffn(u0, c0, posts):
                u = chunks(u0, c0, FFN_FULL, posts)
                split_hi(u + 3)
                silu(c0 + FFN_FULL, u, posts, 256)
                split_hi(u + 4)
                split_hi(u + 5)
                split_hi(u + 6)
                aT_hi_out(c0 + FFN_FULL, 2)
                split_hi(u + 7)

            ffn(U_FFN1, N_EXP, 3)

            act.wait_ge(wr2_in, 16)
            act.wait_ge(route_T, 1)
            act.activation(wr_hi[:, :, :], wr_raw[:, :, :], ACT.Copy).then_inc(wr_split_hi, 1)
            transposed_hi(4, ROW_MIX)
            rms(4)
            act.wait_ge(post_ready, 4)
            for g in range(4):
                split_hi(U_MIX + 2 * g + 3)
                split_hi(U_MIX + 2 * g + 4)
                act.wait_ge(unit_used, U_MIX + 2 * g + 2)
                cs = slice(512 * g, 512 * g + 512)
                for dst, func in ((proj, ACT.Copy), (sq, ACT.Square)):
                    for tt in range(TT):
                        ins = act.activation(dst[:, tt, cs], ps[:, 2 * g + tt, :], func, scale=post[:, tt:tt + 1])
                    ins.then_inc(mix_out, 1)
            act.wait_ge(gates_T, 1)
            for tt in range(TT):
                ins = act.activation(gate_sig[:, tt, :], ps[:, 0, 32 * tt:32 * tt + GATE_COLS], ACT.Sigmoid, scale=post[:, tt:tt + 1])
            ins.then_inc(gsig_ready, 1)
            act.wait_ge(blk_summed, 1)
            act.activation(blk_r, blk_ss, ACT.Sqrt, scale=1.0 / DH, bias=sc[:, 0:1]).then_inc(blk_rms, 1)
            act.wait_ge(bias2_set, 1)
            for kv in range(2):
                i = act.activation(hidT[:, kv, 0:30], ps[:, 2, 64 * kv:64 * kv + 30], ACT.Silu, bias=bias2[:, kv:kv + 1])
            i.then_inc(hid_ready, 1)
            act.wait_ge(kvc_ready, 1)
            act.activation(kc_sq[0:N_CMP], ps[0:N_CMP, 3, 0:P], ACT.Square).then_inc(kcsq_ready, 1)
            act.wait_ge(kcss_ready, 1)
            act.activation(kc_r[0:N_CMP], kc_ss[0:N_CMP], ACT.Sqrt, scale=1.0 / DH, bias=sc[0:N_CMP, 0:1]).then_inc(kcr_ready, 1)

            def exps(n):
                kind, h = n // HEADS, n % HEADS
                w = prob[:, n % 4]
                act.wait_ge(neg_ready, n + 1)
                for qt in range(TT):
                    cs = key_cols(kind, qt)
                    k = 16 * kind + 8 * qt + h
                    i = act.activation(w[:, cs], w[:, cs], ACT.Exp, scale=-1.0, bias=negm[:, k:k + 1], accum_out=sums[:, k:k + 1])
                i.then_inc(p_ready, 1)

            for n in range(4 * HEADS):
                exps(n)
                if n == HEADS + 1:
                    act.wait_ge(sink_ready, 1)
                    act.activation(sink_t, sink_t, ACT.Exp).then_inc(sinkexp, 1)

            transposed_hi(5)
            split_hi(U_MIXOUT + 3)
            split_hi(U_FFN2)
            split_hi(U_FFN2 + 1)
            transposed_hi(6, ROW_FFN2)
            split_hi(U_FFN2 + 2)
            rms(5)
            ffn(U_FFN2, N_EXP + FFN_FULL + 1, 5)

        @block.vector
        def _(dve):
            chain = Chain(dve, dve_seq)
            dve.memset(sc[:, 0:2], EPS).then_inc(eps_set, 1)
            dve.wait_ge(eps_set, 1)

            def split_lo(u, i=None):
                if u >= U_END:
                    return
                dve.wait_ge(hi_ready, u + 1 if i is None else STEP * i + (u + 1))
                dve.tensor_tensor(w_lo[:, u % SPLIT, :], w_raw[:, u % RAW, :], w_hi[:, u % SPLIT, :],
                                  ALU.subtract).then_inc(lo_ready, 1)

            def square_sums():
                dve.tensor_copy(sc[:, 12:14], sc[:, 0:2]).then_inc(x_ready, 1)
                dve.tensor_tensor_reduce(out=tok[:, 0, :], in0=x[:, 0, :], in1=x[:, 0, :], scale=1.0, scalar=0.0,
                                         op0=ALU.mult, op1=ALU.add, accum_out=sc[:, 2:3]).then_inc(ss_ready, 1)

            def normalize(m):
                dve.wait_ge(rms_ready, m + 1)
                chain(dve.reciprocal(sc[:, 6:8], sc[:, 4:6]))
                for t in range(TT):
                    dve.tensor_scalar(tok[:, t, :], x[:, t, :], sc[:, 6 + t:7 + t], None, ALU.mult).then_inc(tok_ready, 1)

            def transposed_lo(t, gain=None):
                for b in range(4):
                    dve.wait_ge(hT_hi, 4 * t + b + 1)
                    for k in (2 * b, 2 * b + 1):
                        src = ps[:, b, (k % 2) * S:(k % 2 + 1) * S]
                        if gain is None:
                            ins = dve.tensor_tensor(h_lo[:, k, :], src, h_hi[:, k, :], ALU.subtract)
                        else:
                            ins = dve.scalar_tensor_tensor(out=h_lo[:, k, :], in0=src, scalar=cols[:, gain + k:gain + k + 1],
                                                           in1=h_hi[:, k, :], op0=ALU.mult, op1=ALU.subtract)
                    ins.then_inc(hT_lo, 1)

            def x_final():
                dve.tensor_copy(sc[:, 18:20], sc[:, 0:2]).then_inc(tok_ready, 2)

            def post_rms(m):
                square_sums()
                dve.wait_ge(rms_ready, m + 1)
                dve.reciprocal(post, sc[:, 4:6]).then_inc(post_ready, 1)

            dve.wait_ge(x_in, 16)
            x_final()
            dve.wait_ge(cols_T, 1)
            dve.tensor_copy(cols[:, 0:N_ROWS], ps[:, 7, 0:N_ROWS]).then_inc(cols_ready, 1)
            split_lo(0)
            transposed_lo(0, ROW_LN1)
            split_lo(1)
            post_rms(0)
            dve.wait_ge(const_in, 16)
            for par in range(2):
                dve.tensor_reduce(half_rows[:, par:par + 1], ident[:, par * DH:(par + 1) * DH], AX, ALU.add).then_inc(half_set, 1)
            dve.wait_ge(cols_ready, 1)
            l0, l1 = cols[:, ROW_LB:ROW_LB + 4], cols[:, ROW_LB + 4:ROW_LB + 8]
            chain(dve.tensor_tensor(small[:, 16:20], l0, l1, ALU.max))
            dve.tensor_tensor(small[:, 0:4], l0, small[:, 16:20], ALU.subtract)
            dve.tensor_tensor(small[:, 4:8], l1, small[:, 16:20], ALU.subtract).then_inc(lb_diff, 1)
            dve.wait_ge(lb_exp, 1)
            chain(dve.tensor_tensor(small[:, 20:24], small[:, 8:12], small[:, 12:16], ALU.add))
            chain(dve.reciprocal(small[:, 24:28], small[:, 20:24]))
            chain(dve.tensor_tensor(small[:, 28:32], small[:, 8:12], small[:, 24:28], ALU.mult))
            dve.tensor_scalar(small[:, 32:36], small[:, 28:32], -1.0, 1.0, ALU.mult, ALU.add).then_inc(lb_ready, 1)

            for g in range(10):
                if g == 2:
                    dve.wait_ge(bias_done, 1)
                    dve.tensor_copy(bias_out[0:HEADS], ps[0:HEADS, 6:8, 0:REL_W]).then_inc(bias_sb, 1)
                split_lo(2 * g + 2)
                split_lo(2 * g + 3)

            dve.wait_ge(stage_T, 1)
            dve.tensor_scalar(qT.rearrange("p (b k) s -> p b (k s)", b=2), ps[:, 0:2, :], DH ** -0.5, None, ALU.mult).then_inc(sbT_ready, 1)
            dve.wait_ge(stage_T, 2)
            dve.tensor_copy(kT.rearrange("p (b k) s -> p b (k s)", b=2), ps[:, 2:4, :]).then_inc(sbT_ready, 1)
            dve.wait_ge(stage_T, 3)
            dve.tensor_copy(qhT.rearrange("p (b k) s -> p b (k s)", b=2), ps[:, 4:6, :]).then_inc(hgT_ready, 1)
            dve.wait_ge(stage_T, 4)
            dve.wait_ge(bias_stored, 32)
            for ct in range(4):
                dve.tensor_scalar(pre[:, ct, :], ps[:, 6 + ct // 2, (ct % 2) * S:(ct % 2 + 1) * S], small[:, 32 + ct:33 + ct],
                                  small[:, 28 + ct:29 + ct], ALU.mult, ALU.add).then_inc(hgT_ready, 1)

            def softplus(ct):
                dve.wait_ge(ln_ready, ct + 1)
                zb = 2 * (ct % 2)
                dve.scalar_tensor_tensor(out=soft[:, ct % 2], in0=ps[:, zb:zb + 2, 0:384], scalar=0.0, in1=soft[:, ct % 2],
                                         op0=ALU.max, op1=ALU.add).then_inc(sp_ready, 1)

            for ct in range(4):
                softplus(ct)
                if ct:
                    split_lo(U_BRANCH + ct - 1)
            dve.wait_ge(s_ready, 4)
            dve.tensor_scalar(hk, pre, -1.0, 1.0, ALU.mult, ALU.add).then_inc(hk_ready, 1)
            dve.wait_ge(ysb_hi, 1)
            dve.tensor_tensor(h_lo[:, 0:4, :].rearrange("p (b k) s -> p b (k s)", b=2), ps[:, 6:8, :],
                              h_hi[:, 0:4, :].rearrange("p (b k) s -> p b (k s)", b=2), ALU.subtract).then_inc(ysb_lo, 1)

            qh_f, pre_f = qhT.rearrange("p c s -> p (c s)"), pre.rearrange("p c s -> p (c s)")
            dve.wait_ge(masks_in, 16)
            dve.wait_ge(zeroed, 1)

            def counted(n):
                return 4 + 2 * n

            def keep_diagonal():
                for b in range(4):
                    par, tt = b // 2, b % 2
                    dve.wait_ge(level_done, b + 1)
                    dve.copy_predicated(sc_near[:, tt, :, par, :], masks[:, LEVELS:LEVELS + 1, :].broadcast_to([P, 4, P]),
                                        ps[:, b, :].rearrange("p (c t) -> p c t", c=4)).then_inc(level_kept, 1)

            def keep(n):
                h = 1 << (n - 1)
                dve.wait_ge(level_kept, counted(n - 1))
                for tt in range(TT):
                    dve.wait_ge(level_done, counted(n - 1) + tt + 1)
                    dst = tok[:, tt, :].rearrange("p (c n two h) -> p c n two h", c=8, two=2, h=h)[:, :, :, 1, :]
                    m = masks[:, n - 1:n, :].broadcast_to([P, 8, P]).rearrange("p c (n two h) -> p c n two h", two=2, h=h)[:, :, :, 1, :]
                    dve.copy_predicated(dst, m, ps[:, 4 * (n % 2) + tt, :].rearrange("p (c n h) -> p c n h", c=8, h=h)).then_inc(level_kept, 1)

            for level in range(LEVELS):
                h, b = 1 << level, level % 2
                if level >= 2:
                    dve.wait_ge(level_done, counted(level - 1))
                for par in range(2):
                    i = dve.scalar_tensor_tensor(out=halves(q_dec[b][:, par, :], h)[:, :, 1, :], in0=halves(qh_f, h)[:, :, 1, :],
                                                 scalar=half_rows[:, par:par + 1], in1=halves(pre_f, h)[:, :, 1, :],
                                                 op0=ALU.mult, op1=ALU.mult)
                i.then_inc(qdec_ready, 1)
                if level:
                    keep(level)
                else:
                    keep_diagonal()
                n = 4 * S // (2 * h)
                dve.wait_ge(suf_done, level + 2)
                dve.tensor_tensor(halves(pre_f, h)[:, :, 1, :], halves(pre_f, h)[:, :, 1, :],
                                  halves(pre_f, h)[:, :, 0, h - 1:h].broadcast_to([P, n, h]), ALU.mult).then_inc(pre_ready, 1)
                dve.wait_ge(pre_ready, level + 1)
            dve.wait_ge(level_done, counted(LEVELS - 1))
            for par in range(2):
                i = dve.scalar_tensor_tensor(out=q_dec[1][:, par, :].rearrange("p (c s) -> p c s", s=S)[:, :, P:S], in0=qhT[:, :, P:S],
                                             scalar=half_rows[:, par:par + 1], in1=pre[:, :, P:S], op0=ALU.mult, op1=ALU.mult)
            i.then_inc(qdec_ready, 1)
            keep(LEVELS)
            dve.wait_ge(far_ready, 1)
            dve.tensor_copy(sc_far.rearrange("p (b c) e t -> p b (c e t)", b=2), ps[:, 0:2, :]).then_inc(level_kept, 1)
            dve.wait_ge(osq_ready, 1)
            dve.tensor_reduce(small[:, 48:64], o_sq.rearrange("p t (h d) -> p (t h) d", d=DH), AX, ALU.add).then_inc(orms_in, 1)
            chain(dve.tensor_tensor(o_gated, ps[:, 2:4, :], g_act, ALU.mult))
            dve.wait_ge(orms_ready, 1)
            chain(dve.reciprocal(small[:, 80:96], small[:, 64:80]))
            og = o_gated.rearrange("p t (h d) -> p (t h) d", d=DH)
            dve.tensor_tensor(og, og, small[:, 80:96].unsqueeze(2).broadcast_to([P, TT * HEADS, DH]), ALU.mult).then_inc(og_ready, 1)
            dve.wait_ge(yhg_hi, 1)
            for ct in range(4):
                i = dve.scalar_tensor_tensor(out=h_lo[:, 4 + ct, :], in0=ps[:, 4 + ct // 2, (ct % 2) * S:(ct % 2 + 1) * S],
                                             scalar=cols[:, ROW_HGN + ct:ROW_HGN + ct + 1], in1=h_hi[:, 4 + ct, :],
                                             op0=ALU.mult, op1=ALU.subtract)
            i.then_inc(yhg_lo, 1)

            split_lo(U_BRANCH + 3)
            for half in range(2):
                cs = slice(512 * half, 512 * half + 512)
                dve.wait_ge(unit_used, U_BRANCH + half + 1)
                chain(dve.tensor_tensor(tok[:, :, cs], ps[:, 6 * half:6 * half + 2, :], gates[:, half], ALU.mult))
            for half in range(2):
                cs = slice(512 * half, 512 * half + 512)
                part = merged_part[half]
                dve.wait_ge(unit_used, U_BRANCH + half + 3)
                chain(dve.tensor_tensor(part, ps[:, 2 + 2 * half:4 + 2 * half, :], gates[:, 2 + half], ALU.mult))
                dve.tensor_tensor(tok[:, :, cs], tok[:, :, cs], part, ALU.add).then_inc(tok_ready, 1)
                split_lo(U_OUT + half)
            split_lo(U_OUT + 2)
            transposed_lo(1)
            split_lo(U_OUT + 3)
            split_lo(U_MOE)
            dve.wait_ge(wr_split_hi, 1)
            dve.tensor_tensor(wr_lo[:, :, 0:20], wr_raw[:, :, 0:20], wr_hi[:, :, 0:20], ALU.subtract).then_inc(wr_split_lo, 1)

            def residual(u0, scale=None):
                for half in range(2):
                    cs = slice(512 * half, 512 * half + 512)
                    dve.wait_ge(unit_used, u0 + 2 * half + 2)
                    chain(dve.tensor_tensor(x[:, :, cs], ps[:, 4 + 2 * half:6 + 2 * half, :], x[:, :, cs], ALU.add))

            residual(U_OUT)
            square_sums()
            normalize(1)
            transposed_lo(2, ROW_LN2)
            split_lo(U_MOE + 1)
            dve.tensor_scalar(zero_r, tok[:, 0, 0:512], 0.0, None, ALU.mult).then_inc(zero_set, 1)
            dve.wait_ge(h2_hi_set, 1)
            dve.tensor_tensor(h2_lo, tok[:, :, :], h2_hi, ALU.subtract).then_inc(h2_lo_set, 1)

            def first_best(dst, src, tmp, best):
                b3 = best.unsqueeze(2).broadcast_to([P, TT, 4])
                chain(dve.tensor_tensor(tmp, src, b3, ALU.is_ge))
                chain(dve.tensor_tensor(tmp, tmp, descend, ALU.mult))
                chain(dve.tensor_reduce(sc[:, 16:18], tmp, AX, ALU.max))
                chain(dve.tensor_tensor(dst, tmp, sc[:, 16:18].unsqueeze(2).broadcast_to([P, TT, 4]), ALU.is_equal))

            def v3(o, n, w):
                return sc[:, o:o + n * w].rearrange("p (a b) -> p a b", a=n)

            def wide(v):
                return v.unsqueeze(2).broadcast_to([P, TT, 4])

            descend = v3(20, TT, 4)
            for tt in range(TT):
                for j in range(4):
                    chain(dve.memset(sc[:, 20 + 4 * tt + j:21 + 4 * tt + j], float(4 - j)))
            lg = v3(32, TT, 20)
            e3, oh_g, tmp4, ig, oh1, oh2, inner = (v3(o, TT, 4) for o in (80, 88, 96, 104, 112, 120, 128))
            prod = sc[:, 160:192]
            comb = sc[:, 192:224].rearrange("p (t e) -> p t e", t=TT)
            gmax, gsum, w_grp, m1, m2, dm, e2, w1, w2 = (sc[:, o:o + 2] for o in range(136, 154, 2))

            def route():
                dve.wait_ge(route_done, 1)
                dve.tensor_copy(route_sb, ps[0:20, 7, 0:S]).then_inc(route_out, 1)
                dve.wait_ge(route_T, 1)
                chain(dve.tensor_copy(lg, ps[:, 7, S:S + 64].rearrange("p (t c) -> p t c", t=TT)[:, :, 0:20]))
                chain(dve.tensor_reduce(gmax, lg[:, :, 0:4], AX, ALU.max))
                dve.tensor_tensor(e3, lg[:, :, 0:4], wide(gmax), ALU.subtract).then_inc(route_sub, 1)
                first_best(oh_g, lg[:, :, 0:4], tmp4, gmax)
                for tt in range(TT):
                    pv = prod[:, 16 * tt:16 * tt + 16].rearrange("p (g j) -> p g j", g=4)
                    chain(dve.tensor_tensor(pv, lg[:, tt, 4:20].rearrange("p (g j) -> p g j", g=4),
                                            oh_g[:, tt, :].unsqueeze(2).broadcast_to([P, 4, 4]), ALU.mult))
                chain(dve.tensor_reduce(ig, prod.rearrange("p (t g j) -> p t j g", t=TT, g=4), AX, ALU.add))
                chain(dve.tensor_reduce(m1, ig, AX, ALU.max))
                first_best(oh1, ig, tmp4, m1)
                chain(dve.scalar_tensor_tensor(out=tmp4, in0=oh1, scalar=-3e38, in1=ig, op0=ALU.mult, op1=ALU.add))
                chain(dve.tensor_reduce(m2, tmp4, AX, ALU.max))
                chain(dve.tensor_copy(ig, tmp4))
                first_best(oh2, ig, tmp4, m2)
                dve.tensor_tensor(dm, m2, m1, ALU.subtract).then_inc(route_sub, 1)
                dve.wait_ge(route_exp, 2)
                chain(dve.tensor_reduce(gsum, e3, AX, ALU.add))
                chain(dve.reciprocal(w_grp, gsum))
                chain(dve.tensor_scalar(w1, e2, 1.0, None, ALU.add))
                chain(dve.reciprocal(w1, w1))
                chain(dve.tensor_tensor(w2, e2, w1, ALU.mult))
                chain(dve.tensor_tensor(w1, w1, w_grp, ALU.mult))
                chain(dve.tensor_tensor(w2, w2, w_grp, ALU.mult))
                chain(dve.tensor_tensor(oh1, oh1, wide(w1), ALU.mult))
                chain(dve.tensor_tensor(oh2, oh2, wide(w2), ALU.mult))
                chain(dve.tensor_tensor(inner, oh1, oh2, ALU.add))
                for tt in range(TT):
                    chain(dve.tensor_tensor(comb[:, tt, :].rearrange("p (g j) -> p g j", g=4),
                                            oh_g[:, tt, :].unsqueeze(2).broadcast_to([P, 4, 4]),
                                            inner[:, tt, :].unsqueeze(1).broadcast_to([P, 4, 4]), ALU.mult))

            coef = sc[:, 8:10]

            def gated(c, u_up, width=512):
                dve.wait_ge(silu_done, c + 1)
                dve.wait_ge(unit_used, u_up + 1)
                if not (isinstance(c, int) and c == 0):
                    dve.wait_ge(aT_done, 2 * c)
                for tt in range(TT):
                    ins = dve.scalar_tensor_tensor(out=act_a[:, tt, 0:width], in0=ps[:, 2 + tt, 0:width], scalar=post[:, tt:tt + 1],
                                                   in1=act_s[:, tt, 0:width], op0=ALU.mult, op1=ALU.mult)
                ins.then_inc(a_done, 1)

            def aT_lo_out(c, n_f=4):
                for tt in range(TT):
                    dve.wait_ge(aT_hi_r, 2 * c + (tt + 1))
                    dve.tensor_tensor(aT_lo[:, 0:n_f, tt * P:(tt + 1) * P],
                                      ps[:, 2 + tt, 0:n_f * P].rearrange("p (f t) -> p f t", f=n_f),
                                      aT_hi[:, 0:n_f, tt * P:(tt + 1) * P], ALU.subtract).then_inc(aT_lo_r, 1)

            def add_down(half, before, u_down):
                cs = slice(512 * half, 512 * half + 512)
                dve.wait_ge(unit_used, u_down + 1)
                dve.wait_ge(down_added, before)
                for tt in range(TT):
                    dve.scalar_tensor_tensor(out=x[:, tt, cs], in0=ps[:, 4 + 2 * half + tt, :], scalar=coef[:, tt:tt + 1],
                                             in1=x[:, tt, cs], op0=ALU.mult, op1=ALU.add).then_inc(down_added, 1)

            def chunks(u0, c0, n, adds0, each=None):
                split_lo(u0 + 3)
                split_lo(u0 + 4)
                gated(c0, u0 + 3)
                split_lo(u0 + 5)
                aT_lo_out(c0)
                split_lo(u0 + 6)
                s0 = u0 + 4
                with dve.Fori(0, n - 1) as i:
                    split_lo(s0 + 3, i)
                    split_lo(s0 + 4, i)
                    split_lo(s0 + 5, i)
                    gated(i + (c0 + 1), STEP * i + (s0 + 3))
                    split_lo(s0 + 6, i)
                    add_down(0, 4 * i + adds0, STEP * i + (s0 + 4))
                    split_lo(s0 + 7, i)
                    aT_lo_out(i + (c0 + 1))
                    split_lo(s0 + 8, i)
                    add_down(1, 4 * i + adds0, STEP * i + (s0 + 5))
                    if each is not None:
                        each(i)
                return s0 + STEP * (n - 1)

            def next_coef(i):
                dve.wait_ge(down_added, 4 * i + 8)
                dve.tensor_copy(coef.unsqueeze(2), comb[:, :, bass.ds(i + 1, 1)]).then_inc(coef_set, 1)
                dve.wait_ge(coef_set, i + 2)

            def first_coef():
                dve.tensor_copy(coef.unsqueeze(2), comb[:, :, 0:1]).then_inc(coef_set, 1)
                dve.wait_ge(coef_set, 1)
                dve.tensor_copy(sc[:, 10:12], coef).then_inc(down_added, 4)

            key = sc[:, 224:256]
            comb_key = sc[:, 192:256].rearrange("p (a e) -> p a e", e=N_EXP)

            def count():
                chain(dve.tensor_scalar(sel, sc[:, 192:224], 0.0, None, ALU.is_gt))
                dve.tensor_copy(sc[:, 14:15], sel[:, 0:1]).then_inc(sel_ready, 1)
                dve.wait_ge(count_T, 1)
                chain(dve.tensor_tensor(key, ps[:, 7, 64:96], sel, ALU.mult))
                chain(dve.tensor_scalar(key, key, -1.0, -1.0, ALU.mult, ALU.add))
                chain(dve.tensor_reduce(few[:, 0:1], ps[:, 7, 96:96 + N_EXP], AX, ALU.min))
                chain(dve.tensor_scalar(few[:, 1:2], few[:, 0:1], float(-P), None, ALU.is_ge))
                dve.tensor_copy(few_i[:, :], few[:, 1:2]).then_inc(few_ready, 1)
                dve.wait_ge(few_ready, 1)

            def pick_of(n):
                if not (isinstance(n, int) and n == 0):
                    dve.wait_ge(gathered, 2 * n)
                    dve.wait_ge(pick_T, n)
                src = comb_key[:, :, n:n + 1] if isinstance(n, int) else comb_key[:, :, bass.ds(n, 1)]
                dve.tensor_copy(cur.unsqueeze(2), src).then_inc(coef_set, 1)
                dve.wait_ge(coef_set, n + 1)
                for tt in range(TT):
                    i = dve.tensor_scalar(pick[:, tt, :], slot_no, cur[:, 2 + tt:3 + tt], None, ALU.is_equal)
                i.then_inc(pick_ready, 1)

            def gather_lo(n, half):
                dve.wait_ge(gath_hi, 2 * n + (half + 1))
                for k in range(4 * half, 4 * half + 4):
                    ins = dve.scalar_tensor_tensor(out=h_lo[:, k, 0:P], in0=ps[:, 0, (k % 4) * P:(k % 4 + 1) * P],
                                                   scalar=cols[:, ROW_LN2 + k:ROW_LN2 + k + 1], in1=h_hi[:, k, 0:P],
                                                   op0=ALU.mult, op1=ALU.subtract)
                ins.then_inc(gath_lo, 1)

            def pickT_out(n):
                dve.wait_ge(pick_T, n + 1)
                one = isinstance(n, int)
                dst = pickT[:, n:n + 1, :] if one else pickT[:, bass.ds(n, 1), :]
                dve.tensor_copy(slot_w[:, n:n + 1] if one else slot_w[:, bass.ds(n, 1)], ps[:, 3, S:S + 1])
                dve.tensor_copy(dst, ps[:, 3:4, 0:S]).then_inc(pickT_set, 1)

            def gated_few(c, u_up):
                dve.wait_ge(silu_done, c + 1)
                dve.wait_ge(unit_used, u_up + 1)
                if not (isinstance(c, int) and c == 0):
                    dve.wait_ge(aT_done, 2 * c)
                dve.tensor_tensor(act_a[:, 0, :], ps[:, 1, :], act_s[:, 0, :], ALU.mult).then_inc(a_done, 1)

            def aT_few_lo(c):
                dve.wait_ge(aT_hi_r, 2 * c + 2)
                dve.tensor_tensor(aT_lo[:, :, 0:P], ps[:, 1, :].rearrange("p (f t) -> p f t", f=4), aT_hi[:, :, 0:P],
                                  ALU.subtract).then_inc(aT_lo_r, 2)

            def y_out_lo(p, half):
                dve.wait_ge(y_half_hi, 2 * p + (half + 1))
                cs = slice(512 * half, 512 * half + 512)
                dve.scalar_tensor_tensor(out=y_lo[:, cs], in0=ps[:, 2 + half, :], scalar=slot_w_now, in1=y_hi[:, cs],
                                         op0=ALU.mult, op1=ALU.subtract).then_inc(down_added, 2)

            def few_experts():
                u = U_MOE
                pick_of(0)
                gather_lo(0, 0)
                pickT_out(0)
                gather_lo(0, 1)
                split_lo(u + 2)
                pick_of(1)
                split_lo(u + 3)
                split_lo(u + 4)
                gated_few(0, u + 3)
                split_lo(u + 5)
                gather_lo(1, 0)
                pickT_out(1)
                split_lo(u + 6)
                aT_few_lo(0)
                gather_lo(1, 1)
                s0 = u + 4
                with dve.Fori(0, N_EXP - 2) as i:
                    split_lo(s0 + 3, i)
                    pick_of(i + 2)
                    split_lo(s0 + 4, i)
                    split_lo(s0 + 5, i)
                    gated_few(i + 1, STEP * i + (s0 + 3))
                    gather_lo(i + 2, 0)
                    pickT_out(i + 2)
                    split_lo(s0 + 6, i)
                    y_out_lo(i, 0)
                    split_lo(s0 + 7, i)
                    y_out_lo(i, 1)
                    gather_lo(i + 2, 1)
                    aT_few_lo(i + 1)
                    split_lo(s0 + 8, i)
                s, p = s0 + STEP * (N_EXP - 2), N_EXP - 2
                split_lo(s + 3)
                split_lo(s + 4)
                split_lo(s + 5)
                gated_few(p + 1, s + 3)
                split_lo(s + 6)
                y_out_lo(p, 0)
                split_lo(s + 7)
                y_out_lo(p, 1)
                aT_few_lo(p + 1)
                split_lo(s + 8)
                y_out_lo(p + 1, 0)
                y_out_lo(p + 1, 1)
                for half in range(2):
                    cs = slice(512 * half, 512 * half + 512)
                    dve.wait_ge(y_used, 2 * N_EXP + half + 1)
                    dve.tensor_tensor(x[:, :, cs], ps[:, 4 + 2 * half:6 + 2 * half, :], x[:, :, cs], ALU.add).then_inc(down_added, 2)

            def all_experts():
                split_lo(U_MOE + 2)
                first_coef()
                u = chunks(U_MOE, 0, N_EXP, 4, next_coef)
                add_down(0, adds, u)
                add_down(1, adds, u + 1)

            adds = 4 + 4 * (N_EXP - 1)
            dve.memset(post, 1.0).then_inc(post_ready, 1)
            route()
            count()
            dve.wait_ge(slots_in, 16)
            is_few = dve.value_load(few_i[0:1, 0:1], min_val=0, max_val=1)
            with dve.If(is_few > 0):
                few_experts()
            with dve.Else():
                all_experts()
            dve.wait_ge(down_added, adds + 4)
            square_sums()
            dve.wait_ge(rms_ready, 3)
            chain(dve.reciprocal(sc[:, 6:8], sc[:, 4:6]))
            dve.wait_ge(fg_in, 16)
            for t in range(TT):
                i = dve.scalar_tensor_tensor(out=x[:, t, :], in0=x[:, t, :], scalar=sc[:, 6 + t:7 + t], in1=final_g,
                                             op0=ALU.mult, op1=ALU.mult)
            chain(i)
            x_final()
            transposed_lo(3, ROW_FFN1)
            split_lo(U_FFN1 + 1)
            post_rms(3)
            split_lo(U_FFN1 + 2)

            def ffn(u0, c0, phase, adds):
                dve.wait_ge(down_added, adds)
                chain(dve.memset(coef, 0.5))
                dve.tensor_copy(sc[:, 10:12], coef).then_inc(down_added, 4)
                adds += 4
                u = chunks(u0, c0, FFN_FULL, adds)
                adds += 4 * (FFN_FULL - 1)
                c = c0 + FFN_FULL
                split_lo(u + 3)
                gated(c, u + 1, 256)
                split_lo(u + 4)
                split_lo(u + 5)
                add_down(0, adds, u + 2)
                split_lo(u + 6)
                add_down(1, adds, u + 3)
                aT_lo_out(c, 2)
                split_lo(u + 7)
                adds += 4
                add_down(0, adds, u + 4)
                add_down(1, adds, u + 4)
                return adds + 4

            adds = ffn(U_FFN1, N_EXP, 1, adds + 4)
            dve.wait_ge(down_added, adds)

            x_final()
            transposed_lo(4, ROW_MIX)
            post_rms(4)
            dve.wait_ge(wr_split_hi, 2)
            dve.tensor_tensor(wr_lo[:, :, :], wr_raw[:, :, :], wr_hi[:, :, :], ALU.subtract).then_inc(wr_split_lo, 1)
            ss = blk_ss.rearrange("p (t b) -> p t b", t=TT)
            for g in range(4):
                split_lo(U_MIX + 2 * g + 3)
                split_lo(U_MIX + 2 * g + 4)
                dve.wait_ge(mix_out, 2 * g + 2)
                for t in range(TT):
                    i = dve.tensor_reduce(ss[:, t, 8 * g:8 * g + 8], sq[:, t, 512 * g:512 * g + 512].rearrange("p (b d) -> p b d", d=DH), AX, ALU.add)
            i.then_inc(blk_summed, 1)
            dve.wait_ge(pos_set, 1)
            pos = kvT[:, :, 2, 0:2 * PAIRS].rearrange("p k (q two) -> p k q two", two=2)[:, :, :, 0]
            dve.tensor_copy(pos, cols[:, ROW_POS:ROW_POS + 2 * PAIRS].rearrange("p (k q) -> p k q", k=2)).then_inc(kvT_ready, 1)
            dve.wait_ge(kv_T, 1)
            kvp = ps[:, 1, :].rearrange("p (k s) -> p k s", k=2)
            for g in range(2):
                src = kvp[g * DH:(g + 1) * DH]
                dve.tensor_copy(kvT[0:DH, :, g, :], src).then_inc(kvT_ready, 1)
                dve.tensor_copy(kvT[DH:P, :, g, 0:S - 1], src[:, :, 1:S]).then_inc(kvT_ready, 1)
            dve.wait_ge(blk_rms, 1)
            chain(dve.reciprocal(blk_ss, blk_r))
            for c0 in (0, OFF_QB):
                v = proj[:, :, c0:c0 + 512].rearrange("p t (b d) -> p t b d", d=DH)
                dve.tensor_tensor(v, v, ss[:, :, c0 // DH:c0 // DH + 8].unsqueeze(3).broadcast_to([P, TT, 8, DH]), ALU.mult).then_inc(q_normed, 1)
            for n, c0 in enumerate((OFF_KA, OFF_KS, OFF_KW)):
                v = proj[:, :, c0:c0 + P].rearrange("p t (b d) -> p t b d", d=DH)
                for dup in range(2):
                    dve.tensor_tensor(k_dup[:, :, 2 * n:2 * n + 2, dup * DH:(dup + 1) * DH], v,
                                      ss[:, :, c0 // DH:c0 // DH + 2].unsqueeze(3).broadcast_to([P, TT, 2, DH]), ALU.mult).then_inc(k_normed, 1)
            dve.wait_ge(half_set, 2)
            for n, row in enumerate((ROW_QA, ROW_QB)):
                chain(dve.tensor_scalar(gain8[:, 2 * n:2 * n + 2], half_rows, cols[:, row:row + 1], DH ** -0.5, ALU.mult, ALU.mult))
            dve.wait_ge(small_in, 64)
            chain(dve.tensor_scalar(nsink, sink, -1.0, None, ALU.mult))
            dve.wait_ge(pre_T, 1)
            pos_cols = ps[:, 2, 0:P].rearrange("p (k c) -> p k c", k=2)[:, :, 30]
            dve.tensor_tensor(bias2, pos_cols, cols[:, ROW_B1:ROW_B1 + 2], ALU.add).then_inc(bias2_set, 1)
            for n in range(2):
                dve.wait_ge(qk_T, n + 1)
                src = ps[:, 4 + 2 * n:6 + 2 * n, :]
                dve.tensor_scalar(qqT_even[:, n].rearrange("p (b k) s -> p b (k s)", b=2), src, gain8[:, 2 * n:2 * n + 1], None, ALU.mult)
                dve.tensor_scalar(qqT_odd[n].rearrange("p b k s -> p b (k s)"), src, gain8[:, 2 * n + 1:2 * n + 2], None,
                                  ALU.mult).then_inc(qk_set, 1)
            dve.wait_ge(kcsq_ready, 1)
            dve.tensor_reduce(kc_ss[0:N_CMP], kc_sq[0:N_CMP].rearrange("p (g d) -> p g d", g=2), AX, ALU.add).then_inc(kcss_ready, 1)
            dve.tensor_copy(v_c[0:N_CMP], ps[0:N_CMP, 3, P:2 * P]).then_inc(kcT_set, 1)
            for n in range(3):
                dve.wait_ge(qk_T, n + 3)
                gain = ROW_KA if n == 0 else ROW_KB
                bank = (0, 1, 4)[n]
                dve.tensor_scalar(kkT[:, 2 * n:2 * n + 2, :].rearrange("p k s -> p (k s)"), ps[:, bank, :], cols[:, gain:gain + 1], None,
                                  ALU.mult).then_inc(qk_set, 1)
            dve.wait_ge(kcr_ready, 1)
            chain(dve.reciprocal(kc_ss[0:N_CMP], kc_r[0:N_CMP]))
            for g in range(2):
                for dup in range(2):
                    dve.tensor_scalar(kc_n[0:N_CMP, g, dup], ps[0:N_CMP, 3, g * DH:(g + 1) * DH], kc_ss[0:N_CMP, g:g + 1], None,
                                      ALU.mult).then_inc(kcn_ready, 1)
            dve.wait_ge(kcT_T, 1)
            dve.tensor_scalar(kcT[:, :, 0:N_CMP], ps[:, 5, 0:32].rearrange("p (g c) -> p g c", g=2)[:, :, 0:N_CMP],
                              cols[:, ROW_KB:ROW_KB + 1], None, ALU.mult).then_inc(kcT_set, 1)

            def neg_logits(n):
                kind, h = n // HEADS, n % HEADS
                dve.wait_ge(lg_ready, n + 1)
                if n >= 4:
                    dve.wait_ge(pT_ready, n - 3)
                for qt in range(TT):
                    cs = key_cols(kind, qt)
                    k = 16 * kind + 8 * qt + h
                    b = bias_t[:, KINDS[kind][3], h]
                    if kind < 3:
                        b = b[:, P:S] if qt == 0 else b
                    else:
                        b = b[:, (P + CMP_LEN - 1 if qt == 0 else CMP_LEN - 1)::CMP_STRIDE]
                    start = nsink[:, h:h + 1] if kind == 0 else (3e38 if kind < 3 else FAR)
                    i = dve.tensor_tensor_reduce(out=prob[:, n % 4, cs], in0=ps[:, n % 4, cs], in1=b, scale=-1.0, scalar=start,
                                                 op0=ALU.add, op1=ALU.min, accum_out=negm[:, k:k + 1])
                i.then_inc(neg_ready, 1)

            def probs_T(n):
                dve.wait_ge(pT_ready, n + 1)
                if n >= 2:
                    dve.wait_ge(pv_done, n - 1)
                if n < 3 * HEADS:
                    dve.tensor_copy(probT[:, n % 2], ps[:, 4 + n % 2, 0:384]).then_inc(pT_set, 1)
                else:
                    dve.tensor_copy(probT[0:7, n % 2, 0:P], ps[0:7, 4 + n % 2, 0:P])
                    dve.tensor_copy(probT[0:N_CMP, n % 2, P:S], ps[0:N_CMP, 4 + n % 2, P:S]).then_inc(pT_set, 1)

            def sink_diff():
                dve.wait_ge(neg_ready, HEADS)
                dve.tensor_tensor(sink_t.rearrange("p (t h) -> p t h", t=TT), negm[:, 0:16].rearrange("p (t h) -> p t h", t=TT),
                                  sink.unsqueeze(1).broadcast_to([P, TT, HEADS]), ALU.add).then_inc(sink_ready, 1)

            def keep_kind(kind):
                sl = slice(16 * kind, 16 * kind + 16)
                dve.wait_ge(p_ready, HEADS * (kind + 1))
                if kind == 0:
                    dve.wait_ge(sinkexp, 1)
                    chain(dve.tensor_tensor(sums[:, sl], sums[:, sl], sink_t, ALU.add))
                if kind == 3:
                    chain(dve.tensor_scalar(sums[:, sl], sums[:, sl], TINY, None, ALU.max))
                chain(dve.reciprocal(o_scale[:, sl], sums[:, sl]))
                if kind:
                    gi = (None, 1, 2, 0)[kind]
                    v = o_scale[:, sl].rearrange("p (t h) -> p t h", t=TT)
                    dve.wait_ge(gsig_ready, 1)
                    chain(dve.tensor_tensor(v, v, gate_sig[:, :, HEADS * gi:HEADS * gi + HEADS], ALU.mult))
                dve.wait_ge(pv_done, HEADS * (kind + 1))
                o = ps[:, 6:8, :].rearrange("p t (h d) -> p t h d", d=DH)
                sv = o_scale[:, sl].rearrange("p (t h) -> p t h", t=TT).unsqueeze(3).broadcast_to([P, TT, HEADS, DH])
                dst = tok[:, :, 0:512] if kind == 0 else tok[:, :, 512:D]
                if kind < 2:
                    i = dve.tensor_tensor(dst.rearrange("p t (h d) -> p t h d", d=DH), o, sv, ALU.mult)
                    i.then_inc(o_used, 1)
                else:
                    dve.tensor_tensor(o_part.rearrange("p t (h d) -> p t h d", d=DH), o, sv, ALU.mult).then_inc(o_used, 1)
                    dve.wait_ge(o_used, kind + 1)
                    chain(dve.tensor_tensor(dst, dst, o_part, ALU.add))

            dve.wait_ge(bias_in, 32)
            for s in range(4 * HEADS + 4):
                if s < 4 * HEADS:
                    neg_logits(s)
                if s == HEADS:
                    sink_diff()
                if 2 <= s < 4 * HEADS + 2:
                    probs_T(s - 2)
                if s >= HEADS + 3 and (s - 3) % HEADS == 0:
                    keep_kind((s - 3) // HEADS - 1)
            dve.tensor_copy(sc[:, 12:14], sc[:, 8:10]).then_inc(tok_ready, 2)
            transposed_lo(5)
            split_lo(U_MIXOUT + 3)
            split_lo(U_FFN2)
            residual(U_MIXOUT)
            x_final()
            transposed_lo(6, ROW_FFN2)
            split_lo(U_FFN2 + 1)
            post_rms(5)
            split_lo(U_FFN2 + 2)
            adds = ffn(U_FFN2, N_EXP + FFN_FULL + 1, 2, adds)
            dve.wait_ge(down_added, adds)
            dve.tensor_copy(sc[:, 12:14], sc[:, 8:10]).then_inc(out_ready, 2)

        @block.tensor
        def _(pe):
            pe.wait_ge(const_in, 16)
            def transpose_tok(t):
                src = x if t in (0, 3, 4, 6) else tok
                pe.wait_ge(tok_ready, 2 * (t + 1))
                for b in range(4):
                    for k in (2 * b, 2 * b + 1):
                        for tt in range(TT):
                            c0 = (k % 2) * S + tt * P
                            ins = pe.transpose(ps[:, b, c0:c0 + P], src[:, tt, k * P:(k + 1) * P], ident)
                    ins.then_inc(xT_ready, 1)

            def product(out, hi, lo, w_h, w_l, first, last):
                pe.matmul(out, hi, w_h, start=first, stop=False)
                pe.matmul(out, hi, w_l, start=False, stop=False)
                return pe.matmul(out, lo, w_h, start=False, stop=last)

            def unit(u, banks, k0, first, last, i=None, n_k=4, src=(h_hi, h_lo)):
                pe.wait_ge(lo_ready, u + 1 if i is None else STEP * i + (u + 1))
                width = UNIT // n_k
                for k in range(n_k):
                    for tt in range(TT):
                        c = slice(tt * P, (tt + 1) * P)
                        wc = slice(k * width, k * width + 512)
                        ins = product(ps[:, banks[tt], :], src[0][:, k0 + k, c], src[1][:, k0 + k, c],
                                      w_hi[:, u % SPLIT, wc], w_lo[:, u % SPLIT, wc],
                                      first and k == 0, last and k == n_k - 1)
                ins.then_inc(unit_used, 1)

            def bias_by_distance():
                pe.wait_ge(tbl_in, 16)
                pe.wait_ge(onehot_in, 16)
                pe.wait_ge(ones_ready, 2)
                for n in range(2):
                    i = pe.matmul(ps[0:HEADS, 6 + n, 0:REL_W], tbl[:, n * HEADS:(n + 1) * HEADS], onehot[0:33, n], start=True, stop=True)
                i.then_inc(bias_done, 1)

            transpose_tok(0)
            pe.wait_ge(rows_in, 16 * 13)
            pe.transpose(ps[:, 7, 0:N_ROWS], rows[:, :], ident[0:N_ROWS, 0:N_ROWS]).then_inc(cols_T, 1)
            pe.wait_ge(hT_lo, 4)
            for g in range(11):
                if g == 2:
                    bias_by_distance()
                if g == 3:
                    pe.wait_ge(bias_sb, 1)
                if g >= 4:
                    pe.wait_ge(proj_out, g - 3)
                banks = (2 * (g % 4), 2 * (g % 4) + 1)
                unit(2 * g, banks, 0, True, False)
                unit(2 * g + 1, banks, 4, False, True)

            pe.wait_ge(proj_out, 11)
            for n in range(4):
                for ct in range(4):
                    for tt in range(TT):
                        c0 = (ct % 2) * S + tt * P
                        i = pe.transpose(ps[:, 2 * n + ct // 2, c0:c0 + P], stage[:, n, tt, ct * P:(ct + 1) * P], ident)
                i.then_inc(stage_T, 1)

            def z_of(ct, par, bank, first, last):
                r = slice(par * DH, (par + 1) * DH)
                if first:
                    pe.matmul(ps[:, bank, 0:S], kT[r, ct, 0:P], qT[r, ct, :], start=True, stop=True)
                    return pe.matmul(ps[:, bank, S:S + P], kT[r, ct, P:S], qT[r, ct, P:S], start=True, stop=True)

            def logits(ct):
                if ct >= 2:
                    pe.wait_ge(sp_ready, ct - 1)
                for par in range(2):
                    i = z_of(ct, par, 2 * (ct % 2) + par, True, True)
                i.then_inc(z_ready, 1)

            def survive(ct):
                pe.wait_ge(spm_ready, ct + 1)
                if ct >= 1:
                    pe.wait_ge(a_ready, ct)
                for par in range(2):
                    r = slice(par * DH, (par + 1) * DH)
                    s_ = soft[:, ct % 2, par]
                    bank = ps[:, 4 + par, :]
                    pe.matmul(bank[:, 0:S], kT[r, ct, 0:P], qT[r, ct, :], start=True, stop=False, skip_group_check=True)
                    pe.matmul(bank[:, 0:S], neg_tri, s_[:, 0:S], start=False, stop=False, skip_group_check=True)
                    pe.matmul(bank[:, P:S], neg_ones, s_[:, S:S + P], start=False, stop=True, skip_group_check=True)
                    pe.matmul(bank[:, S:S + P], kT[r, ct, P:S], qT[r, ct, P:S], start=True, stop=False, skip_group_check=True)
                    i = pe.matmul(bank[:, S:S + P], neg_tri, s_[:, S:S + P], start=False, stop=True, skip_group_check=True)
                i.then_inc(s_ready, 1)

            def values(ct):
                pe.wait_ge(am_ready, ct + 1)
                for par in range(2):
                    r = slice(par * DH, (par + 1) * DH)
                    hc = slice((2 * ct + par) * DH, (2 * ct + par + 1) * DH)
                    o = ps[r, 6 + ct // 2, (ct % 2) * S:(ct % 2 + 1) * S]
                    w = att[:, ct % 2, par]
                    pe.matmul(o, v_sb[:, 0, hc], w[:, 0:S], start=True, stop=False, skip_group_check=True)
                    i = pe.matmul(o[:, P:S], v_sb[:, 1, hc], w[:, S:S + P], start=False, stop=True, skip_group_check=True)
                i.then_inc(y_ready, 1)

            pe.wait_ge(sbT_ready, 2)
            logits(0)
            logits(1)
            pe.wait_ge(hgT_ready, 5)
            for ct in range(4):
                survive(ct)
                if ct + 2 < 4:
                    logits(ct + 2)
                values(ct)

            pe.wait_ge(hk_ready, 1)
            for b in range(4):
                par, tt = b // 2, b % 2
                r, c = slice(par * DH, (par + 1) * DH), slice(tt * P, (tt + 1) * P)
                for ct in range(4):
                    i = pe.matmul(ps[:, b, ct * P:(ct + 1) * P], hk[r, ct, c], qhT[r, ct, c], start=True, stop=True)
                i.then_inc(level_done, 1)

            def scores(n):
                h, b = 1 << (n - 1), (n - 1) % 2
                pe.wait_ge(qdec_ready, n)
                pe.wait_ge(kdec_ready, n)
                if n >= 2:
                    pe.wait_ge(level_kept, 4 + 2 * (n - 2))
                for tt in range(TT):
                    for ct in range(4):
                        c0 = ct * S + tt * P
                        q = q_dec[b][:, :, c0:c0 + P].rearrange("p e (n two h) -> p e n two h", two=2, h=h)[:, :, :, 1, :]
                        i = pe.matmul(ps[:, 4 * (n % 2) + tt, ct * P:(ct + 1) * P], k_dec[:, b, ct, tt * P:(tt + 1) * P], q,
                                      start=True, stop=True)
                    i.then_inc(level_done, 1)

            for level in range(LEVELS):
                scores(level + 1)
            pe.wait_ge(qdec_ready, LEVELS + 1)
            pe.wait_ge(kdec_ready, LEVELS + 1)
            pe.wait_ge(level_kept, 4 + 2 * (LEVELS - 1))
            for ct in range(4):
                i = pe.matmul(ps[:, ct // 2, (ct % 2) * S:(ct % 2 + 1) * S], k_dec[:, 1, ct, 0:P],
                              q_dec[1][:, :, ct * S + P:(ct + 1) * S], start=True, stop=True)
            i.then_inc(far_ready, 1)
            pe.wait_ge(level_kept, 4 + 2 * LEVELS + 1)
            for tt in range(TT):
                for h in range(HEADS):
                    par, ct = h % 2, h // 2
                    o = ps[:, 2 + tt, h * DH:(h + 1) * DH]
                    i = pe.matmul(o, sc_near[:, tt, ct, par, :], v_hg[:, tt, h * DH:(h + 1) * DH], start=True, stop=(tt == 0))
                    if tt == 1:
                        i = pe.matmul(o, sc_far[:, ct, par, :], v_hg[:, 0, h * DH:(h + 1) * DH], start=False, stop=True)
            i.then_inc(o_ready, 1)
            pe.wait_ge(ysb_lo, 1)
            for half in range(2):
                unit(U_BRANCH + half, (6 * half, 6 * half + 1), 0, True, True)
            pe.wait_ge(og_ready, 1)
            for ct in range(4):
                for tt in range(TT):
                    c0 = (ct % 2) * S + tt * P
                    i = pe.transpose(ps[:, 4 + ct // 2, c0:c0 + P], o_gated[:, tt, ct * P:(ct + 1) * P], ident)
            i.then_inc(oT_ready, 1)

            pe.wait_ge(yhg_lo, 1)
            for half in range(2):
                unit(U_BRANCH + 2 + half, (2 + 2 * half, 3 + 2 * half), 4, True, True)
            transpose_tok(1)

            def square_product(u0):
                for half in range(2):
                    banks = (4 + 2 * half, 5 + 2 * half)
                    unit(u0 + 2 * half, banks, 0, True, False)
                    unit(u0 + 2 * half + 1, banks, 4, False, True)

            pe.wait_ge(hT_lo, 8)
            square_product(U_OUT)
            transpose_tok(2)
            pe.wait_ge(hT_lo, 12)

            pe.wait_ge(wr_split_lo, 1)
            pe.wait_ge(small_in, 64)
            pe.wait_ge(ones_ready, 1)
            o = ps[0:20, 7, 0:S]
            for k in range(KT):
                pe.matmul(o, wr_hi[:, k, 0:20], h_hi[:, k, :], start=(k == 0), stop=False)
                pe.matmul(o, wr_hi[:, k, 0:20], h_lo[:, k, :], start=False, stop=False)
                pe.matmul(o, wr_lo[:, k, 0:20], h_hi[:, k, :], start=False, stop=False)
            pe.matmul(o, rb_row[:, 0:20], one_row[:, 0:1].broadcast_to([1, S]), start=False, stop=True).then_inc(route_done, 1)
            pe.wait_ge(route_out, 1)
            for tt in range(TT):
                i = pe.transpose(ps[:, 7, S + 32 * tt:S + 32 * tt + 20], route_sb[:, tt * P:(tt + 1) * P], ident[0:20, 0:20])
            i.then_inc(route_T, 1)

            down = (aT_hi, aT_lo)

            def transpose_a(c, n_f=4):
                pe.wait_ge(a_done, c + 1)
                for tt in range(TT):
                    for f in range(n_f):
                        i = pe.transpose(ps[:, 2 + tt, f * P:(f + 1) * P], act_a[:, tt, f * P:(f + 1) * P], ident)
                    i.then_inc(aT_done, 1)

            def chunks(u0, c0, n, adds0):
                unit(u0, (0, 1), 0, True, False)
                unit(u0 + 1, (0, 1), 4, False, True)
                if c0:
                    pe.wait_ge(aT_lo_r, 2 * c0)
                unit(u0 + 2, (2, 3), 0, True, False)
                unit(u0 + 3, (2, 3), 4, False, True)
                transpose_a(c0)
                s0 = u0 + 4
                with pe.Fori(0, n - 1) as i:
                    c = i + (c0 + 1)
                    unit(s0, (0, 1), 0, True, False, i)
                    unit(s0 + 1, (0, 1), 4, False, True, i)
                    pe.wait_ge(aT_lo_r, 2 * i + 2 * (c0 + 1))
                    unit(s0 + 2, (2, 3), 0, True, False, i)
                    unit(s0 + 3, (2, 3), 4, False, True, i)
                    pe.wait_ge(down_added, 4 * i + (adds0 - 2))
                    unit(s0 + 4, (4, 5), 0, True, True, i, src=down)
                    pe.wait_ge(down_added, 4 * i + adds0)
                    unit(s0 + 5, (6, 7), 0, True, True, i, src=down)
                    transpose_a(c)
                return s0 + STEP * (n - 1)

            def count():
                pe.wait_ge(sel_ready, 1)
                o = ps[:, 7, :]
                pe.matmul(o[:, 64:80], neg_tri, sel[:, 0:16], start=True, stop=False)
                pe.matmul(o[:, 64:80], neg_ones, sel[:, 16:32], start=False, stop=True)
                pe.matmul(o[:, 80:96], neg_tri, sel[:, 16:32], start=True, stop=True)
                pe.matmul(o[:, 96:112], neg_ones, sel[:, 0:16], start=True, stop=False)
                pe.matmul(o[:, 96:112], neg_ones, sel[:, 16:32], start=False, stop=True).then_inc(count_T, 1)

            def last_down(u, c, adds):
                pe.wait_ge(aT_lo_r, 2 * (c + 1))
                pe.wait_ge(down_added, adds - 2)
                unit(u, (4, 5), 0, True, True, src=down)
                pe.wait_ge(down_added, adds)
                unit(u + 1, (6, 7), 0, True, True, src=down)

            def unit_few(u, bank, k0, first, last, i=None, src=(h_hi, h_lo)):
                pe.wait_ge(lo_ready, u + 1 if i is None else STEP * i + (u + 1))
                for k in range(4):
                    wc = slice(k * 512, k * 512 + 512)
                    ins = product(ps[:, bank, :], src[0][:, k0 + k, 0:P], src[1][:, k0 + k, 0:P],
                                  w_hi[:, u % SPLIT, wc], w_lo[:, u % SPLIT, wc], first and k == 0, last and k == 3)
                ins.then_inc(unit_used, 1)

            def gather(half):
                for k in range(4 * half, 4 * half + 4):
                    o = ps[:, 0, (k % 4) * P:(k % 4 + 1) * P]
                    n = 0
                    for h2 in (h2_hi, h2_lo):
                        for tt in range(TT):
                            ins = pe.matmul(o, h2[:, tt, k * P:(k + 1) * P], pick[:, tt, :], start=(n == 0), stop=(n == 3))
                            n += 1
                ins.then_inc(gathered, 1)

            def transpose_pick():
                for tt in range(TT):
                    pe.transpose(ps[:, 3, tt * P:(tt + 1) * P], pick_f[:, tt, :], ident)
                for tt in range(TT):
                    ins = pe.matmul(ps[:, 3, S:S + 1], pick_f[:, tt, :], cur[:, tt:tt + 1], start=(tt == 0), stop=(tt == 1))
                ins.then_inc(pick_T, 1)

            def transpose_a_few(c):
                pe.wait_ge(a_done, c + 1)
                for f in range(4):
                    i = pe.transpose(ps[:, 1, f * P:(f + 1) * P], act_a[:, 0, f * P:(f + 1) * P], ident)
                i.then_inc(aT_done, 2)

            def scatter(p, half, last=False):
                pe.wait_ge(down_added, 4 * p + (2 * half + 2))
                pe.wait_ge(pickT_moved, p + 1)
                for tt in range(TT):
                    pT = pickT_now[:, tt * P:(tt + 1) * P]
                    o = ps[:, 4 + 2 * half + tt, :]
                    for n, y in enumerate((y_hi, y_lo)):
                        ins = pe.matmul(o, pT, y[:, 512 * half:512 * half + 512], start=False, stop=last and n == 1,
                                        skip_group_check=True)
                ins.then_inc(y_used, 1)

            def few_experts():
                pe.wait_ge(zero_set, 1)
                for b in range(4, 8):
                    ins = pe.matmul(ps[:, b, :], zero_r[:, 0:P], zero_r, start=True, stop=False, skip_group_check=True)
                ins.then_inc(y_used, 2)
                u = U_MOE
                pe.wait_ge(h2_lo_set, 1)
                pe.wait_ge(pick_ready, 1)
                gather(0)
                transpose_pick()
                pe.wait_ge(gath_lo, 1)
                gather(1)
                pe.wait_ge(gath_lo, 2)
                unit_few(u, 0, 0, True, False)
                unit_few(u + 1, 0, 4, False, True)
                unit_few(u + 2, 1, 0, True, False)
                unit_few(u + 3, 1, 4, False, True)
                pe.wait_ge(pick_ready, 2)
                pe.wait_ge(silu_done, 1)
                gather(0)
                pe.wait_ge(pickT_set, 1)
                transpose_pick()
                transpose_a_few(0)
                pe.wait_ge(gath_lo, 3)
                gather(1)
                s0 = u + 4
                with pe.Fori(0, N_EXP - 2) as i:
                    pe.wait_ge(gath_lo, 2 * i + 4)
                    unit_few(s0, 0, 0, True, False, i)
                    unit_few(s0 + 1, 0, 4, False, True, i)
                    pe.wait_ge(aT_lo_r, 2 * i + 2)
                    unit_few(s0 + 2, 1, 0, True, False, i)
                    unit_few(s0 + 3, 1, 4, False, True, i)
                    pe.wait_ge(pick_ready, i + 3)
                    pe.wait_ge(silu_done, i + 2)
                    gather(0)
                    transpose_pick()
                    unit_few(s0 + 4, 2, 0, True, True, i, src=down)
                    transpose_a_few(i + 1)
                    pe.wait_ge(pickT_set, i + 3)
                    unit_few(s0 + 5, 3, 0, True, True, i, src=down)
                    pe.wait_ge(gath_lo, 2 * i + 5)
                    gather(1)
                    scatter(i, 0)
                    scatter(i, 1)
                s, p = s0 + STEP * (N_EXP - 2), N_EXP - 2
                pe.wait_ge(gath_lo, 2 * N_EXP)
                unit_few(s, 0, 0, True, False)
                unit_few(s + 1, 0, 4, False, True)
                pe.wait_ge(aT_lo_r, 2 * (p + 1))
                unit_few(s + 2, 1, 0, True, False)
                unit_few(s + 3, 1, 4, False, True)
                unit_few(s + 4, 2, 0, True, True, src=down)
                transpose_a_few(p + 1)
                unit_few(s + 5, 3, 0, True, True, src=down)
                scatter(p, 0)
                scatter(p, 1)
                pe.wait_ge(aT_lo_r, 2 * (p + 2))
                unit_few(s + 6, 2, 0, True, True, src=down)
                unit_few(s + 7, 3, 0, True, True, src=down)
                scatter(p + 1, 0, True)
                scatter(p + 1, 1, True)

            adds = 4 + 4 * (N_EXP - 1)
            count()
            pe.wait_ge(few_ready, 1)
            is_few = pe.value_load(few_i[0:1, 0:1], min_val=0, max_val=1)
            with pe.If(is_few > 0):
                few_experts()
            with pe.Else():
                u = chunks(U_MOE, 0, N_EXP, 4)
                last_down(u, N_EXP - 1, adds)
            transpose_tok(3)
            pe.wait_ge(hT_lo, 16)

            def narrow(u, banks):
                pe.wait_ge(lo_ready, u + 1)
                for k in range(KT):
                    for tt in range(TT):
                        c = slice(tt * P, (tt + 1) * P)
                        wc = slice(k * 256, (k + 1) * 256)
                        i = product(ps[:, banks[tt], 0:256], h_hi[:, k, c], h_lo[:, k, c], w_hi[:, u % SPLIT, wc],
                                    w_lo[:, u % SPLIT, wc], k == 0, k == KT - 1)
                i.then_inc(unit_used, 1)

            def ffn(u0, c0, adds):
                u = chunks(u0, c0, FFN_FULL, adds)
                adds += 4 * (FFN_FULL - 1)
                c = c0 + FFN_FULL
                narrow(u, (0, 1))
                pe.wait_ge(aT_lo_r, 2 * c)
                narrow(u + 1, (2, 3))
                last_down(u + 2, c - 1, adds)
                transpose_a(c, 2)
                pe.wait_ge(lo_ready, u + 5)
                pe.wait_ge(aT_lo_r, 2 * (c + 1))
                for half in range(2):
                    pe.wait_ge(down_added, adds + 2 * half + 2)
                    for k in range(2):
                        for tt in range(TT):
                            t = slice(tt * P, (tt + 1) * P)
                            wc = slice(k * D + half * 512, k * D + half * 512 + 512)
                            i = product(ps[:, 4 + 2 * half + tt, :], aT_hi[:, k, t], aT_lo[:, k, t], w_hi[:, (u + 4) % SPLIT, wc],
                                        w_lo[:, (u + 4) % SPLIT, wc], k == 0, k == 1)
                i.then_inc(unit_used, 1)
                return adds + 8

            adds = ffn(U_FFN1, N_EXP, adds + 8)

            transpose_tok(4)
            pe.wait_ge(hT_lo, 20)
            for g in range(4):
                unit(U_MIX + 2 * g, (2 * g, 2 * g + 1), 0, True, False)
                unit(U_MIX + 2 * g + 1, (2 * g, 2 * g + 1), 4, False, True)
            pe.wait_ge(wr_split_lo, 2)
            pe.wait_ge(mix_out, 2)
            for tt in range(TT):
                c = slice(tt * P, (tt + 1) * P)
                for k in range(KT):
                    i = product(ps[:, 0, 32 * tt:32 * tt + GATE_COLS], h_hi[:, k, c], h_lo[:, k, c], wr_hi[:, k, :], wr_lo[:, k, :],
                                k == 0, k == KT - 1)
            i.then_inc(gates_T, 1)
            pe.wait_ge(mix_out, 8)
            for kv in range(2):
                for tt in range(TT):
                    i = pe.transpose(ps[:, 1, kv * S + tt * P:kv * S + (tt + 1) * P], proj[:, tt, OFF_KC + kv * P:OFF_KC + (kv + 1) * P], ident)
            i.then_inc(kv_T, 1)
            pe.wait_ge(cmp_in, 32)
            pe.wait_ge(kvT_ready, 5)
            for kv in range(2):
                for pp in range(PAIRS):
                    i = pe.matmul(ps[:, 2, 64 * kv:64 * kv + 3 * N_CMP], cmp_w1[:, kv, pp, :],
                                  kvT[:, kv, :, 2 * pp:2 * pp + CMP_STRIDE * (N_CMP - 1) + 1:CMP_STRIDE],
                                  start=(pp == 0), stop=(pp == PAIRS - 1))
            i.then_inc(pre_T, 1)
            for n, c0 in enumerate((0, OFF_QB)):
                pe.wait_ge(q_normed, n + 1)
                for ct in range(4):
                    for tt in range(TT):
                        o = (ct % 2) * S + tt * P
                        i = pe.transpose(ps[:, 4 + 2 * n + ct // 2, o:o + P], proj[:, tt, c0 + ct * P:c0 + (ct + 1) * P], ident)
                i.then_inc(qk_T, 1)
            pe.wait_ge(hid_ready, 1)
            for kv in range(2):
                for g in range(2):
                    o = ps[0:N_CMP, 3, kv * P + g * DH:kv * P + (g + 1) * DH]
                    pe.matmul(o, hidT[:, kv, g * N_CMP:(g + 1) * N_CMP], cmp_w2[:, kv, :], start=True, stop=False)
                    i = pe.matmul(o, one_row[:, 0:N_CMP], b2_row[:, kv, :], start=False, stop=True)
            i.then_inc(kvc_ready, 1)
            pe.wait_ge(gsig_ready, 1)
            for n in range(3):
                pe.wait_ge(k_normed, 2 * n + 2)
                if n == 2:
                    pe.wait_ge(qk_set, 1)
                for g in range(2):
                    for tt in range(TT):
                        i = pe.transpose(ps[:, (0, 1, 4)[n], g * S + tt * P:g * S + (tt + 1) * P], k_dup[:, tt, 2 * n + g, :], ident)
                i.then_inc(qk_T, 1)
            pe.wait_ge(kcn_ready, 4)
            for g in range(2):
                i = pe.transpose(ps[:, 5, 16 * g:16 * g + N_CMP], kc_n[0:N_CMP, g].rearrange("p a d -> p (a d)"), ident[0:N_CMP, 0:N_CMP])
            i.then_inc(kcT_T, 1)

            def logits_of(n):
                kind, h = n // HEADS, n % HEADS
                qi, k0, _, _ = KINDS[kind]
                ct, g = h // 2, h // (HEADS // 2)
                if n >= 4:
                    pe.wait_ge(neg_ready, n - 3)
                for qt in range(TT):
                    o = ps[:, n % 4, key_cols(kind, qt)]
                    w = o.shape[-1]
                    keys = kkT[:, k0 + g, 0:w] if kind < 3 else kcT[:, g, 0:w]
                    q = qqT_odd[qi][:, ct // 2, ct % 2] if h % 2 else qqT_even[:, qi, ct]
                    i = pe.matmul(o, q[:, qt * P:(qt + 1) * P], keys, start=True, stop=True)
                i.then_inc(lg_ready, 1)

            def transpose_p(n):
                kind = n // HEADS
                w = prob[:, n % 4]
                pe.wait_ge(p_ready, n + 1)
                if n >= 2:
                    pe.wait_ge(pT_set, n - 1)
                if kind < 3:
                    for b in range(3):
                        i = pe.transpose(ps[:, 4 + n % 2, b * P:(b + 1) * P], w[:, b * P:(b + 1) * P], ident)
                else:
                    for qt in range(TT):
                        cs = key_cols(3, qt)
                        i = pe.transpose(ps[0:cs.stop - cs.start, 4 + n % 2, qt * P:(qt + 1) * P], w[:, cs], ident)
                i.then_inc(pT_ready, 1)

            def weighted(n):
                kind, h = n // HEADS, n % HEADS
                g = h // (HEADS // 2)
                pe.wait_ge(pT_set, n + 1)
                if kind and h == 0:
                    pe.wait_ge(o_used, kind)
                cs = slice(h * DH, (h + 1) * DH)
                if kind < 3:
                    vc = slice(KINDS[kind][2] + g * DH, KINDS[kind][2] + (g + 1) * DH)
                    pe.matmul(ps[:, 6, cs], probT[:, n % 2, 0:P], proj[:, 0, vc], start=True, stop=True)
                    pe.matmul(ps[:, 7, cs], probT[:, n % 2, P:2 * P], proj[:, 0, vc], start=True, stop=False)
                    i = pe.matmul(ps[:, 7, cs], probT[:, n % 2, 2 * P:3 * P], proj[:, 1, vc], start=False, stop=True)
                else:
                    vc = slice(g * DH, (g + 1) * DH)
                    for qt in range(TT):
                        w = key_cols(3, qt)
                        w = w.stop - w.start
                        i = pe.matmul(ps[:, 6 + qt, cs], probT[0:w, n % 2, qt * P:(qt + 1) * P], v_c[0:w, vc], start=True, stop=True)
                i.then_inc(pv_done, 1)

            pe.wait_ge(qk_set, 5)
            pe.wait_ge(kcT_set, 2)
            for s in range(4 * HEADS + 3):
                if s < 4 * HEADS:
                    logits_of(s)
                if 2 <= s < 4 * HEADS + 2:
                    transpose_p(s - 2)
                if s >= 3:
                    weighted(s - 3)

            transpose_tok(5)
            pe.wait_ge(hT_lo, 24)
            square_product(U_MIXOUT)
            transpose_tok(6)
            pe.wait_ge(hT_lo, 28)
            ffn(U_FFN2, N_EXP + FFN_FULL + 1, adds + 4)

        @block.gpsimd
        def _(pool):

            pool.memset(one_row[:, :], 1.0).then_inc(ones_ready, 1)
            pool.memset(tbl[32:33, :], 1.0).then_inc(ones_ready, 1)

            def causal(buf):
                for block_cols in (slice(0, P), slice(2 * P, 3 * P)):
                    v = buf[:, :, block_cols]
                    i = pool.affine_select(out=v, in_=v, compare_op=ALU.is_gt, fill=0.0, base=0,
                                           pattern=[[0, 2], [1, P]], channel_multiplier=-1)
                return i

            def mask_soft(ct):
                pool.wait_ge(sp_ready, ct + 1)
                causal(soft[:, ct % 2]).then_inc(spm_ready, 1)

            pool.wait_ge(stage_T, 1)
            pool.memset(tok[:, :, :], 0.0).then_inc(zeroed, 1)
            mask_soft(0)
            mask_soft(1)
            for ct in range(4):
                pool.wait_ge(a_ready, ct + 1)
                causal(att[:, ct % 2]).then_inc(am_ready, 1)
                if ct + 2 < 4:
                    mask_soft(ct + 2)
            pool.wait_ge(s_ready, 4)
            hk_f, pre_f, suf_f = (v.rearrange("p c s -> p (c s)") for v in (hk, pre, suf))
            pool.memset(suf, 1.0).then_inc(suf_done, 1)
            pool.wait_ge(suf_done, 1)
            pool.wait_ge(hk_ready, 1)
            pool.wait_ge(y_ready, 4)
            for level in range(LEVELS):
                h, b = 1 << level, level % 2
                n = 4 * S // (2 * h)
                if level >= 2:
                    pool.wait_ge(level_done, 4 + 2 * (level - 1))
                k_f = k_dec[:, b].rearrange("p c s -> p (c s)")
                pool.tensor_tensor(halves(k_f, h)[:, :, 0, :], halves(hk_f, h)[:, :, 0, :], halves(suf_f, h)[:, :, 0, :],
                                   ALU.mult).then_inc(kdec_ready, 1)
                if level:
                    pool.wait_ge(pre_ready, level)
                pool.tensor_tensor(halves(suf_f, h)[:, :, 0, :], halves(suf_f, h)[:, :, 0, :],
                                   halves(pre_f, h)[:, :, 1, h - 1:h].broadcast_to([P, n, h]), ALU.mult).then_inc(suf_done, 1)
                pool.wait_ge(suf_done, level + 2)
            pool.wait_ge(level_done, 4 + 2 * (LEVELS - 1))
            pool.tensor_tensor(k_dec[:, 1, :, 0:P], hk[:, :, 0:P], suf[:, :, 0:P], ALU.mult).then_inc(kdec_ready, 1)
            pool.wait_ge(level_kept, 4 + 2 * LEVELS)
            pool.dma_start(final_g, a["final_g"].rearrange("(o d) -> o d", o=1).broadcast_to([P, D])).then_inc(fg_in, 16)

            pool.wait_ge(wr_split_lo, 1)
            pool.dma_start(wr_raw[:, :, 0:GATE_COLS], a["w_mix_in_2"][0][:, 2048:D_MIX].rearrange("(k p) n -> p k n", p=P)).then_inc(wr2_in, 16)
            pool.wait_ge(tok_ready, 4)
            pool.dma_start(slot_no, slots_dram).then_inc(slots_in, 16)
            pool.wait_ge(few_ready, 1)
            is_few = pool.value_load(few_i[0:1, 0:1], min_val=0, max_val=1)
            with pool.If(is_few > 0):
                with pool.Fori(0, N_EXP) as p:
                    pool.wait_ge(pickT_set, p + 1)
                    pool.wait_ge(y_used, 2 * p + 2)
                    pool.tensor_copy(slot_w_now, slot_w[:, bass.ds(p, 1)])
                    pool.tensor_copy(pickT_now.unsqueeze(1), pickT[:, bass.ds(p, 1), :]).then_inc(pickT_moved, 1)
            pool.wait_ge(ss_ready, 3)
            pool.memset(kvT[:, :, 2, :], 0.0).then_inc(pos_set, 1)




_INS = ["x", "ln1_g", "w_in", "w_branch_sb", "w_branch_hg", "hg_norm_g", "hg_lb_logits", "w_out", "ln2_g",
        "w_router_group", "b_router_group", "w_router_expert", "b_router_expert", "w_exp_gate", "w_exp_up",
        "w_exp_down", "final_g", "rel_bias_table_2", "ffn1_norm_2", "ffn1_w_in_2", "ffn1_w_out_2", "mix_norm_2",
        "w_mix_in_2", "w_mix_out_2", "q_norm_a_2", "k_norm_a_2", "sinks_a_2", "q_norm_b_2", "k_norm_b_2",
        "cmp_pos_2", "cmp_w1_2", "cmp_b1_2", "cmp_w2_2", "cmp_b2_2", "ffn2_norm_2", "ffn2_w_in_2", "ffn2_w_out_2"]


def kernel(**inputs):
    import concourse.bacc as bacc
    from concourse.bass_utils import run_bass_kernel_spmd

    nc = bacc.Bacc("TRN2", target_bir_lowering=False, num_devices=1, dynamic_dma_scratch_size=2048)
    arrays, handles = {}, {}
    for name in _INS:
        arr = np.ascontiguousarray(inputs[name])
        arrays[f"in_{name}"] = arr
        handles[name] = nc.dram_tensor(f"in_{name}", arr.shape, F32, kind="ExternalInput").ap()
    out = nc.dram_tensor("out_x", (1, S, D), F32, kind="ExternalOutput").ap()
    two_blocks_kernel(nc, handles, out)
    result = run_bass_kernel_spmd(nc, [arrays], core_ids=[0])
    return result.results[0]["out_x"]
```
